# Optimizing a Trainium2 kernel written in Bass

```python
import jax
import jax.numpy as jnp
from jax import lax
import numpy as np
import math
import jax, jax.numpy as jnp

D_MODEL = 1024
BATCH = 1
SEQ = 512
DEPTH = 2

GRID_W = 64
CTX_LEN = 256
EPS = 1e-6
F_MIN = 1e-6
A_HEAD_DIM = 128
A_HEADS = D_MODEL // (2 * A_HEAD_DIM)
A_WIDTH = A_HEADS * A_HEAD_DIM
HGRN_CHUNK = 64
B_GROUPS = 4
B_WIDTH = D_MODEL - A_WIDTH
B_GROUP_DIM = B_WIDTH // B_GROUPS
B_CHUNK = 128
EV_IN = 5 * A_WIDTH + 2 * B_WIDTH
C_WIDTH = D_MODEL // 4
C_GROUPS = 4
C_GROUP_DIM = C_WIDTH // C_GROUPS
MLA_V_DIM = 128
MLA_HEADS = (D_MODEL - C_WIDTH) // MLA_V_DIM
MLA_NOPE = 128
MLA_ROPE = 64
MLA_QK = MLA_NOPE + MLA_ROPE
Q_LORA = 384
KV_LORA = 256
OD_IN = C_WIDTH + Q_LORA + KV_LORA + MLA_ROPE
ROPE_THETA = 10000.0
ATTN_BLOCK = 128
D_FF = 2816
CONV_W = 3


def rms_norm(x, w):
    xf = x.astype(jnp.float32)
    y = xf * lax.rsqrt(jnp.mean(xf * xf, axis=-1, keepdims=True) + EPS)
    return y.astype(x.dtype) * w

def modulate(x, norm_w, shift, scale):
    return rms_norm(x, norm_w) * (1 + scale) + shift

def to_heads(a, n_heads):
    bsz, t_len, width = a.shape
    return a.reshape(bsz, t_len, n_heads, width // n_heads).transpose(0, 2, 1, 3)

def flip_t(a):
    return a[:, :, ::-1]

def gla_chunked(q, k, v, log_f, s0):
    bsz, nh, t_len, _ = q.shape
    dv = v.shape[-1]
    n_chunks = t_len // HGRN_CHUNK

    def to_chunks(a):
        return a.reshape(bsz, nh, n_chunks, HGRN_CHUNK, a.shape[-1]).transpose(2, 0, 1, 3, 4)

    prefix_mask = jnp.tril(jnp.ones((HGRN_CHUNK, HGRN_CHUNK), dtype=bool))[:, :, None]

    def step(state, inp):
        qc, kc, vc, gc = inp
        b = jnp.cumsum(gc, axis=2)
        diff = b[:, :, :, None, :] - b[:, :, None, :, :]
        decay = jnp.where(prefix_mask, jnp.exp(jnp.minimum(diff, 0.0)), 0.0)
        scores = jnp.einsum('bhtk,bhsk,bhtsk->bhts', qc, kc, decay)
        out = (jnp.einsum('bhtk,bhkv->bhtv', qc * jnp.exp(b), state)
               + jnp.einsum('bhts,bhsv->bhtv', scores, vc))
        b_last = b[:, :, -1:, :]
        new_state = (jnp.exp(b_last[:, :, 0, :])[..., None] * state
                     + jnp.einsum('bhsk,bhsv->bhkv', kc * jnp.exp(b_last - b), vc))
        return new_state, out

    s_fin, o = lax.scan(step, s0, (to_chunks(q), to_chunks(k), to_chunks(v), to_chunks(log_f)))
    return o.transpose(1, 2, 0, 3, 4).reshape(bsz, nh, t_len, dv), s_fin

def hgrn2_features(p, lb):
    f32 = jnp.float32
    q = to_heads(jax.nn.silu(p[..., :A_WIDTH]).astype(f32), A_HEADS)
    v = to_heads(p[..., A_WIDTH:2 * A_WIDTH].astype(f32), A_HEADS)
    out = []
    for d in range(2):
        z = p[..., (2 + d) * A_WIDTH:(3 + d) * A_WIDTH].astype(f32)
        f = jnp.maximum(lb[d] + (1.0 - lb[d]) * jax.nn.sigmoid(z), F_MIN)
        log_f = jnp.log(f)
        k = 1.0 - f
        out.append((q, to_heads(k, A_HEADS), v, to_heads(log_f, A_HEADS)))
    return out

def hgrn2_readout(o, g, onorm_w):
    bsz, _, t_len, _ = o.shape
    o = rms_norm(o.transpose(0, 2, 1, 3), onorm_w).reshape(bsz, t_len, A_WIDTH)
    return (o * jax.nn.silu(g.astype(jnp.float32))).astype(g.dtype)

def hgrn2_mixer(pl, pc, lb, onorm_w, with_ctx):
    fwd_l, bwd_l = hgrn2_features(pl, lb)
    fwd_c, bwd_c = hgrn2_features(pc, lb)
    s0 = jnp.zeros((pl.shape[0], A_HEADS, A_HEAD_DIM, A_HEAD_DIM), jnp.float32)
    oc_f, sc_f = gla_chunked(*fwd_c, s0)
    ol_f, _ = gla_chunked(*fwd_l, sc_f)
    oc_b, sc_b = gla_chunked(*[flip_t(a) for a in bwd_c], s0)
    ol_b, _ = gla_chunked(*[flip_t(a) for a in bwd_l], sc_b)
    g_sl = slice(4 * A_WIDTH, 5 * A_WIDTH)
    yl = hgrn2_readout(ol_f + flip_t(ol_b), pl[..., g_sl], onorm_w)
    yc = None
    if with_ctx:
        yc = hgrn2_readout(oc_f + flip_t(oc_b), pc[..., g_sl], onorm_w)
    return yl, yc

def chunk_mlp(u_pre, v_pre, vnorm_w, ws, bs):
    bsz, t_len, _ = u_pre.shape
    n = t_len // B_CHUNK
    u = jax.nn.gelu(u_pre)
    v = rms_norm(jax.nn.gelu(v_pre).reshape(bsz, n, B_CHUNK, B_GROUPS, B_GROUP_DIM), vnorm_w)
    sv = jnp.einsum('gts,bnsgc->bntgc', ws, v) + bs.T[:, :, None]
    return u * sv.reshape(bsz, t_len, B_WIDTH)

def even_mixer(hl, hc, w_in, lb, onorm_w, vnorm_w, ws, bs, w_out, with_ctx):
    pl = hl @ w_in
    pc = hc @ w_in
    a_sl = slice(0, 5 * A_WIDTH)
    u_sl = slice(5 * A_WIDTH, 5 * A_WIDTH + B_WIDTH)
    v_sl = slice(5 * A_WIDTH + B_WIDTH, EV_IN)
    al, ac = hgrn2_mixer(pl[..., a_sl], pc[..., a_sl], lb, onorm_w, with_ctx)
    yl = jnp.concatenate([al, chunk_mlp(pl[..., u_sl], pl[..., v_sl], vnorm_w, ws, bs)], -1) @ w_out
    yc = None
    if with_ctx:
        yc = jnp.concatenate([ac, chunk_mlp(pc[..., u_sl], pc[..., v_sl], vnorm_w, ws, bs)], -1) @ w_out
    return yl, yc

def fourier_mix(p):
    bsz, t_len, _ = p.shape
    xg = p.reshape(bsz, t_len, C_GROUPS, C_GROUP_DIM).astype(jnp.float32)
    y = jnp.fft.fft2(xg, axes=(1, 3), norm='ortho').real
    return y.reshape(bsz, t_len, C_WIDTH).astype(p.dtype)

def rope_2d(x, cos, sin):
    xr = x.reshape(*x.shape[:-1], 2, 2, MLA_ROPE // 4)
    x1, x2 = xr[..., 0, :], xr[..., 1, :]
    return jnp.stack([x1 * cos - x2 * sin, x2 * cos + x1 * sin], axis=-2).reshape(x.shape)

def mla_project(p, qa_w, w_qb, kva_w, w_kvb, qn_w, kn_w, cos, sin):
    bsz, t_len, _ = p.shape
    q_lat = rms_norm(p[..., :Q_LORA], qa_w)
    kv_lat = rms_norm(p[..., Q_LORA:Q_LORA + KV_LORA], kva_w)
    k_pe = rms_norm(p[..., Q_LORA + KV_LORA:], kn_w[MLA_NOPE:])
    q = (q_lat @ w_qb).reshape(bsz, t_len, MLA_HEADS, MLA_QK)
    kv = (kv_lat @ w_kvb).reshape(bsz, t_len, MLA_HEADS, MLA_NOPE + MLA_V_DIM)
    q_nope = rms_norm(q[..., :MLA_NOPE], qn_w[:MLA_NOPE])
    q_pe = rms_norm(q[..., MLA_NOPE:], qn_w[MLA_NOPE:])
    k_nope = rms_norm(kv[..., :MLA_NOPE], kn_w[:MLA_NOPE])
    if cos is not None:
        q_pe = rope_2d(q_pe, cos[:, None], sin[:, None])
        k_pe = rope_2d(k_pe, cos, sin)
    k_pe = jnp.broadcast_to(k_pe[:, :, None, :], (bsz, t_len, MLA_HEADS, MLA_ROPE))
    q = jnp.concatenate([q_nope, q_pe], -1)
    k = jnp.concatenate([k_nope, k_pe], -1)
    return q, k, kv[..., MLA_NOPE:]

def attend(q, k, v):
    bsz, tq, nh, dq = q.shape
    nb = tq // ATTN_BLOCK
    qb = q.reshape(bsz, nb, ATTN_BLOCK, nh, dq).transpose(1, 0, 2, 3, 4)
    scale = dq ** -0.5

    def one_block(qblk):
        s = jnp.einsum('bqhd,bkhd->bhqk', qblk, k).astype(jnp.float32) * scale
        p = jax.nn.softmax(s, axis=-1).astype(v.dtype)
        return jnp.einsum('bhqk,bkhd->bqhd', p, v)

    o = lax.map(one_block, qb)
    return o.transpose(1, 0, 2, 3, 4).reshape(bsz, tq, nh * v.shape[-1])

def odd_mixer(hl, hc, w_in, qa_w, w_qb, kva_w, w_kvb, qn_w, kn_w, w_out, cos, sin, with_ctx):
    pl = hl @ w_in
    pc = hc @ w_in
    ql, kl, vl = mla_project(pl[..., C_WIDTH:], qa_w, w_qb, kva_w, w_kvb, qn_w, kn_w, cos, sin)
    qc, kc, vc = mla_project(pc[..., C_WIDTH:], qa_w, w_qb, kva_w, w_kvb, qn_w, kn_w, None, None)
    k_all = jnp.concatenate([kc, kl], axis=1)
    v_all = jnp.concatenate([vc, vl], axis=1)
    yl = jnp.concatenate([fourier_mix(pl[..., :C_WIDTH]), attend(ql, k_all, v_all)], -1) @ w_out
    yc = None
    if with_ctx:
        yc = jnp.concatenate([fourier_mix(pc[..., :C_WIDTH]), attend(qc, kc, vc)], -1) @ w_out
    return yl, yc

def conv_ffn(h, w_up, conv_w, conv_b, w_down):
    t_len = h.shape[1]
    up = h @ w_up
    gate, val = up[..., :D_FF], up[..., D_FF:]
    pad = CONV_W // 2
    gp = jnp.pad(gate, ((0, 0), (pad, pad), (0, 0)))
    gate_c = conv_b
    for j in range(CONV_W):
        gate_c = gate_c + gp[:, j:j + t_len] * conv_w[j]
    return (jax.nn.silu(gate_c) * val) @ w_down

def first_inputs(seed: int = 0) -> dict:
    key = jax.random.key(seed)
    ks = jax.random.split(key, 27)
    f32 = jnp.float32
    n_ev = (DEPTH + 1) // 2
    n_od = DEPTH // 2

    def normal(k, shape, scale):
        return jax.random.normal(k, shape, f32) * scale

    def gain(k, shape):
        return 1.0 + 0.02 * jax.random.normal(k, shape, f32)

    return {
        'x': normal(ks[0], (BATCH, SEQ, D_MODEL), 1.0),
        'c': normal(ks[1], (BATCH, D_MODEL), 1.0),
        'ctx': normal(ks[2], (BATCH, CTX_LEN, D_MODEL), 1.0),
        'c_ctx': normal(ks[3], (D_MODEL,), 1.0),
        'ada_w': normal(ks[4], (DEPTH, D_MODEL, 6 * D_MODEL), 0.5 * D_MODEL ** -0.5),
        'ada_b': normal(ks[5], (DEPTH, 6 * D_MODEL), 0.02),
        'norm_mix_w': gain(ks[6], (DEPTH, D_MODEL)),
        'norm_ffn_w': gain(ks[7], (DEPTH, D_MODEL)),
        'ev_w_in': normal(ks[8], (n_ev, D_MODEL, EV_IN), D_MODEL ** -0.5),
        'ev_lb_logits': normal(ks[9], (n_ev, 2, A_WIDTH), 1.0),
        'ev_onorm_w': gain(ks[10], (n_ev, A_HEAD_DIM)),
        'ev_vnorm_w': gain(ks[11], (n_ev, B_GROUPS, B_GROUP_DIM)),
        'ev_ws': normal(ks[12], (n_ev, B_GROUPS, B_CHUNK, B_CHUNK), B_CHUNK ** -0.5),
        'ev_bs': 1.0 + normal(ks[13], (n_ev, B_GROUPS, B_CHUNK), 0.1),
        'ev_w_out': normal(ks[14], (n_ev, D_MODEL, D_MODEL), D_MODEL ** -0.5),
        'od_w_in': normal(ks[15], (n_od, D_MODEL, OD_IN), D_MODEL ** -0.5),
        'od_qa_norm_w': gain(ks[16], (n_od, Q_LORA)),
        'od_w_qb': normal(ks[17], (n_od, Q_LORA, MLA_HEADS * MLA_QK), Q_LORA ** -0.5),
        'od_kva_norm_w': gain(ks[18], (n_od, KV_LORA)),
        'od_w_kvb': normal(ks[19], (n_od, KV_LORA, MLA_HEADS * (MLA_NOPE + MLA_V_DIM)), KV_LORA ** -0.5),
        'od_q_norm_w': gain(ks[20], (n_od, MLA_QK)),
        'od_k_norm_w': gain(ks[21], (n_od, MLA_QK)),
        'od_w_out': normal(ks[22], (n_od, D_MODEL, D_MODEL), D_MODEL ** -0.5),
        'ffn_w_up': normal(ks[23], (DEPTH, D_MODEL, 2 * D_FF), D_MODEL ** -0.5),
        'ffn_conv_w': normal(ks[24], (DEPTH, CONV_W, D_FF), CONV_W ** -0.5),
        'ffn_conv_b': normal(ks[25], (DEPTH, D_FF), 0.02),
        'ffn_w_down': normal(ks[26], (DEPTH, D_FF, D_MODEL), D_FF ** -0.5),
    }

def first_block(x, c, ctx, c_ctx, ada_w, ada_b, norm_mix_w, norm_ffn_w, ev_w_in, ev_lb_logits,
              ev_onorm_w, ev_vnorm_w, ev_ws, ev_bs, ev_w_out, od_w_in, od_qa_norm_w, od_w_qb,
              od_kva_norm_w, od_w_kvb, od_q_norm_w, od_k_norm_w, od_w_out, ffn_w_up, ffn_conv_w,
              ffn_conv_b, ffn_w_down):
    f32 = jnp.float32
    n_lat = x.shape[1]
    ROWS = n_lat // GRID_W
    row = jnp.repeat(jnp.arange(ROWS), GRID_W)
    col = jnp.tile(jnp.arange(GRID_W), ROWS)
    r_axis = MLA_ROPE // 2
    inv_freq = ROPE_THETA ** (-jnp.arange(0, r_axis, 2, dtype=f32) / r_axis)
    ang = jnp.stack([row, col], axis=-1).astype(f32)[:, :, None] * inv_freq
    cos = jnp.cos(ang).astype(x.dtype)
    sin = jnp.sin(ang).astype(x.dtype)
    lb_p = jax.nn.softmax(ev_lb_logits.astype(f32), axis=0)
    lbs = jnp.cumsum(lb_p, axis=0) - lb_p[0]

    silu_c = jax.nn.silu(c)
    silu_cc = jax.nn.silu(c_ctx)
    xl, xc = x, ctx
    for l in range(DEPTH):
        with_ctx = l < DEPTH - 1
        mod_l = (silu_c @ ada_w[l] + ada_b[l])[:, None, :]
        mod_c = (silu_cc @ ada_w[l] + ada_b[l])[None, None, :]
        sh1, sc1, g1, sh2, sc2, g2 = jnp.split(mod_l, 6, axis=-1)
        csh1, csc1, cg1, csh2, csc2, cg2 = jnp.split(mod_c, 6, axis=-1)
        hl = modulate(xl, norm_mix_w[l], sh1, sc1)
        hc = modulate(xc, norm_mix_w[l], csh1, csc1)
        if l % 2 == 0:
            e = l // 2
            yl, yc = even_mixer(hl, hc, ev_w_in[e], lbs[e], ev_onorm_w[e], ev_vnorm_w[e],
                                ev_ws[e], ev_bs[e], ev_w_out[e], with_ctx)
        else:
            o = l // 2
            yl, yc = odd_mixer(hl, hc, od_w_in[o], od_qa_norm_w[o], od_w_qb[o], od_kva_norm_w[o],
                               od_w_kvb[o], od_q_norm_w[o], od_k_norm_w[o], od_w_out[o],
                               cos, sin, with_ctx)
        xl = xl + g1 * yl
        xl = xl + g2 * conv_ffn(modulate(xl, norm_ffn_w[l], sh2, sc2), ffn_w_up[l],
                                ffn_conv_w[l], ffn_conv_b[l], ffn_w_down[l])
        if with_ctx:
            xc = xc + cg1 * yc
            xc = xc + cg2 * conv_ffn(modulate(xc, norm_ffn_w[l], csh2, csc2), ffn_w_up[l],
                                     ffn_conv_w[l], ffn_conv_b[l], ffn_w_down[l])
    return xl


HEAD_DIM = 64
MIX_WIDTH = D_MODEL
A_HEADS_2 = MIX_WIDTH // 2 // HEAD_DIM
A_PATTERNS = ((128, 1), (512, 4), (2048, 16))
B_HEADS = MIX_WIDTH // 2 // (2 * HEAD_DIM)
C_HEADS = MIX_WIDTH // HEAD_DIM
C_KV_HEADS = C_HEADS // 4
C_HALF_WINDOW = 128
Q_BLOCK = 128
A_WIDTH_2 = A_HEADS_2 * HEAD_DIM
B_QK_WIDTH = B_HEADS * 2 * HEAD_DIM
B_V_WIDTH = B_HEADS * 2 * HEAD_DIM
EVEN_IN = 3 * A_WIDTH_2 + 2 * B_QK_WIDTH + B_V_WIDTH + MIX_WIDTH
C_KV_WIDTH = C_KV_HEADS * HEAD_DIM
ODD_IN = MIX_WIDTH + 2 * C_KV_WIDTH + MIX_WIDTH
NEG_INF = -1e30


def rms_norm_2(x, g):
    x32 = x.astype(jnp.float32)
    y = x32 * lax.rsqrt(jnp.mean(x32 * x32, axis=-1, keepdims=True) + EPS)
    return (y * g.astype(jnp.float32)).astype(x.dtype)

def alibi_slopes(n):
    return 2.0 ** (-8.0 * jnp.arange(1, n + 1, dtype=jnp.float32) / n)

def banded_attention(q, k, v, slopes, spacing, W):
    B, G, R, L, dh = q.shape
    nb = -(-L // W)
    Lp = nb * W
    pad = Lp - L
    qb = jnp.pad(q, ((0, 0), (0, 0), (0, 0), (0, pad), (0, 0))).reshape(B, G, R, nb, W, dh)

    def windows(t):
        tp = jnp.pad(t, ((0, 0), (0, 0), (W, W + pad), (0, 0))).reshape(B, G, nb + 2, W, t.shape[-1])
        return jnp.concatenate([tp[:, :, 0:nb], tp[:, :, 1:nb + 1], tp[:, :, 2:nb + 2]], axis=3)

    kw, vw = windows(k), windows(v)
    s = jnp.einsum('bgrnid,bgncd->bgrnic', qb, kw, preferred_element_type=jnp.float32)
    blk = jnp.arange(nb)[:, None, None]
    qpos = blk * W + jnp.arange(W)[None, :, None]
    kpos = blk * W - W + jnp.arange(3 * W)[None, None, :]
    rel = jnp.abs(kpos - qpos)
    valid = (rel <= W) & (kpos >= 0) & (kpos < L)
    dist = (rel * spacing).astype(jnp.float32)
    s = s - slopes.astype(jnp.float32)[None, :, :, None, None, None] * dist
    s = jnp.where(valid, s, NEG_INF)
    m = jnp.max(s, axis=-1)
    p = jnp.exp(s - m[..., None])
    l = jnp.sum(p, axis=-1)
    acc = jnp.einsum('bgrnic,bgncd->bgrnid', p, vw.astype(jnp.float32))
    m = m.reshape(B, G, R, Lp)[..., :L]
    l = l.reshape(B, G, R, Lp)[..., :L]
    acc = acc.reshape(B, G, R, Lp, -1)[:, :, :, :L]
    return m, l, acc

def dilated_mixture_attention(q, k, v):
    B, H, S, dh = q.shape
    q = q * (dh ** -0.5)
    slopes = alibi_slopes(H)
    ms, ls, accs = [], [], []
    for window, dil in A_PATTERNS:
        L = S // dil
        half = window // (2 * dil)

        def to_res(t):
            return t.reshape(B, H, L, dil, t.shape[-1]).transpose(0, 1, 3, 2, 4).reshape(B, H * dil, L, t.shape[-1])

        def from_res(t):
            t = t.reshape((B, H, dil, L) + t.shape[3:])
            t = jnp.swapaxes(t, 2, 3)
            return t.reshape((B, H, S) + t.shape[4:])

        m, l, acc = banded_attention(to_res(q)[:, :, None], to_res(k), to_res(v),
                                     jnp.repeat(slopes, dil)[:, None], dil, half)
        ms.append(from_res(m[:, :, 0]))
        ls.append(from_res(l[:, :, 0]))
        accs.append(from_res(acc[:, :, 0]))
    m = jnp.stack(ms)
    w = jnp.exp(m - jnp.max(m, axis=0))
    num = jnp.sum(w[..., None] * jnp.stack(accs), axis=0)
    den = jnp.sum(w * jnp.stack(ls), axis=0)
    return num / den[..., None]

def differential_attention(q1, q2, k1, k2, v, lam, lam_init, subln_g):
    B, H, S, dh = q1.shape
    scale = dh ** -0.5
    slopes = alibi_slopes(H)
    kpos = jnp.arange(S)
    v32 = v.astype(jnp.float32)

    def block(n):
        start = n * Q_BLOCK
        qpos = start + jnp.arange(Q_BLOCK)
        bias = -slopes[:, None, None] * jnp.abs(qpos[:, None] - kpos[None, :]).astype(jnp.float32)

        def attn(q, k):
            qs = lax.dynamic_slice_in_dim(q, start, Q_BLOCK, axis=2)
            s = jnp.einsum('bhqd,bhkd->bhqk', qs, k, preferred_element_type=jnp.float32) * scale + bias
            return jax.nn.softmax(s, axis=-1)

        a = attn(q1, k1) - lam * attn(q2, k2)
        return jnp.einsum('bhqk,bhkd->bhqd', a, v32)

    out = lax.map(block, jnp.arange(S // Q_BLOCK))
    out = jnp.moveaxis(out, 0, 2).reshape(B, H, S, 2 * dh)
    return rms_norm_2(out, subln_g) * (1.0 - lam_init)

def even_mixer_2(h, w_in, w_out, lq1, lk1, lq2, lk2, subln_g, lam_init):
    B, S, _ = h.shape
    proj = h @ w_in
    cuts = np.cumsum([A_WIDTH_2] * 3 + [B_QK_WIDTH] * 2 + [B_V_WIDTH]).tolist()
    qa, ka, va, qb, kb, vb, g = jnp.split(proj, cuts, axis=-1)

    def heads(t, n):
        return t.reshape(B, S, n, -1).transpose(0, 2, 1, 3)

    ya = dilated_mixture_attention(heads(qa, A_HEADS_2), heads(ka, A_HEADS_2), heads(va, A_HEADS_2))
    qb, kb, vb = heads(qb, B_HEADS), heads(kb, B_HEADS), heads(vb, B_HEADS)
    f32 = jnp.float32
    lam = (jnp.exp(jnp.sum(lq1.astype(f32) * lk1.astype(f32)))
           - jnp.exp(jnp.sum(lq2.astype(f32) * lk2.astype(f32))) + lam_init)
    yb = differential_attention(qb[..., :HEAD_DIM], qb[..., HEAD_DIM:],
                                kb[..., :HEAD_DIM], kb[..., HEAD_DIM:], vb, lam, lam_init, subln_g)
    y = jnp.concatenate([ya.transpose(0, 2, 1, 3).reshape(B, S, A_WIDTH_2),
                         yb.transpose(0, 2, 1, 3).reshape(B, S, B_V_WIDTH)], axis=-1).astype(h.dtype)
    return (y * jax.nn.silu(g)) @ w_out

def odd_mixer_2(h, w_in, w_out, sink):
    B, S, _ = h.shape
    R = C_HEADS // C_KV_HEADS
    proj = h @ w_in
    q, k, v, g = jnp.split(proj, [MIX_WIDTH, MIX_WIDTH + C_KV_WIDTH, MIX_WIDTH + 2 * C_KV_WIDTH], axis=-1)
    q = q.reshape(B, S, C_KV_HEADS, R, HEAD_DIM).transpose(0, 2, 3, 1, 4) * (HEAD_DIM ** -0.5)
    k = k.reshape(B, S, C_KV_HEADS, HEAD_DIM).transpose(0, 2, 1, 3)
    v = v.reshape(B, S, C_KV_HEADS, HEAD_DIM).transpose(0, 2, 1, 3)
    slopes = alibi_slopes(C_HEADS).reshape(C_KV_HEADS, R)
    m, l, acc = banded_attention(q, k, v, slopes, 1, C_HALF_WINDOW)
    sk = sink.astype(jnp.float32).reshape(C_KV_HEADS, R)[None, :, :, None]
    M = jnp.maximum(m, sk)
    e = jnp.exp(m - M)
    y = acc * e[..., None] / (l * e + jnp.exp(sk - M))[..., None]
    y = y.transpose(0, 3, 1, 2, 4).reshape(B, S, MIX_WIDTH).astype(h.dtype)
    return (y * jax.nn.silu(g)) @ w_out

def second_inputs(seed: int = 0) -> dict:
    key = jax.random.key(seed)
    ks = jax.random.split(key, 16)
    n_even = (DEPTH + 1) // 2
    n_odd = DEPTH // 2

    def nrm(k, shape, scale):
        return jax.random.normal(k, shape, jnp.float32) * scale

    return {
        "x": nrm(ks[0], (BATCH, SEQ, D_MODEL), 1.0),
        "c": nrm(ks[1], (BATCH, D_MODEL), 1.0),
        "ada_w": nrm(ks[2], (DEPTH, D_MODEL, 3 * D_MODEL), 0.5 * D_MODEL ** -0.5),
        "ada_b": nrm(ks[3], (DEPTH, 3 * D_MODEL), 0.02),
        "norm_g": 1.0 + nrm(ks[4], (DEPTH, D_MODEL), 0.05),
        "ab_w_in": nrm(ks[5], (n_even, D_MODEL, EVEN_IN), D_MODEL ** -0.5),
        "ab_w_out": nrm(ks[6], (n_even, MIX_WIDTH, D_MODEL), MIX_WIDTH ** -0.5),
        "diff_lq1": nrm(ks[7], (n_even, HEAD_DIM), 0.1),
        "diff_lk1": nrm(ks[8], (n_even, HEAD_DIM), 0.1),
        "diff_lq2": nrm(ks[9], (n_even, HEAD_DIM), 0.1),
        "diff_lk2": nrm(ks[10], (n_even, HEAD_DIM), 0.1),
        "diff_subln_g": 1.0 + nrm(ks[11], (n_even, 2 * HEAD_DIM), 0.05),
        "c_w_in": nrm(ks[12], (n_odd, D_MODEL, ODD_IN), D_MODEL ** -0.5),
        "c_w_out": nrm(ks[13], (n_odd, MIX_WIDTH, D_MODEL), MIX_WIDTH ** -0.5),
        "c_sink": nrm(ks[14], (n_odd, C_HEADS), 1.0),
        "final_g": 1.0 + nrm(ks[15], (D_MODEL,), 0.05),
    }

def second_block(x, c, ada_w, ada_b, norm_g, ab_w_in, ab_w_out, diff_lq1, diff_lk1,
              diff_lq2, diff_lk2, diff_subln_g, c_w_in, c_w_out, c_sink, final_g):
    cs = jax.nn.silu(c)
    for layer in range(DEPTH):
        mod = cs @ ada_w[layer] + ada_b[layer]
        shift, scale, gate = jnp.split(mod, 3, axis=-1)
        h = rms_norm_2(x, norm_g[layer]) * (1.0 + scale[:, None, :]) + shift[:, None, :]
        j = layer // 2
        if layer % 2 == 0:
            lam_init = 0.8 - 0.6 * math.exp(-0.3 * layer)
            y = even_mixer_2(h, ab_w_in[j], ab_w_out[j], diff_lq1[j], diff_lk1[j],
                           diff_lq2[j], diff_lk2[j], diff_subln_g[j], lam_init)
        else:
            y = odd_mixer_2(h, c_w_in[j], c_w_out[j], c_sink[j])
        x = x + gate[:, None, :] * y
    return rms_norm_2(x, final_g)


def setup_inputs(seed=0):
    out = dict(first_inputs(seed))
    for name, value in second_inputs(seed + 1).items():
        if name != "x":
            out[name + "_2"] = value
    return out


def reference(
    x, c, ctx, c_ctx, ada_w, ada_b, norm_mix_w, norm_ffn_w, ev_w_in, ev_lb_logits, ev_onorm_w,
    ev_vnorm_w, ev_ws, ev_bs, ev_w_out, od_w_in, od_qa_norm_w, od_w_qb, od_kva_norm_w, od_w_kvb,
    od_q_norm_w, od_k_norm_w, od_w_out, ffn_w_up, ffn_conv_w, ffn_conv_b, ffn_w_down, c_2,
    ada_w_2, ada_b_2, norm_g_2, ab_w_in_2, ab_w_out_2, diff_lq1_2, diff_lk1_2, diff_lq2_2,
    diff_lk2_2, diff_subln_g_2, c_w_in_2, c_w_out_2, c_sink_2, final_g_2,
):
    x = first_block(
        x, c, ctx, c_ctx, ada_w, ada_b, norm_mix_w, norm_ffn_w, ev_w_in, ev_lb_logits,
        ev_onorm_w, ev_vnorm_w, ev_ws, ev_bs, ev_w_out, od_w_in, od_qa_norm_w, od_w_qb,
        od_kva_norm_w, od_w_kvb, od_q_norm_w, od_k_norm_w, od_w_out, ffn_w_up, ffn_conv_w,
        ffn_conv_b, ffn_w_down,
    )
    return second_block(
        x, c_2, ada_w_2, ada_b_2, norm_g_2, ab_w_in_2, ab_w_out_2, diff_lq1_2, diff_lk1_2,
        diff_lq2_2, diff_lk2_2, diff_subln_g_2, c_w_in_2, c_w_out_2, c_sink_2, final_g_2,
    )


_drawn_inputs = setup_inputs


def setup_inputs(seed=0):
    import zlib

    import numpy as np

    out = dict(_drawn_inputs(seed))
    spreads = {}
    factors = {'ctx': 6.542,
     'norm_mix_w': 7.765,
     'norm_ffn_w': 6.514,
     'ev_onorm_w': 8.0,
     'ev_vnorm_w': 8.0,
     'ev_bs': 3.59,
     'od_qa_norm_w': 8.0,
     'od_w_qb': 2.852,
     'od_kva_norm_w': 8.0,
     'od_q_norm_w': 8.0,
     'od_k_norm_w': 8.0,
     'ffn_conv_b': 8.0,
     'ada_b_2': 4.487,
     'norm_g_2': 5.438,
     'diff_lq1_2': 8.0,
     'diff_lk1_2': 8.0,
     'diff_lq2_2': 8.0,
     'diff_lk2_2': 8.0,
     'diff_subln_g_2': 8.0,
     'c_sink_2': 5.434}
    for name, (base, spread) in spreads.items():
        noise = np.random.default_rng([zlib.crc32(name.encode()), seed]).standard_normal(out[name].shape)
        drawn = base * np.exp(spread * noise) if base else spread * noise
        out[name] = jnp.asarray(drawn.astype(out[name].dtype))
    for name, factor in factors.items():
        out[name] = (out[name] * factor).astype(out[name].dtype)
    return out
```

```python
from contextlib import ExitStack

import numpy as np
import concourse.bass as bass
from concourse import mybir

F32 = mybir.dt.float32
U32 = mybir.dt.uint32
ALU = mybir.AluOpType
ACT = mybir.ActivationFunctionType
AX = mybir.AxisListType

P = 128
D = 1024
KT = D // P
S = 512
CTX = 256
T = S + CTX
SEGS = [(0, S), (S, CTX)]
FF = 2816
FT = FF // P
EPS = 1e-6
F_MIN = 1e-6
HEADS_M = 6
NSLOT = 3
SLOT = FF
LEVELS = (64, 32, 16, 8, 4)
LEAF = 4
LAM_INIT = 0.8 - 0.6
WINDOW = 128

CONST = dict(ident=P, ones=P, ones64=P, rot=P, masks=12 * P, scan=T + 1)
VECS = dict(
    c=KT, cc=KT, c2=KT, ab0=48, ab1=48, ab2=24, ab3=24, nm0=KT, nm1=KT, nf0=KT, nf1=KT, ng0=KT, ng1=KT,
    fg=KT, lb=8, onorm=1, cw0=3 * FT, cw1=3 * FT, cb0=FT, cb1=FT, qa=3, kva=2, qn=1, qp=1, kn=1, kp=1,
    subln=1, lam=4 * 64, sink=16,
)


def offsets(table):
    at, out = 0, {}
    for name, n in table.items():
        out[name] = (at, at + n)
        at += n
    return out, at


CONST_AT, CONST_N = offsets(CONST)
VECS_AT, VECS_N = offsets(VECS)

WEIGHTS = dict(
    ada0=(24, 2048, (0, 1, 2)), ada1=(24, 2048, (0, 1, 2)), ada2=(12, 2048, (0, 1, 2)), ada3=(12, 2048, (0, 1, 2)),
    win0=(5, 2048, (0, 1, 2)), win1=(5, 2048, (0, 1, 2)), wmlp=(4, 2048, (0, 1, 2)), wout0=(4, 2048, (0, 1, 2)),
    up0=(22, 2048, (0, 1)), down0=(8, 2816, (0, 1)),
    winM=(4, 2048, (0, 1, 2)), qb=(3, 1152, (0, 1, 2)), kvb=(3, 1024, (0, 1, 2)), woutM=(4, 2048, (0, 1, 2)),
    up1=(22, 2048, (0, 1)), down1=(8, 2816, (0, 1)),
    winE=(16, 2048, (0, 1, 2)), woutE=(4, 2048, (0, 1, 2)),
    winC=(10, 2048, (0, 1, 2)), woutC=(4, 2048, (0, 1, 2)),
)
B8 = tuple(range(8))
SUMS = dict(
    ada0=(1, (0,)), ada1=(1, (1,)), ada2=(1, (2,)), ada3=(1, (3,)),
    n0=(2, B8), win0=(22, B8), hgS0=(36, (0, 1, 2)), hgK0=(6, (3,)), hgO0=(12, (4, 5)), hgU0=(10, (6, 7)), ro0=(4, B8),
    win1=(22, B8), hgS1=(36, (0, 1, 2)), hgK1=(6, (3,)), hgO1=(12, (4, 5)), hgU1=(10, (6, 7)), ro1=(4, B8),
    wmlp=(20, B8), sv=(8, B8), wout0=(16, B8),
    n1=(2, B8), up0=(88, B8), down0=(16, B8),
    n2=(2, B8), winM=(11, B8), nlat=(5, B8), ropek=(1, B8), qb=(9, B8), kvb=(30, B8), nqk=(21, B8), ropeq=(3, B8),
    fa=(4, B8), fb=(2, B8),
    mS=(24, (0, 2)), mT=(24, (4,)), mV=(6, (6, 7)), woutM=(8, B8),
    n3=(1, B8), up1=(44, (0, 1, 2, 3)), down1=(8, (0, 1, 2, 3)),
    n4=(1, B8), winE=(40, B8), aS=(32, (0, 1, 2)), aT=(32, (3, 4, 5)), aV=(4, (6, 7)),
    bS=(32, (0, 1, 2)), bT=(16, (3, 4, 5)), bV=(4, (6, 7)), nB=(4, B8), woutE=(8, B8),
    n5=(1, B8), winC=(22, B8), cS=(64, (0, 1, 2)), cT=(64, (3, 4, 5)), cV=(8, (6, 7)), woutC=(8, B8),
    n6=(1, B8),
)


def uses(table, n_rings, ring):
    total, out = [0] * n_rings, {}
    for name, row in table.items():
        n, places = row[0], row[ring]
        out[name] = {b: total[b] for b in places}
        for k in range(n):
            total[places[k % len(places)]] += 1
    return out


SLOT_USED = uses(WEIGHTS, NSLOT, 2)
BANK_USED = uses(SUMS, 8, 1)


def slot_use(stage, k, loops=0):
    ring = WEIGHTS[stage][2]
    s = ring[k % len(ring)]
    return s, loops + (SLOT_USED[stage][s] + k // len(ring))


def bank_use(stage, k, loops=0):
    ring = SUMS[stage][1]
    b = ring[k % len(ring)]
    return b, loops + (BANK_USED[stage][b] + k // len(ring))


BANKS_BEFORE = {}
_n = [0] * 8
for _name, (_k, _places) in SUMS.items():
    BANKS_BEFORE[_name] = list(_n)
    for _j in range(_k):
        _n[_places[_j % len(_places)]] += 1
NORM_STAGES = [x for x in SUMS if x in ("n0", "ro0", "ro1", "n1", "n2", "nlat", "nqk", "n3", "n4", "nB", "n5", "n6")]
NORMS_UP_TO = {x: sum(SUMS[y][0] for y in NORM_STAGES[:NORM_STAGES.index(x) + 1]) for x in NORM_STAGES}

PASSES = dict(a=(8, 1), b=(4, 2), c=(16, 1))
HEADS_BEFORE = dict(a=0, b=8, c=12)
PROBS_BEFORE = dict(a=0, b=32, c=64)
BANDED_ORDER = [8 * a + r + 4 * x for a in range(2) for r in range(4) for x in range(2)]


class Step:

    def __init__(self, eng, sem):
        self.eng, self.sem, self.n = eng, sem, 0

    def mark(self, ins):
        self.n += 1
        ins.then_inc(self.sem, 1)
        return self.n

    def link(self, ins):
        self.eng.wait_ge(self.sem, self.mark(ins))

    def settle(self):
        if self.n:
            self.eng.wait_ge(self.sem, self.n)


def hgrn_steps():
    out = []
    for i in range(3):
        fwd = (4, 5) if i == 0 else (2 * i - 2, 2 * i - 1)
        bwd = (5, 4) if i == 0 else (5 - 2 * i, 4 - 2 * i)
        out += [(0, fwd, i), (1, bwd, i)]
    return out


def two_blocks(nc, dram, out):
    with ExitStack() as ctx:
        def sb(name, *shape):
            return ctx.enter_context(nc.sbuf_tensor(name, [P, *shape], F32))

        def sem(name):
            return ctx.enter_context(nc.semaphore(name))

        ps = ctx.enter_context(nc.psum_tensor("ps", [P, 8, 512], F32))
        const, vecs = sb("const", CONST_N), sb("vecs", VECS_N)
        XL, XC = sb("XL", KT, S), sb("XC", KT, CTX)
        HL, HC = sb("HL", KT, S), sb("HC", KT, CTX)
        ring = sb("ring", NSLOT, SLOT)
        mod = sb("mod", 2, 48, 2)
        mod2 = sb("mod2", 2, 24)
        gain = sb("gain", 4, KT, 2)
        gain2 = sb("gain2", 2, KT)
        cs = sb("cs", KT, 2)
        cs2 = sb("cs2", KT)
        small = sb("small", 96)
        SQ = sb("SQ", 2, S)
        R = sb("R", 2, S)
        ARENA = 26200
        arena = sb("arena", ARENA)

        def C(name):
            a, b = CONST_AT[name]
            return const[:, a:b]

        def V(name, k=None):
            a, b = VECS_AT[name]
            return vecs[:, a:b] if k is None else vecs[:, a + k:a + k + 1]

        def carve(*shapes, at=0):
            views = []
            for shape in shapes:
                n = int(np.prod(shape))
                v = arena[:, at:at + n]
                if len(shape) > 1:
                    names = [f"d{i}" for i in range(len(shape))]
                    v = v.rearrange(f"p ({' '.join(names)}) -> p {' '.join(names)}",
                                    **dict(zip(names[1:], shape[1:])))
                views.append(v)
                at += n
            assert at <= ARENA, at
            return views

        X, H = (XL, XC), (HL, HC)
        ident = C("ident")
        masks = C("masks").rearrange("p (l n) -> p l n", n=P)

        bank_full = [sem(f"bank_full{b}") for b in B8]
        bank_free = [sem(f"bank_free{b}") for b in B8]
        slot_full = [sem(f"slot_full{s}") for s in range(NSLOT)]
        slot_free = [sem(f"slot_free{s}") for s in range(NSLOT)]
        act_step, dve_step, pool_step = sem("act_step"), sem("dve_step"), sem("pool_step")
        const_in = sem("const_in")
        mods_ready = sem("mods_ready")
        cs_ready = sem("cs_ready")
        sq_ready, sq_used = sem("sq_ready"), sem("sq_used")
        norm_done = sem("norm_done")
        h_ready = sem("h_ready")
        lb_step = sem("lb_step")
        out_done = sem("out_done")

        def bank_ap(stage, k):
            return ps[:, bank_use(stage, k)[0], :]

        def open_bank(eng, stage, k, loops=0):
            b, used = bank_use(stage, k, loops)
            if not (isinstance(used, int) and used == 0):
                eng.wait_ge(bank_free[b], used)
            return ps[:, b, :]

        def sums_done(ins, stage, k):
            ins.then_inc(bank_full[bank_use(stage, k)[0]], 1)

        def await_sums(eng, stage, k, loops=0):
            b, used = bank_use(stage, k, loops)
            eng.wait_ge(bank_full[b], used + 1)
            return ps[:, b, :]

        def taken(ins, stage, k):
            ins.then_inc(bank_free[bank_use(stage, k)[0]], 1)

        def await_taken(eng, stage, k, loops=0):
            b, used = bank_use(stage, k, loops)
            eng.wait_ge(bank_free[b], used + 1)

        def await_all_taken(eng, stage, n=None):
            n = SUMS[stage][0] if n is None else n
            for k in range(max(0, n - len(SUMS[stage][1])), n):
                await_taken(eng, stage, k)

        def await_chunk(eng, stage, k, loops=0):
            s, used = slot_use(stage, k, loops)
            eng.wait_ge(slot_full[s], (used + 1) * 16)
            return ring[:, s, :]

        def chunk_done(ins, stage, k):
            ins.then_inc(slot_free[slot_use(stage, k)[0]], 1)

        def load_chunk(eng, stage, k, row, loops=0):
            s, used = slot_use(stage, k, loops)
            if not (isinstance(used, int) and used == 0):
                eng.wait_ge(slot_free[s], used)
            L = WEIGHTS[stage][1]
            eng.dma_start(ring[:, s, 0:L], dram[stage][row]).then_inc(slot_full[s], 16)

        class Norms:

            def __init__(self, eng, step=None):
                self.eng, self.step, self.sq, self.items = eng, step, 0, 0

            def squares(self, srcs):
                for src in srcs:
                    if self.sq >= 2:
                        self.eng.wait_ge(sq_used, self.sq - 1)
                    n = src.shape[-1]
                    nc.scalar.activation(SQ[:, self.sq % 2, 0:n], src, ACT.Square).then_inc(sq_ready, 1)
                    self.sq += 1

            def mean(self, stage, k, ones, srcs):
                bank = open_bank(self.eng, stage, k)
                n = srcs[0].shape[-1]
                for j, src in enumerate(srcs):
                    self.eng.wait_ge(sq_ready, self.sq + 1)
                    ins = nc.tensor.matmul(bank[:, 0:n], ones, SQ[:, self.sq % 2, 0:n],
                                           start=(j == 0), stop=(j == len(srcs) - 1))
                    ins.then_inc(sq_used, 1)
                    self.sq += 1
                self.eng.wait_ge(sq_used, self.sq)
                self.eng.sem_inc(bank_full[bank_use(stage, k)[0]], 1)

            def root(self, stage, k, n, width):
                if self.items >= 2:
                    self.eng.wait_ge(norm_done, self.items - 1)
                bank = await_sums(self.eng, stage, k)
                taken(nc.scalar.activation(R[:, self.items % 2, 0:n], bank[:, 0:n], ACT.Sqrt,
                                           bias=small[:, 0:1], scale=1.0 / width), stage, k)
                self.items += 1

            def scale(self, stage, k, srcs, gains, dsts, shifts=None, done=None):
                await_taken(self.eng, stage, k)
                n = srcs[0].shape[-1]
                r = R[:, self.items % 2, 0:n]
                self.step.link(nc.vector.reciprocal(r, r))
                for j, (src, g, dst) in enumerate(zip(srcs, gains, dsts)):
                    ins = nc.vector.scalar_tensor_tensor(dst, src, g, r, ALU.mult, ALU.mult)
                    if j == len(srcs) - 1:
                        ins.then_inc(norm_done, 1)
                    elif shifts:
                        self.step.mark(ins)
                self.items += 1
                if shifts:
                    self.step.settle()
                    self.eng.wait_ge(norm_done, self.items)
                    for j, dst in enumerate(dsts):
                        ins = nc.vector.tensor_scalar(dst, dst, shifts[j], None, ALU.add)
                    ins.then_inc(done, 1)

        def modulated(l, which, segs):
            items = []
            for s in segs:
                x, h = X[s], H[s]
                items.append(([x[:, k, :] for k in range(KT)], (C("ones"), D),
                              [gain[:, 2 * l + which, k, s:s + 1] for k in range(KT)],
                              [h[:, k, :] for k in range(KT)],
                              [mod[:, l, 24 * which + k, s:s + 1] for k in range(KT)]))
            return items

        def modulated2(l):
            return [([XL[:, k, :] for k in range(KT)], (C("ones"), D), [gain2[:, l, k:k + 1] for k in range(KT)],
                     [HL[:, k, :] for k in range(KT)], [mod2[:, l, k:k + 1] for k in range(KT)])]

        def norm_act(nrm, stage, items, before=None):
            for k, it in enumerate(items):
                if before:
                    before(k)
                nrm.squares(it[0])
                if k:
                    nrm.root(stage, k - 1, items[k - 1][0][0].shape[-1], items[k - 1][1][1])
            nrm.root(stage, len(items) - 1, items[-1][0][0].shape[-1], items[-1][1][1])

        def norm_pe(nrm, stage, items):
            for k, it in enumerate(items):
                nrm.mean(stage, k, it[1][0], it[0])

        def norm_dve(nrm, stage, items, done=None):
            for k, it in enumerate(items):
                nrm.scale(stage, k, it[0], it[2], it[3], it[4], done)

        def features(pe, stage, sums, g, w, kt, m, width, src, segs, loops=0, last=None, kmaj=None):
            for i, s in enumerate(segs):
                bank = open_bank(pe, sums, g + i, loops)
                n = SEGS[s][1]
                for k in range(kt):
                    ins = nc.tensor.matmul(bank[:, 0:n], w[:, k * width + m:k * width + m + P], src(s, k),
                                           start=(k == 0), stop=(k == kt - 1))
                sums_done(ins, sums, g + i)
            return g + len(segs)

        def tokens(pe, sums, g, w, kt, width, m0, n, src, tiles):
            for t in tiles:
                bank = open_bank(pe, sums, g)
                for k in range(kt):
                    ins = nc.tensor.matmul(bank[:, 0:n], src(t, k), w[:, k * width + m0:k * width + m0 + n],
                                           start=(k == 0), stop=(k == kt - 1))
                sums_done(ins, sums, g)
                g += 1
            return g

        def h_seg(s, k):
            return H[s][:, k, :]

        def h_tok(t, k):
            return HL[:, k, t * P:(t + 1) * P] if t < 4 else HC[:, k, (t - 4) * P:(t - 3) * P]

        def release(pe, stage, k, sums, g, loops=0):
            await_sums(pe, sums, g, loops)
            pe.sem_inc(slot_free[slot_use(stage, k)[0]], 1)

        Y, = carve((8, T))
        (A_q, A_k0, A_b0, A_k1, A_b1, A_v, A_g, WK, ACC, KD, ST, EL) = carve(
            (2, T), (2, T), (2, T), (2, T), (2, T), (6, 256), (2, T), (2, 9, 2, 2, P), (2, 2, 2, P), (2, 2, 2, P),
            (2, 2, 2, P), (2, 2, 2), at=4 * T)
        A_k, A_b = (A_k0, A_k1), (A_b0, A_b1)
        U, VB, VNW, BSB, WST, MT, VSQ = carve((4, T), (24, P), (4, P), (4, P), (4, P), (2, S), (24, P), at=8 * T)
        VB4 = VB.rearrange("p (t q) n -> p t q n", q=4)
        ssq, rsq = small[:, 8:32], small[:, 32:56]
        G, FA = carve((FT, T), (2, T))

        hg_q = sem("hg_q")
        hg_g = sem("hg_g")
        hg_b = sem("hg_b")
        hg_e = sem("hg_e")
        hg_f = sem("hg_f")
        hg_ln = sem("hg_ln")
        hg_diff = sem("hg_diff")
        hg_exp = sem("hg_exp")
        hg_ops = sem("hg_ops")
        hg_acc = sem("hg_acc")
        hg_st = sem("hg_st")
        hg_round = sem("hg_round")
        mlp_v = sem("mlp_v")
        mlp_u = sem("mlp_u")
        mlp_tab = sem("mlp_tab")
        y_ready = sem("y_ready")

        STEPS = hgrn_steps()
        STATE_NO = {}
        for _d, _chunks, _i in STEPS:
            for _j in range(2):
                if 2 * _i + _j < 5:
                    STATE_NO[(_d, 2 * _i + _j)] = len(STATE_NO)

        def half(ap, m, second):
            v = ap.rearrange("p h (g x) -> p h g x", x=2 * m)
            return v[:, :, :, m:2 * m] if second else v[:, :, :, 0:m]

        def wk(w, a):
            return WK[:, w, a, :, :, :].rearrange("p h c n -> p h (c n)")

        def tok(buf, chunks):
            t0 = min(chunks) * P
            return buf[:, :, t0:t0 + 2 * P]

        def readout_items(r):
            return [([Y[:, 2 * r + j, a:a + n]], (C("ones"), P), [V("onorm", 0)], [Y[:, 2 * r + j, a:a + n]], None)
                    for j in range(2) for a, n in SEGS]

        def seg_of(buf, k, s):
            return buf[:, k, SEGS[s][0]:SEGS[s][0] + SEGS[s][1]]

        def lat_items():
            q = [M_QL[:, k, :] for k in range(3)]
            items = [(q, (C("ones"), 3 * P), [V("qa", k) for k in range(3)], q, None)]
            for s in range(2):
                kv = [seg_of(M_KV, k, s) for k in range(2)]
                items.append((kv, (C("ones"), 2 * P), [V("kva", k) for k in range(2)], kv, None))
            for s in range(2):
                pe_ = [seg_of(M_PE, 0, s)]
                items.append((pe_, (C("ones64"), 64), [V("kp", 0)], pe_, None))
            return items

        def qk_items():
            tiles = [(M_QN[:, h, :], C("ones"), P, V("qn", 0)) for h in range(6)]
            tiles += [(M_QP[:, j, :], C("ones64"), 64, V("qp", 0)) for j in range(3)]
            tiles += [(seg_of(M_KN, h, s), C("ones"), P, V("kn", 0)) for h in range(6) for s in range(2)]
            return [([x], (o, w), [g], [x], None) for x, o, w, g in tiles]

        def subln_items():
            return [([HL[:, 4 + h, :]], (C("ones"), P), [small[:, 6:7]], [HL[:, 4 + h, :]], None) for h in range(4)]

        def final_items():
            return [([XL[:, k, :] for k in range(KT)], (C("ones"), D), [V("fg", k) for k in range(KT)],
                     [HL[:, k, :] for k in range(KT)], None)]

        ffn_tap = [sem("ffn_tap0"), sem("ffn_tap1")]
        ffn_silu = [sem("ffn_silu0"), sem("ffn_silu1")]

        (M_C, M_QL, M_KV, M_PE, M_QN, M_QP, M_KN, M_V, M_P, M_T, M_COS, M_SIN) = carve(
            (2, S), (3, S), (2, T), (1, T), (6, S), (3, S), (6, T), (6, 6, P), (2, T), (6, S), (S,), (S,))
        M_T2, = carve((6, S), at=2 * S)
        M_PT = (M_T, M_T2)
        M_AB, = carve((4, 2, 2 * P), at=2 * S)
        M_DFT, = carve((8, S), at=2 * S + 3 * S + 2 * T + T + 6 * S + 3 * S + 6 * T + 6 * T)
        M_TMP = M_T[:, 5, :]
        M_CC, = carve((2 * P,), at=ARENA - 2 * P)
        M_DG, = carve((2, P), at=ARENA - 4 * P)
        YM = HL
        m_tab = sem("m_tab")
        m_dft = sem("m_dft")
        m_rope = sem("m_rope")
        m_max = sem("m_max")
        m_diag = sem("m_diag")

        (E_QA, E_KA, E_VA, E_QB, E_KB, E_VB, E_G, E_S, E_P, E_T, E_BIAS, E_DG) = carve(
            (4, S), (4, S), (4, 4, P), (4, S), (4, S), (4, 4, P), (8, S), (2, S), (4, S), (2, 4, S), (2, 896), (4, P))
        (C_Q, C_K, C_V, C_G) = carve((8, S), (2, S), (4, 2, P), (8, S))
        C_BIAS = E_BIAS[:, :, 0:384]
        e_bias = [sem("e_bias0"), sem("e_bias1")]
        e_p, e_dg = sem("e_p"), sem("e_dg")
        SINKS = small[:, 24:40]
        e_head = sem("e_head")
        lam_sem = sem("lam_sem")

        def key_tiles(kind, i):
            return range(4) if kind != "c" else range(max(0, i - 1), min(4, i + 2))

        block = ctx.enter_context(nc.Block())

        @block.sync
        def _(sp):
            sp.dma_start(vecs[:, :], dram["vecs"]).then_inc(const_in, 16)
            sp.dma_start(const[:, :], dram["const"]).then_inc(const_in, 16)
            sp.dma_start(XL[:, :, :], dram["xl"]).then_inc(const_in, 16)
            sp.dma_start(XC[:, :, :], dram["xc"]).then_inc(const_in, 16)
            for stage, (n, _, slots) in WEIGHTS.items():
                body = len(slots)
                first = body if SLOT_USED[stage][slots[0]] == 0 else 0
                for k in range(first):
                    load_chunk(sp, stage, k, k)
                rounds = n // body
                if rounds > 1:
                    with sp.Fori(first // body, rounds) as i:
                        for k in range(body):
                            load_chunk(sp, stage, k, i * body + k, i)
                for k in range(rounds * body if rounds > 1 else first, n):
                    load_chunk(sp, stage, k, k)
            sp.wait_ge(norm_done, NORMS_UP_TO["n6"])
            sp.dma_start(out, HL[:, :, :]).then_inc(out_done, 16)
            sp.wait_ge(out_done, 16)

        @block.tensor
        def _(pe):
            nrm = Norms(pe)

            def mods(stage, vec, n):
                rounds = WEIGHTS[stage][0] // NSLOT
                w_ = vec.shape[-1] if len(vec.shape) == 3 else 1
                bank = open_bank(pe, stage, 0)
                with pe.Fori(0, rounds) as i:
                    for c in range(NSLOT):
                        w = await_chunk(pe, stage, c, i)
                        for m in range(2):
                            for k in range(KT):
                                ins = nc.tensor.matmul(
                                    ps[:, SUMS[stage][1][0], bass.ds((i * NSLOT + c) * 2 * w_ + m * w_, w_)],
                                    w[:, k * 256 + m * P:k * 256 + (m + 1) * P],
                                    vec[:, k, :] if w_ == 2 else vec[:, k:k + 1],
                                    start=(k == 0), stop=(k == KT - 1))
                        chunk_done(ins, stage, c)
                s, used = slot_use(stage, WEIGHTS[stage][0] - 1)
                pe.wait_ge(slot_free[s], used + 1)
                pe.sem_inc(bank_full[bank_use(stage, 0)[0]], 1)

            pe.wait_ge(const_in, 64)
            pe.wait_ge(cs_ready, 3)
            mods("ada0", cs, 2)
            mods("ada1", cs, 2)
            mods("ada2", cs2, 1)
            mods("ada3", cs2, 1)

            norm_pe(nrm, "n0", modulated(0, 0, (0, 1)))
            pe.wait_ge(h_ready, 2)

            def hgrn(r):
                win, SS, SK, SO, SU = (f"{x}{r}" for x in ("win", "hgS", "hgK", "hgO", "hgU"))
                g = 0
                for c in range(5):
                    w = await_chunk(pe, win, c)
                    if c == 3:
                        g = tokens(pe, win, g, w, KT, 256, 0, 256, h_tok, range(6))
                    else:
                        for m in range(2):
                            g = features(pe, win, win, g, w, KT, m * P, 256, h_seg, (0, 1))
                    release(pe, win, c, win, g - 1)

                def scores(n):
                    w = n % 2
                    pe.wait_ge(hg_ops, 6 * r + n + 1)
                    for l in range(6):
                        bank = open_bank(pe, SS, 6 * n + l).rearrange("p (h c t) -> p h c t", h=2, c=2)
                        ka, qa = (l, l) if l < 5 else (6, 5)
                        for h in range(2):
                            for c in range(2):
                                ins = nc.tensor.matmul(bank[:, h, c, :], WK[:, w, ka, h, c, :], WK[:, w, qa, h, c, :],
                                                       start=True, stop=True)
                        sums_done(ins, SS, 6 * n + l)
                    bank = open_bank(pe, SK, n).rearrange("p (h c t) -> p h c t", h=2, c=2)
                    for h in range(2):
                        for c in range(2):
                            ins = nc.tensor.transpose(bank[:, h, c, :], WK[:, w, 7, h, c, :], ident)
                    sums_done(ins, SK, n)

                def outputs(n):
                    d, chunks, i = STEPS[n]
                    w, lo = n % 2, min(chunks)
                    pe.wait_ge(hg_acc, 6 * r + n + 1)
                    await_taken(pe, SK, n)
                    for j, ch in enumerate(chunks):
                        c, q = ch - lo, 2 * i + j
                        if q:
                            pe.wait_ge(hg_st, 10 * r + STATE_NO[(d, q - 1)] + 1)
                        bank = open_bank(pe, SO, 2 * n + j)
                        for h in range(2):
                            ins = nc.tensor.matmul(bank[:, h * P:(h + 1) * P], A_v[:, ch, h * P:(h + 1) * P],
                                                   ACC[:, w, h, c, :], start=True, stop=(q == 0))
                            if q:
                                ins = nc.tensor.matmul(bank[:, h * P:(h + 1) * P], ST[:, d, (q - 1) % 2, h, :],
                                                       WK[:, w, 8, h, c, :], start=False, stop=True)
                        sums_done(ins, SO, 2 * n + j)
                        if q < 5:
                            u = STATE_NO[(d, q)]
                            bank = open_bank(pe, SU, u)
                            for h in range(2):
                                ins = nc.tensor.matmul(bank[:, h * P:(h + 1) * P], KD[:, w, h, c, :],
                                                       A_v[:, ch, h * P:(h + 1) * P], start=True, stop=True)
                            sums_done(ins, SU, u)

                for n in range(7):
                    if n < 6:
                        scores(n)
                    if n:
                        outputs(n - 1)
                norm_pe(nrm, f"ro{r}", readout_items(r))

            hgrn(0)
            hgrn(1)

            g = 0
            for c in range(4):
                w = await_chunk(pe, "wmlp", c)
                if c < 2:
                    for m in range(2):
                        g = features(pe, "wmlp", "wmlp", g, w, KT, m * P, 256, h_seg, (0, 1))
                else:
                    g = tokens(pe, "wmlp", g, w, KT, 256, 0, 256, h_tok, range(6))
                release(pe, "wmlp", c, "wmlp", g - 1)
            pe.wait_ge(mlp_v, 1)
            for q in range(4):
                for i, (a, n) in enumerate(SEGS):
                    bank = open_bank(pe, "sv", 2 * q + i)
                    for c in range(n // P):
                        ins = nc.tensor.matmul(bank[:, c * P:(c + 1) * P], VB4[:, a // P + c, q, :], WST[:, q, :],
                                               start=True, stop=True)
                    sums_done(ins, "sv", 2 * q + i)

            def project_out(stage, src, segs):
                g = 0
                for c in range(4):
                    w = await_chunk(pe, stage, c)
                    for m in range(2):
                        g = features(pe, stage, stage, g, w, KT, m * P, 256, src, segs)
                    release(pe, stage, c, stage, g - 1)

            def ffn(l, segs):
                up, down = f"up{l}", f"down{l}"
                ns = len(segs)
                with pe.Fori(0, FT // 2) as i:
                    for c in range(2):
                        w = await_chunk(pe, up, c, i)
                        g = 2 * ns * c
                        for m in range(2):
                            g = features(pe, up, up, g, w, KT, m * P, 256, h_seg, segs, loops=i)
                        release(pe, up, c, up, g - 1, i)
                await_all_taken(pe, up)
                with pe.Fori(0, 2) as i:
                    for c in range(4):
                        w = await_chunk(pe, down, c, 2 * i)
                        features(pe, down, down, ns * c, w, FT, 0, P,
                                 lambda s, k: G[:, k, SEGS[s][0]:SEGS[s][0] + SEGS[s][1]], segs, loops=i)
                        release(pe, down, c, down, ns * c + ns - 1, i)

            pe.wait_ge(y_ready, 1)
            project_out("wout0", lambda s, k: Y[:, k, SEGS[s][0]:SEGS[s][0] + SEGS[s][1]], (0, 1))
            norm_pe(nrm, "n1", modulated(0, 1, (0, 1)))
            pe.wait_ge(h_ready, 4)
            ffn(0, (0, 1))

            norm_pe(nrm, "n2", modulated(1, 0, (0, 1)))
            pe.wait_ge(h_ready, 6)
            g = 0
            for c in range(4):
                w = await_chunk(pe, "winM", c)
                for m in range(2):
                    g = features(pe, "winM", "winM", g, w, KT, m * P, 256, h_seg, (0,) if 2 * c + m < 5 else (0, 1))
                release(pe, "winM", c, "winM", g - 1)
            norm_pe(nrm, "nlat", lat_items())
            pe.wait_ge(norm_done, NORMS_UP_TO["nlat"])
            bank = open_bank(pe, "ropek", 0)
            pe.wait_ge(m_tab, 32)
            sums_done(nc.tensor.matmul(bank[:, :], C("rot"), M_PE[:, 0, 0:S], start=True, stop=True), "ropek", 0)
            g = 0
            for c in range(3):
                w = await_chunk(pe, "qb", c)
                for m in range(3):
                    g = features(pe, "qb", "qb", g, w, 3, m * P, 3 * P, lambda s, k: M_QL[:, k, :], (0,))
                release(pe, "qb", c, "qb", g - 1)
            g = 0
            for c in range(3):
                w = await_chunk(pe, "kvb", c)
                for m in range(2):
                    g = features(pe, "kvb", "kvb", g, w, 2, m * P, 4 * P,
                                 lambda s, k: M_KV[:, k, SEGS[s][0]:SEGS[s][0] + SEGS[s][1]], (0, 1))
                g = tokens(pe, "kvb", g, w, 2, 4 * P, 2 * P, 2 * P, lambda t, k: M_KV[:, k, t * P:(t + 1) * P], range(6))
                release(pe, "kvb", c, "kvb", g - 1)
            norm_pe(nrm, "nqk", qk_items())
            pe.wait_ge(norm_done, NORMS_UP_TO["nqk"])
            for j in range(3):
                bank = open_bank(pe, "ropeq", j)
                sums_done(nc.tensor.matmul(bank[:, :], C("rot"), M_QP[:, j, :], start=True, stop=True), "ropeq", j)
            pe.wait_ge(m_rope, 4)
            pe.wait_ge(m_dft, 32)
            for t in range(4):
                bank = open_bank(pe, "fa", t).rearrange("p (c n) -> p c n", c=2)
                for c in range(2):
                    ins = nc.tensor.matmul(bank[:, c, :], M_C[:, c, t * P:(t + 1) * P], M_CC, start=True, stop=True)
                sums_done(ins, "fa", t)
            await_all_taken(pe, "fa")
            for c in range(2):
                bank = open_bank(pe, "fb", c)
                for t in range(4):
                    for s in range(2):
                        ins = nc.tensor.matmul(bank[:, :], M_AB[:, t, c, s * P:(s + 1) * P], M_DFT[:, 4 * s + t, :],
                                               start=(t == 0 and s == 0), stop=(t == 3 and s == 1))
                sums_done(ins, "fb", c)
            await_all_taken(pe, "fb")
            for b in range(8):
                pe.wait_ge(bank_free[b], BANKS_BEFORE["mS"][b])
            units = [(h, i) for h in range(HEADS_M) for i in range(4)]

            def m_scores(u):
                h, i = units[u]
                b = bank_use("mS", u)[0]
                open_bank(pe, "mS", u)
                o = 64 * (h % 2)
                for j, (a, n) in enumerate(SEGS):
                    nc.tensor.matmul(ps[:, b + j, 0:n], M_QN[:, h, i * P:(i + 1) * P], M_KN[:, h, a:a + n],
                                     start=True, stop=False)
                    ins = nc.tensor.matmul(ps[:, b + j, 0:n], M_QP[o:o + 64, h // 2, i * P:(i + 1) * P],
                                           M_PE[o:o + 64, 0, a:a + n], start=False, stop=True)
                sums_done(ins, "mS", u)

            def m_turn(u):
                await_taken(pe, "mS", u)
                pe.wait_ge(m_diag, u + 1)
                open_bank(pe, "mT", u)
                for t in range(6):
                    ins = nc.tensor.matmul(ps[:, 4 + t // 4, (t % 4) * P:(t % 4 + 1) * P],
                                           M_P[:, u % 2, t * P:(t + 1) * P], M_DG[:, u % 2, :], start=True, stop=True)
                sums_done(ins, "mT", u)

            def m_values(h):
                await_taken(pe, "mT", 4 * h + 3)
                bank = open_bank(pe, "mV", h)
                for t in range(6):
                    ins = nc.tensor.matmul(bank[:, :], M_V[:, t, h, :], M_PT[h % 2][:, t, :],
                                           start=(t == 0), stop=(t == 5))
                sums_done(ins, "mV", h)

            for u in range(24 + 2):
                if u < 24:
                    m_scores(u)
                if 1 <= u <= 24:
                    m_turn(u - 1)
                if u >= 5 and u % 4 == 1:
                    m_values((u - 5) // 4)
            await_all_taken(pe, "mV")
            project_out("woutM", lambda s, k: YM[:, k, :], (0,))
            norm_pe(nrm, "n3", modulated(1, 1, (0,)))
            pe.wait_ge(h_ready, 7)
            ffn(1, (0,))

            norm_pe(nrm, "n4", modulated2(0))
            pe.wait_ge(h_ready, 8)
            g = 0
            for c in range(16):
                w = await_chunk(pe, "winE", c)
                if c in (4, 5, 10, 11):
                    g = tokens(pe, "winE", g, w, KT, 256, 0, 256, h_tok, range(4))
                else:
                    for m in range(2):
                        g = features(pe, "winE", "winE", g, w, KT, m * P, 256, h_seg, (0,))
                release(pe, "winE", c, "winE", g - 1)
            await_all_taken(pe, "winE")

            def attention(kind):
                heads, two = PASSES[kind]
                n = 4 * heads
                probs = PROBS_BEFORE[kind]

                def scores(u):
                    h, i = u // 4, u % 4
                    kts = key_tiles(kind, i)
                    a, b = kts[0] * P, (kts[-1] + 1) * P
                    for x in range(two):
                        bank = open_bank(pe, kind + "S", two * u + x)
                        if kind == "a":
                            o, q, k = 64 * (h % 2), E_QA[:, h // 2, :], E_KA[:, h // 2, :]
                        elif kind == "b":
                            o, q, k = 64 * x, E_QB[:, h, :], E_KB[:, h, :]
                        else:
                            o, q, k = 64 * (h % 2), C_Q[:, h // 2, :], C_K[:, h // 8, :]
                        ins = nc.tensor.matmul(bank[:, 0:b - a], q[o:o + 64, i * P:(i + 1) * P], k[o:o + 64, a:b],
                                               start=True, stop=True)
                        sums_done(ins, kind + "S", two * u + x)

                def turn(u):
                    pe.wait_ge(e_p, probs + two * (u + 1))
                    pe.wait_ge(e_dg, probs + two * (u + 1))
                    bank = open_bank(pe, kind + "T", u)
                    for j in range(len(key_tiles(kind, u % 4))):
                        for x in range(two):
                            v = probs + two * u + x
                            ins = nc.tensor.matmul(bank[:, j * P:(j + 1) * P], E_P[:, v % 4, j * P:(j + 1) * P],
                                                   E_DG[:, v % 4, :], start=(x == 0), stop=(x == two - 1))
                    sums_done(ins, kind + "T", u)

                def values(h):
                    await_taken(pe, kind + "T", 4 * h + 3)
                    if kind == "b":
                        k, first, last = h, True, True
                        out_, v = slice(0, P), E_VB[:, :, h, :]
                    else:
                        k, first, last = h // 2, h % 2 == 0, h % 2 == 1
                        out_ = slice(64 * (h % 2), 64 * (h % 2) + 64)
                        v = E_VA[:, :, h // 2, out_] if kind == "a" else C_V[:, :, h // 8, out_]
                    if kind == "c":
                        jobs = [(i * P, P, list(key_tiles("c", i))) for i in range(4)]
                    else:
                        jobs = [(0, S, list(range(4)))]
                    bank = open_bank(pe, kind + "V", k) if first else bank_ap(kind + "V", k)
                    for a, n_, kts in jobs:
                        for j, t in enumerate(kts):
                            ins = nc.tensor.matmul(bank[out_, a:a + n_], v[:, t, :], E_T[:, h % 2, t, a:a + n_],
                                                   start=(j == 0), stop=(j == len(kts) - 1))
                    ins.then_inc(e_head, 1)
                    if last:
                        pe.wait_ge(e_head, HEADS_BEFORE[kind] + h + 1)
                        pe.sem_inc(bank_full[bank_use(kind + "V", k)[0]], 1)

                for u in range(n + 2):
                    if u < n:
                        scores(u)
                    if 1 <= u <= n:
                        turn(u - 1)
                    if u >= 5 and u % 4 == 1:
                        values((u - 5) // 4)

            attention("a")
            attention("b")
            norm_pe(nrm, "nB", subln_items())
            pe.wait_ge(y_ready, 2)
            project_out("woutE", lambda s, k: HL[:, k, :], (0,))
            norm_pe(nrm, "n5", modulated2(1))
            pe.wait_ge(h_ready, 9)
            g = 0
            for c in range(10):
                w = await_chunk(pe, "winC", c)
                if c == 5:
                    g = tokens(pe, "winC", g, w, KT, 256, 0, 256, h_tok, range(4))
                else:
                    for m in range(2):
                        g = features(pe, "winC", "winC", g, w, KT, m * P, 256, h_seg, (0,))
                release(pe, "winC", c, "winC", g - 1)
            await_all_taken(pe, "winC")
            attention("c")
            await_all_taken(pe, "cV")
            project_out("woutC", lambda s, k: HL[:, k, :], (0,))
            norm_pe(nrm, "n6", final_items())

        @block.scalar
        def _(act):
            nrm = Norms(act)
            A = nc.scalar.activation

            act.wait_ge(const_in, 64)
            A(cs[:, :, 0], V("c"), ACT.Silu).then_inc(cs_ready, 1)
            A(cs[:, :, 1], V("cc"), ACT.Silu).then_inc(cs_ready, 1)
            A(cs2[:, :], V("c2"), ACT.Silu).then_inc(cs_ready, 1)
            act.wait_ge(lb_step, 3)
            A(small[:, 72:80], small[:, 72:80], ACT.Exp)
            A(small[:, 3:5], small[:, 1:3], ACT.Exp).then_inc(lam_sem, 1)

            norm_act(nrm, "n0", modulated(0, 0, (0, 1)))

            def hgrn(r):
                win, SS, SK, SO, SU = (f"{x}{r}" for x in ("win", "hgS", "hgK", "hgO", "hgU"))
                if r:
                    act.wait_ge(hg_diff, 6)
                for d in range(2):
                    for j in range(2):
                        for i, (a, n) in enumerate(SEGS):
                            g = 4 * d + 2 * j + i
                            bank = await_sums(act, win, g)
                            taken(A(A_b[d][:, j, a:a + n], bank[:, 0:n], ACT.Exp, scale=-1.0), win, g)
                for d in range(2):
                    act.wait_ge(hg_f, 2 * r + d + 1)
                    A(A_b[d][:, :, :], A_b[d][:, :, :], ACT.Ln).then_inc(hg_ln, 1)
                if r:
                    act.wait_ge(hg_ops, 6)
                for j in range(2):
                    for i, (a, n) in enumerate(SEGS):
                        g = 8 + 2 * j + i
                        bank = await_sums(act, win, g)
                        taken(A(A_q[:, j, a:a + n], bank[:, 0:n], ACT.Silu), win, g)

                def turned_keys(n):
                    if n >= 2:
                        await_sums(act, SO, 2 * (n - 2) + 1)
                        d, _, i = STEPS[n - 2]
                        await_sums(act, SU, STATE_NO[(d, min(2 * i + 1, 4))])
                    bank = await_sums(act, SK, n)
                    taken(A(KD[:, n % 2, :, :, :].rearrange("p h c n -> p (h c n)"), bank[:, :], ACT.Copy), SK, n)

                for n, (d, chunks, i) in enumerate(STEPS):
                    w = n % 2
                    act.wait_ge(hg_diff, 6 * r + n + 1)
                    b = tok(A_b[d], chunks)
                    A(WK[:, w, 0:8, :, :, :].rearrange("p a h c n -> p (a h c n)"),
                      WK[:, w, 0:8, :, :, :].rearrange("p a h c n -> p (a h c n)"), ACT.Exp)
                    e = b.rearrange("p h (c n) -> p h c n", c=2)[:, :, :, P - 1 if d == 0 else 0]
                    if n >= 2:
                        d2, _, i2 = STEPS[n - 2]
                        act.wait_ge(hg_st, 10 * r + STATE_NO[(d2, min(2 * i2 + 1, 4))] + 1)
                    elif r:
                        act.wait_ge(hg_st, 10)
                    A(EL[:, w, :, :], e, ACT.Exp)
                    A(wk(w, 8), b, ACT.Exp).then_inc(hg_exp, 1)
                    if n:
                        turned_keys(n - 1)
                turned_keys(5)
                A(A_g[:, :, :], A_g[:, :, :], ACT.Silu).then_inc(hg_g, 1)
                await_taken(act, SO, 10)
                await_taken(act, SO, 11)
                norm_act(nrm, f"ro{r}", readout_items(r))

            hgrn(0)
            hgrn(1)

            act.wait_ge(hg_round, 2)
            g = 0
            for q in range(4):
                for a, n in SEGS:
                    bank = await_sums(act, "wmlp", g)
                    taken(A(U[:, q, a:a + n], bank[:, 0:n], ACT.Gelu_apprx_tanh), "wmlp", g)
                    g += 1
            for c in range(2):
                for t in range(6):
                    bank = await_sums(act, "wmlp", g)
                    taken(A(VB4[:, t, 2 * c:2 * c + 2, :], bank[:, 0:256].rearrange("p (q n) -> p q n", q=2),
                            ACT.Gelu_apprx_tanh), "wmlp", g)
                    g += 1
            act.wait_ge(mlp_u, 1)
            A(rsq, ssq, ACT.Sqrt, bias=small[:, 0:1], scale=1.0 / P).then_inc(mlp_u, 1)

            def ffn(l, segs):
                up = f"up{l}"
                ns = len(segs)
                width = sum(SEGS[s][1] for s in segs)
                with act.Fori(0, FT // 2) as i:
                    for c in range(2):
                        g = 2 * ns * c
                        for x in range(ns):
                            await_taken(act, up, g + x, i)
                        A(FA[:, c, 0:width], FA[:, c, 0:width], ACT.Silu).then_inc(ffn_silu[c], 1)

            await_all_taken(act, "wout0")
            norm_act(nrm, "n1", modulated(0, 1, (0, 1)))
            ffn(0, (0, 1))
            await_all_taken(act, "down0")
            norm_act(nrm, "n2", modulated(1, 0, (0, 1)))

            dst = [M_C[:, 0, :], M_C[:, 1, :]] + [M_QL[:, k, :] for k in range(3)]
            dst += [seg_of(M_KV, k, s) for k in range(2) for s in range(2)] + [seg_of(M_PE, 0, s) for s in range(2)]
            for g, to in enumerate(dst):
                bank = await_sums(act, "winM", g)
                taken(A(to, bank[:, 0:to.shape[-1]], ACT.Copy), "winM", g)
            await_all_taken(act, "winM")
            norm_act(nrm, "nlat", lat_items())
            for g in range(9):
                c, m = g // 3, g % 3
                bank = await_sums(act, "qb", g)
                taken(A(M_QN[:, 2 * c + m, :] if m < 2 else M_QP[:, c, :], bank[:, :], ACT.Copy), "qb", g)
            for c in range(3):
                for m in range(2):
                    for s in range(2):
                        g = 10 * c + 2 * m + s
                        bank = await_sums(act, "kvb", g)
                        taken(A(seg_of(M_KN, 2 * c + m, s), bank[:, 0:SEGS[s][1]], ACT.Copy), "kvb", g)
            await_all_taken(act, "qb")
            await_all_taken(act, "kvb")
            norm_act(nrm, "nqk", qk_items())
            for t in range(4):
                bank = await_sums(act, "fa", t)
                taken(A(M_AB[:, t, :, :].rearrange("p c n -> p (c n)"), bank[:, :], ACT.Copy), "fa", t)
            for u in range(25):
                if u < 24:
                    act.wait_ge(m_max, u + 1)
                    b = bank_use("mS", u)[0]
                    taken(A(M_P[:, u % 2, :], ps[:, b:b + 2, :].rearrange("p b n -> p (b n)")[:, 0:T], ACT.Exp,
                            bias=small[:, 8 + u % 2:9 + u % 2], scale=float(192 ** -0.5),
                            accum_out=small[:, 12 + u % 2:13 + u % 2]), "mS", u)
                if u:
                    h, i = (u - 1) // 4, (u - 1) % 4
                    if h >= 2 and i == 0:
                        await_sums(act, "mV", h - 2)
                    await_sums(act, "mT", u - 1)
                    taken(A(M_PT[h % 2][:, :, i * P:(i + 1) * P],
                            ps[:, 4:6, :].rearrange("p b n -> p (b n)")[:, 0:T].rearrange("p (t n) -> p t n", t=6),
                            ACT.Copy), "mT", u - 1)
            await_all_taken(act, "woutM")
            norm_act(nrm, "n3", modulated(1, 1, (0,)))
            ffn(1, (0,))
            await_all_taken(act, "down1")

            norm_act(nrm, "n4", modulated2(0))
            dst = [(E_QA[:, k, :], 0.125) for k in range(4)] + [(E_KA[:, k, :], 1.0) for k in range(4)] + [None] * 8
            dst += [(E_QB[:, k, :], 0.125) for k in range(4)] + [(E_KB[:, k, :], 1.0) for k in range(4)] + [None] * 8
            for g, to in enumerate(dst):
                if to:
                    bank = await_sums(act, "winE", g)
                    taken(A(to[0], bank[:, :], ACT.Copy, scale=to[1]), "winE", g)
            for k in range(8):
                bank = await_sums(act, "winE", 32 + k)
                taken(A(E_G[:, k, :], bank[:, :], ACT.Silu), "winE", 32 + k)

            def attention(kind):
                heads, two = PASSES[kind]
                probs = PROBS_BEFORE[kind]
                for u in range(4 * heads + 1):
                    if u < 4 * heads:
                        n = P * len(key_tiles(kind, u % 4))
                        for x in range(two):
                            v = probs + two * u + x
                            await_taken(act, kind + "S", two * u + x)
                            if kind == "c":
                                A(small[:, 20 + v % 4:21 + v % 4], V("sink", u // 4), ACT.Exp,
                                  bias=small[:, 8 + v % 4:9 + v % 4])
                            A(E_P[:, v % 4, 0:n], E_S[:, v % 2, 0:n], ACT.Exp, scale=-1.0,
                              bias=small[:, 8 + v % 4:9 + v % 4],
                              accum_out=small[:, 12 + v % 4:13 + v % 4]).then_inc(e_p, 1)
                    if u:
                        h, i = (u - 1) // 4, (u - 1) % 4
                        n = HEADS_BEFORE[kind] + h
                        if n >= 2 and i == 0:
                            act.wait_ge(e_head, n - 1)
                        kts = key_tiles(kind, i)
                        bank = await_sums(act, kind + "T", u - 1)
                        taken(A(E_T[:, h % 2, kts[0]:kts[-1] + 1, i * P:(i + 1) * P],
                                bank[:, 0:P * len(kts)].rearrange("p (t n) -> p t n", n=P), ACT.Copy),
                              kind + "T", u - 1)

            attention("a")
            attention("b")
            await_all_taken(act, "bV")
            norm_act(nrm, "nB", subln_items())
            await_all_taken(act, "woutE")
            norm_act(nrm, "n5", modulated2(1))
            for g in range(10):
                bank = await_sums(act, "winC", g)
                to, scale = (C_Q[:, g, :], 0.125) if g < 8 else (C_K[:, g - 8, :], 1.0)
                taken(A(to, bank[:, :], ACT.Copy, scale=scale), "winC", g)
            for k in range(8):
                bank = await_sums(act, "winC", 14 + k)
                taken(A(C_G[:, k, :], bank[:, :], ACT.Silu), "winC", 14 + k)
            attention("c")
            await_all_taken(act, "woutC")
            norm_act(nrm, "n6", final_items())

        @block.gpsimd
        def _(pool):
            TT = nc.gpsimd.tensor_tensor

            def differences(r, n):
                d, chunks, _ = STEPS[n]
                w, SO = n % 2, f"hgO{r}"
                if n >= 2:
                    await_sums(pool, SO, 2 * (n - 2) + 1)
                elif r:
                    await_sums(pool, "hgO0", 2 * (n + 4) + 1)
                pool.wait_ge(hg_b, 2 * r + d + 1)
                b = tok(A_b[d], chunks)
                for l, m in enumerate(LEVELS):
                    x = wk(w, l)
                    g = CTX // (2 * m)
                    at = b.rearrange("p h (g x) -> p h g x", x=2 * m)[:, :, :, m - 1 + d:m + d]
                    at = at.to_broadcast([P, 2, g, m])
                    early, late = half(b, m, False), half(b, m, True)
                    if d == 0:
                        TT(half(x, m, False), at, early, ALU.subtract)
                        TT(half(x, m, True), late, at, ALU.subtract)
                    else:
                        TT(half(x, m, False), early, at, ALU.subtract)
                        TT(half(x, m, True), at, late, ALU.subtract)
                def blocks(y, m):
                    return y.rearrange("p h (g x) -> p h g x", x=m)
                lb_ = blocks(b, LEAF)
                at = lb_[:, :, :, 1 + d:2 + d].to_broadcast([P, 2, CTX // LEAF, LEAF])
                TT(blocks(wk(w, 5), LEAF), lb_, at, ALU.subtract)
                TT(blocks(wk(w, 6), LEAF), at, lb_, ALU.subtract)
                cb = blocks(b, P)
                e = P - 1 if d == 0 else 0
                TT(blocks(wk(w, 7), P), cb[:, :, :, e:e + 1].to_broadcast([P, 2, 2, P]), cb,
                   ALU.subtract).then_inc(hg_diff, 1)

            for r in range(2):
                for n in range(6):
                    differences(r, n)
            pool.wait_ge(hg_round, 2)
            for name, to in (("vnw", VNW), ("bsb", BSB), ("wst", WST)):
                pool.dma_start(to, dram[name]).then_inc(mlp_tab, 16)
            await_all_taken(pool, "wout0")
            for name, to in (("cos", M_COS), ("sin", M_SIN)):
                pool.dma_start(to, dram[name]).then_inc(m_tab, 16)
            for name, to in (("cc", M_CC), ("dft", M_DFT)):
                pool.dma_start(to, dram[name]).then_inc(m_dft, 16)
            await_all_taken(pool, "woutM")
            hh = 0
            for kind in "abc":
                for h in range(PASSES[kind][0]):
                    if hh >= 2:
                        pk = "a" if hh - 2 < 8 else "b" if hh - 2 < 12 else "c"
                        u = (4 * (hh - 2 - HEADS_BEFORE[pk]) + 4) * PASSES[pk][1] - 1
                        await_taken(pool, pk + "S", u)
                    to = E_BIAS[:, hh % 2, :] if kind != "c" else C_BIAS[:, hh % 2, :]
                    pool.dma_start(to, dram["bias_" + kind][h]).then_inc(e_bias[hh % 2], 16)
                    hh += 1

        @block.vector
        def _(dve):
            step = Step(dve, dve_step)
            nrm = Norms(dve, step)
            TT, TS, STT = nc.vector.tensor_tensor, nc.vector.tensor_scalar, nc.vector.scalar_tensor_tensor

            dve.wait_ge(const_in, 64)
            step.mark(nc.vector.memset(small[:, 0:1], EPS))
            TT(small[:, 72:80], V("lb"), V("lb"), ALU.subtract).then_inc(lb_step, 1)
            lam = V("lam").rearrange("p (a n) -> p a n", a=4)
            for x in range(2):
                nc.vector.tensor_tensor_reduce(SQ[:, x, 0:64], lam[:, 2 * x, :], lam[:, 2 * x + 1, :], 1.0, 0.0,
                                               ALU.mult, ALU.add, small[:, 1 + x:2 + x]).then_inc(lb_step, 1)
            step.mark(TS(small[:, 6:7], V("subln", 0), 1.0 - LAM_INIT, None, ALU.mult))
            dve.wait_ge(lam_sem, 1)
            step.link(nc.vector.reciprocal(small[:, 80:88], small[:, 72:80]))
            step.link(TT(small[:, 72:80], small[:, 72:80], small[:, 80:88], ALU.mult))
            step.link(TT(small[:, 56:64], small[:, 72:80], small[:, 72:80], ALU.subtract))
            step.mark(TS(small[:, 64:72], small[:, 56:64], -1.0, 1.0, ALU.mult, ALU.add))
            step.link(TT(small[:, 5:6], small[:, 4:5], small[:, 3:4], ALU.subtract))
            step.link(TS(small[:, 5:6], small[:, 5:6], -LAM_INIT, None, ALU.add))

            for l in range(2):
                bank = await_sums(dve, f"ada{l}", 0)
                taken(TT(mod[:, l, :, :], bank[:, 0:96].rearrange("p (k s) -> p k s", s=2),
                         V(f"ab{l}").unsqueeze(2).to_broadcast([P, 48, 2]), ALU.add), f"ada{l}", 0)
                await_taken(dve, f"ada{l}", 0)
                for which, name in enumerate((f"nm{l}", f"nf{l}")):
                    o = 24 * which + 8
                    step.mark(STT(gain[:, 2 * l + which, :, :], mod[:, l, o:o + 8, :], 1.0,
                                  V(name).unsqueeze(2).to_broadcast([P, KT, 2]), ALU.add, ALU.mult))
            for l in range(2):
                bank = await_sums(dve, f"ada{2 + l}", 0)
                taken(TT(mod2[:, l, :], bank[:, 0:24], V(f"ab{2 + l}"), ALU.add), f"ada{2 + l}", 0)
                await_taken(dve, f"ada{2 + l}", 0)
                step.mark(STT(gain2[:, l, :], mod2[:, l, 8:16], 1.0, V(f"ng{l}"), ALU.add, ALU.mult))
            step.settle()

            norm_dve(nrm, "n0", modulated(0, 0, (0, 1)), h_ready)

            touched = set()

            def hgrn(r):
                win, SS, SK, SO, SU = (f"{x}{r}" for x in ("win", "hgS", "hgK", "hgO", "hgU"))
                for d in range(2):
                    for g in range(4 * d, 4 * d + 4):
                        await_taken(dve, win, g)
                    b, k = A_b[d], A_k[d]
                    step.link(TS(b[:, :, :], b[:, :, :], 1.0, None, ALU.add))
                    step.link(nc.vector.reciprocal(b[:, :, :], b[:, :, :]))
                    for j in range(2):
                        o = 4 * d + 2 * r + j
                        step.mark(TS(b[:, j, :], b[:, j, :], small[:, 64 + o:65 + o], small[:, 56 + o:57 + o],
                                     ALU.mult, ALU.add))
                    step.settle()
                    step.link(TS(b[:, :, :], b[:, :, :], F_MIN, None, ALU.max))
                    TS(k[:, :, :], b[:, :, :], -1.0, 1.0, ALU.mult, ALU.add).then_inc(hg_f, 1)
                for d in range(2):
                    dve.wait_ge(hg_ln, 2 * r + d + 1)
                    for j in range(2):
                        x = A_b[d][:, j, :]
                        keep = C("scan")[:, 0:T] if d == 0 else C("scan")[:, 1:T + 1]
                        if d:
                            x, keep = x[:, ::-1], keep[:, ::-1]
                        ins = nc.vector.tensor_tensor_scan(x, keep, x, 0.0, ALU.mult, ALU.add)
                    ins.then_inc(hg_b, 1)
                for t in range(6):
                    bank = await_sums(dve, win, 12 + t)
                    taken(nc.vector.tensor_copy(A_v[:, t, :], bank[:, 0:256]), win, 12 + t)
                for g in range(8, 12):
                    await_taken(dve, win, g)

                def operands(n):
                    d, chunks, _ = STEPS[n]
                    w = n % 2
                    dve.wait_ge(hg_exp, 6 * r + n + 1)
                    q, k = tok(A_q, chunks), tok(A_k[d], chunks)
                    for l, m in enumerate(LEVELS):
                        x = wk(w, l)
                        for second in (False, True):
                            f = q if second == (d == 0) else k
                            TT(half(x, m, second), half(x, m, second), half(f, m, second), ALU.mult)
                    for a, f in ((5, q), (6, k), (7, k), (8, q)):
                        ins = TT(wk(w, a), wk(w, a), f, ALU.mult)
                    ins.then_inc(hg_ops, 1)

                def mask_scores(n):
                    d, w = STEPS[n][0], n % 2
                    acc = ACC[:, w, :, :, :].rearrange("p h c n -> p (h c) n")
                    for l in range(6):
                        bank = await_sums(dve, SS, 6 * n + l).rearrange("p (g n) -> p g n", n=P)
                        m = masks[:, 6 * d + l:6 * d + l + 1, :].to_broadcast([P, 4, P])
                        if l == 0:
                            ins = TT(acc, bank, m, ALU.mult)
                        else:
                            ins = nc.vector.copy_predicated(acc, m.bitcast(U32), bank)
                        taken(ins, SS, 6 * n + l)
                        await_taken(dve, SS, 6 * n + l)
                    dve.sem_inc(hg_acc, 1)

                def results(n):
                    d, chunks, i = STEPS[n]
                    w, lo = n % 2, min(chunks)
                    for j, ch in enumerate(chunks):
                        q = 2 * i + j
                        bank = await_sums(dve, SO, 2 * n + j)[:, 0:2 * P].rearrange("p (h n) -> p h n", h=2)
                        y = Y[:, 2 * r:2 * r + 2, ch * P:(ch + 1) * P]
                        if (r, ch) in touched:
                            ins = TT(y, bank, y, ALU.add)
                        else:
                            ins = nc.vector.tensor_copy(y, bank)
                            touched.add((r, ch))
                        taken(ins, SO, 2 * n + j)
                        if q < 5:
                            u = STATE_NO[(d, q)]
                            bank = await_sums(dve, SU, u)
                            c = ch - lo
                            for h in range(2):
                                new = ST[:, d, q % 2, h, :]
                                if q == 0:
                                    step.mark(nc.vector.tensor_copy(new, bank[:, h * P:(h + 1) * P]))
                                else:
                                    step.mark(STT(new, ST[:, d, (q - 1) % 2, h, :], EL[:, w, h, c:c + 1],
                                                  bank[:, h * P:(h + 1) * P], ALU.mult, ALU.add))
                            step.settle()
                            dve.sem_inc(bank_free[bank_use(SU, u)[0]], 1)
                            dve.sem_inc(hg_st, 1)

                for n in range(7):
                    if n < 6:
                        operands(n)
                    if n == 0:
                        for j in range(2):
                            for i, (a, m) in enumerate(SEGS):
                                g = 18 + 2 * j + i
                                bank = await_sums(dve, win, g)
                                taken(nc.vector.tensor_copy(A_g[:, j, a:a + m], bank[:, 0:m]), win, g)
                    if n < 6:
                        mask_scores(n)
                    if n:
                        results(n - 1)
                norm_dve(nrm, f"ro{r}", readout_items(r))
                dve.wait_ge(norm_done, NORMS_UP_TO[f"ro{r}"])
                dve.wait_ge(hg_g, r + 1)
                TT(Y[:, 2 * r:2 * r + 2, :], Y[:, 2 * r:2 * r + 2, :], A_g[:, :, :], ALU.mult).then_inc(hg_round, 1)

            hgrn(0)
            hgrn(1)

            await_all_taken(dve, "wmlp")
            step.link(TT(VSQ, VB, VB, ALU.mult))
            nc.vector.tensor_reduce(ssq, VSQ, AX.X, ALU.add).then_inc(mlp_u, 1)
            dve.wait_ge(mlp_u, 2)
            step.link(nc.vector.reciprocal(rsq, rsq))
            dve.wait_ge(mlp_tab, 48)
            for t in range(6):
                for q in range(4):
                    o = 4 * t + q
                    ins = STT(VB4[:, t, q, :], VB4[:, t, q, :], rsq[:, o:o + 1], VNW[:, q, :], ALU.mult, ALU.mult)
            ins.then_inc(mlp_v, 1)
            for q in range(4):
                for i, (a, n) in enumerate(SEGS):
                    g = 2 * q + i
                    bank = await_sums(dve, "sv", g)
                    b = BSB[:, q:q + 1, :].to_broadcast([P, n // P, P])
                    taken(TT(MT[:, i, 0:n].rearrange("p (c n) -> p c n", n=P),
                             bank[:, 0:n].rearrange("p (c n) -> p c n", n=P), b, ALU.add), "sv", g)
                    await_taken(dve, "sv", g)
                    ins = TT(Y[:, 4 + q, a:a + n], MT[:, i, 0:n], U[:, q, a:a + n], ALU.mult)
            ins.then_inc(y_ready, 1)

            def add_out(stage, segs, scalar):
                g = 0
                for k in range(KT):
                    for s in segs:
                        bank = await_sums(dve, stage, g)
                        n = SEGS[s][1]
                        taken(STT(X[s][:, k, :], bank[:, 0:n], scalar(k, s), X[s][:, k, :], ALU.mult, ALU.add),
                              stage, g)
                        g += 1

            def ffn(l, segs):
                up, down = f"up{l}", f"down{l}"
                ns = len(segs)
                cw = V(f"cw{l}")
                taps = l * (FT // 2) * 4
                rounds = l * (FT // 2)
                with dve.Fori(0, FT // 2) as i:
                    for c in range(2):
                        g = 2 * ns * c
                        for x, s in enumerate(segs):
                            a, n = SEGS[s]
                            bank = await_sums(dve, up, g + x, i)
                            TS(FA[:, c, a:a + n], bank[:, 0:n], cw[:, bass.ds(i * 2 + (FT + c), 1)],
                               V(f"cb{l}")[:, bass.ds(i * 2 + c, 1)], ALU.mult, ALU.add).then_inc(ffn_tap[c], 1)
                            dve.wait_ge(ffn_tap[c], i * (2 * ns) + (taps + 2 * x + 1))
                            STT(FA[:, c, a + 1:a + n], bank[:, 0:n - 1], cw[:, bass.ds(i * 2 + c, 1)],
                                FA[:, c, a + 1:a + n], ALU.mult, ALU.add).then_inc(ffn_tap[c], 1)
                            dve.wait_ge(ffn_tap[c], i * (2 * ns) + (taps + 2 * x + 2))
                            taken(STT(FA[:, c, a:a + n - 1], bank[:, 1:n], cw[:, bass.ds(i * 2 + (2 * FT + c), 1)],
                                      FA[:, c, a:a + n - 1], ALU.mult, ALU.add), up, g + x)
                        dve.wait_ge(ffn_silu[c], i + (rounds + 1))
                        for x, s in enumerate(segs):
                            a, n = SEGS[s]
                            bank = await_sums(dve, up, g + ns + x, i)
                            taken(TT(G.rearrange("p k n -> p (k n)")[:, bass.ds(i * (2 * T) + (c * T + a), n)],
                                     bank[:, 0:n], FA[:, c, a:a + n], ALU.mult), up, g + ns + x)
                with dve.Fori(0, 2) as i:
                    for c in range(4):
                        for x, s in enumerate(segs):
                            n = SEGS[s][1]
                            bank = await_sums(dve, down, ns * c + x, i)
                            xs = X[s][:, :, :].rearrange("p k n -> p (k n)")[:, bass.ds(i * (4 * n) + c * n, n)]
                            gate = mod[:, l, :, :].rearrange("p k s -> p (k s)")[:, bass.ds(i * 8 + (80 + 2 * c + s), 1)]
                            taken(STT(xs, bank[:, 0:n], gate, xs, ALU.mult, ALU.add), down, ns * c + x)

            add_out("wout0", (0, 1), lambda k, s: mod[:, 0, 16 + k, s:s + 1])
            norm_dve(nrm, "n1", modulated(0, 1, (0, 1)), h_ready)
            ffn(0, (0, 1))
            norm_dve(nrm, "n2", modulated(1, 0, (0, 1)), h_ready)

            norm_dve(nrm, "nlat", lat_items())

            def rotate(stage, g, x, before):
                bank = await_sums(dve, stage, g)
                dve.wait_ge(m_tab, 32)
                if before:
                    dve.wait_ge(m_rope, before)
                taken(TT(M_TMP, bank[:, :], M_SIN, ALU.mult), stage, g)
                step.link(TT(x, x, M_COS, ALU.mult))
                await_taken(dve, stage, g)
                TT(x, x, M_TMP, ALU.add).then_inc(m_rope, 1)

            dve.wait_ge(norm_done, NORMS_UP_TO["nlat"])
            rotate("ropek", 0, M_PE[:, 0, 0:S], 0)
            for c in range(3):
                for t in range(6):
                    g = 10 * c + 4 + t
                    bank = await_sums(dve, "kvb", g)
                    taken(nc.vector.tensor_copy(M_V[:, t, 2 * c:2 * c + 2, :],
                                                bank[:, 0:2 * P].rearrange("p (h n) -> p h n", h=2)), "kvb", g)
            norm_dve(nrm, "nqk", qk_items())
            dve.wait_ge(norm_done, NORMS_UP_TO["nqk"])
            for j in range(3):
                rotate("ropeq", j, M_QP[:, j, :], j + 1)
            for c in range(2):
                bank = await_sums(dve, "fb", c)
                taken(nc.vector.tensor_copy(YM[:, c, :], bank[:, :]), "fb", c)

            def m_out(h):
                bank = await_sums(dve, "mV", h)
                taken(nc.vector.tensor_copy(YM[:, 2 + h, :], bank[:, :]), "mV", h)

            for u in range(25):
                if u < 24:
                    await_sums(dve, "mS", u)
                    b = bank_use("mS", u)[0]
                    step.link(nc.vector.tensor_reduce(small[:, 10 + u % 2:11 + u % 2],
                                                      ps[:, b:b + 2, :].rearrange("p b n -> p (b n)")[:, 0:T],
                                                      AX.X, ALU.max))
                    TS(small[:, 8 + u % 2:9 + u % 2], small[:, 10 + u % 2:11 + u % 2], -float(192 ** -0.5), None,
                       ALU.mult).then_inc(m_max, 1)
                if u:
                    v = (u - 1) % 2
                    await_taken(dve, "mS", u - 1)
                    step.link(nc.vector.reciprocal(small[:, 14 + v:15 + v], small[:, 12 + v:13 + v]))
                    TS(M_DG[:, v, :], ident, small[:, 14 + v:15 + v], None, ALU.mult).then_inc(m_diag, 1)
                if u >= 6 and u % 4 == 2:
                    m_out((u - 6) // 4)
            m_out(5)
            add_out("woutM", (0,), lambda k, s: mod[:, 1, 16 + k, s:s + 1])
            norm_dve(nrm, "n3", modulated(1, 1, (0,)), h_ready)
            ffn(1, (0,))

            norm_dve(nrm, "n4", modulated2(0), h_ready)
            for v, c0, g0 in ((E_VA, 4, 8), (E_VB, 10, 24)):
                for c in range(2):
                    for t in range(4):
                        g = g0 + 4 * c + t
                        bank = await_sums(dve, "winE", g)
                        taken(nc.vector.tensor_copy(v[:, t, 2 * c:2 * c + 2, :],
                                                    bank[:, 0:2 * P].rearrange("p (h n) -> p h n", h=2)), "winE", g)

            def attention(kind, gates):
                heads, two = PASSES[kind]
                probs, hb = PROBS_BEFORE[kind], HEADS_BEFORE[kind]

                def negate_and_bound(u, x):
                    v, h, i = probs + two * u + x, u // 4, u % 4
                    kts = key_tiles(kind, i)
                    n = P * len(kts)
                    at = 384 - P * i if kind != "c" else P * (kts[0] - i + 1)
                    hh = hb + h
                    dve.wait_ge(e_bias[hh % 2], 16 * (hh // 2 + 1))
                    if v >= 2:
                        dve.wait_ge(e_p, v - 1)
                    bank = await_sums(dve, kind + "S", two * u + x)
                    init = 3.0e38 if kind != "c" else SINKS[:, h:h + 1]
                    taken(nc.vector.tensor_tensor_reduce(
                        E_S[:, v % 2, 0:n], bank[:, 0:n], E_BIAS[:, hh % 2, at:at + n], -1.0, init,
                        ALU.add, ALU.min, small[:, 8 + v % 4:9 + v % 4]), kind + "S", two * u + x)

                def inverse(u, x):
                    v = probs + two * u + x
                    dve.wait_ge(e_p, v + 1)
                    s, r = small[:, 12 + v % 4:13 + v % 4], small[:, 16 + v % 4:17 + v % 4]
                    if kind == "c":
                        step.link(TT(s, s, small[:, 20 + v % 4:21 + v % 4], ALU.add))
                    step.link(nc.vector.reciprocal(r, s))
                    if x == 0:
                        ins = TS(E_DG[:, v % 4, :], ident, r, None, ALU.mult)
                    else:
                        ins = TS(E_DG[:, v % 4, :], ident, r, small[:, 5:6], ALU.mult, ALU.mult)
                    ins.then_inc(e_dg, 1)

                def gated(k):
                    bank = await_sums(dve, kind + "V", k)
                    y = HL[:, (4 if kind == "b" else 0) + k, :]
                    if kind == "b":
                        ins = nc.vector.tensor_copy(y, bank[:, :])
                    else:
                        ins = TT(y, bank[:, :], gates[:, k, :], ALU.mult)
                    taken(ins, kind + "V", k)

                pairs = heads // (1 if kind == "b" else 2)
                wait = 4 if kind == "b" else 8
                for u in range(4 * heads + 1):
                    for x in range(two):
                        if u < 4 * heads:
                            negate_and_bound(u, x)
                    for x in range(two):
                        if u:
                            inverse(u - 1, x)
                    if u >= wait + 2 and (u - 2) % wait == 0:
                        gated((u - 2) // wait - 1)
                gated(pairs - 1)

            await_all_taken(dve, "winE")
            attention("a", E_G)
            attention("b", E_G)
            norm_dve(nrm, "nB", subln_items())
            dve.wait_ge(norm_done, NORMS_UP_TO["nB"])
            TT(HL[:, 4:8, :], HL[:, 4:8, :], E_G[:, 4:8, :], ALU.mult).then_inc(y_ready, 1)
            add_out("woutE", (0,), lambda k, s: mod2[:, 0, 16 + k:17 + k])
            norm_dve(nrm, "n5", modulated2(1), h_ready)
            for t in range(4):
                bank = await_sums(dve, "winC", 10 + t)
                taken(nc.vector.tensor_copy(C_V[:, t, :, :], bank[:, 0:2 * P].rearrange("p (h n) -> p h n", h=2)),
                      "winC", 10 + t)
            step.link(TS(SINKS, V("sink"), -1.0, None, ALU.mult))
            await_all_taken(dve, "winC")
            attention("c", C_G)
            add_out("woutC", (0,), lambda k, s: mod2[:, 1, 16 + k:17 + k])
            norm_dve(nrm, "n6", final_items())


def shape_tables():
    f = np.float32
    i = np.arange(P)
    const = np.zeros((P, CONST_N), f)

    def put(name, x):
        a, b = CONST_AT[name]
        const[:, a:b] = x
    put("ident", np.eye(P, dtype=f))
    put("ones", 1.0)
    put("ones64", (i[:, None] // 64 == i[None, :] // 64).astype(f))
    rot = np.zeros((P, P), f)
    for j in range(P):
        if j % 32 < 16:
            rot[j + 16, j] = -1.0
        else:
            rot[j - 16, j] = 1.0
    put("rot", rot)
    m = np.zeros((2, 6, P, P), f)
    s, t = i[:, None], i[None, :]
    for l, h in enumerate(LEVELS):
        m[0, l] = (s // (2 * h) == t // (2 * h)) & (s % (2 * h) < h) & (t % (2 * h) >= h)
    m[0, 5] = (s // LEAF == t // LEAF) & (s <= t)
    m[1] = m[0].transpose(0, 2, 1)
    put("masks", m.reshape(12, P, P).transpose(1, 0, 2).reshape(P, -1))
    put("scan", (np.arange(T + 1) % P != 0).astype(f)[None, :])

    row, col = np.arange(S) // 64, np.arange(S) % 64
    inv = (f(10000.0) ** (-np.arange(0, 32, 2, dtype=f) / f(32))).astype(f)
    ang = np.stack([row, col], 0).astype(f)[:, :, None] * inv
    ang = ang.transpose(0, 2, 1)
    ang = np.tile(np.repeat(ang[:, None], 2, 1).reshape(64, S), (2, 1))
    n = np.arange(64)
    a64 = 2 * np.pi * ((n[:, None] * n[None, :]) % 64) / 64
    n = np.arange(S)
    a512 = 2 * np.pi * ((n[:, None] * n[None, :]) % S) / S
    eye2 = np.eye(2)
    cc = np.concatenate([np.kron(eye2, np.cos(a64)), -np.kron(eye2, np.sin(a64))], 1) / np.sqrt(S * 64.0)
    dft = np.concatenate([np.cos(a512).reshape(4, P, S), np.sin(a512).reshape(4, P, S)], 0).transpose(1, 0, 2)

    def slopes(n):
        return (f(2.0) ** (f(-8.0) * np.arange(1, n + 1, dtype=f) / f(n))).astype(f)
    delta = np.abs(np.arange(896)[None, :] - 384 - i[:, None])
    times = (delta <= 64).astype(int) + ((delta % 4 == 0) & (delta <= 256)) + (delta % 16 == 0)
    log_times = np.where(times > 0, np.log(np.maximum(times, 1)), -1e30)
    bias_a = np.stack([-sl * delta.astype(f) + log_times for sl in slopes(8)])
    bias_b = np.stack([-sl * delta.astype(f) for sl in slopes(4)])
    delta = np.abs(np.arange(384)[None, :] - P - i[:, None])
    sl = slopes(16)
    bias_c = np.stack([np.where(delta <= WINDOW, -sl[h] * delta.astype(f), -1e30) for h in BANDED_ORDER])
    return {k: np.ascontiguousarray(v, dtype=f) for k, v in dict(
        const=const, cos=np.cos(ang), sin=np.sin(ang), cc=cc, dft=dft, bias_a=bias_a, bias_b=bias_b,
        bias_c=bias_c).items()}


def chunks_of(w, columns):
    k = w.shape[0] // P
    w = w.reshape(k, P, w.shape[1])
    return np.stack([np.ascontiguousarray(w[:, :, c].transpose(1, 0, 2)).reshape(P, -1) for c in columns])


def laid_out(a):
    r = np.arange
    even = [r(c * 256, (c + 1) * 256) for c in range(64)]

    def col(v):
        v = np.asarray(v)
        return v.reshape(-1, P).T

    out = dict(shape_tables())
    for l in range(2):
        out[f"ada{l}"] = chunks_of(a["ada_w"][l], even[:24])
        out[f"ada{2 + l}"] = chunks_of(a["ada_w_2"][l], even[:12])
        w = a["ffn_w_up"][l]
        out[f"up{l}"] = chunks_of(w, [np.concatenate([r(j * P, (j + 1) * P), FF + r(j * P, (j + 1) * P)])
                                      for j in range(FT)])
        out[f"down{l}"] = chunks_of(a["ffn_w_down"][l], [r(c * P, (c + 1) * P) for c in range(KT)])
    w = a["ev_w_in"][0]
    for h in range(2):
        out[f"win{h}"] = chunks_of(w, [x + 256 * h + r(256) for x in (1024, 1536, 0, 512, 2048)])
    out["wmlp"] = chunks_of(w, [2560 + r(256), 2816 + r(256), 3072 + r(256), 3328 + r(256)])
    out["wout0"] = chunks_of(a["ev_w_out"][0], even[:4])
    out["winM"] = chunks_of(a["od_w_in"][0], [r(256), 256 + r(256), 512 + r(256),
                                              np.concatenate([768 + r(128), 896 + r(64), 896 + r(64)])])
    out["qb"] = chunks_of(a["od_w_qb"][0], [np.concatenate([384 * c + r(128), 384 * c + 192 + r(128),
                                                            384 * c + 128 + r(64), 384 * c + 320 + r(64)])
                                            for c in range(3)])
    out["kvb"] = chunks_of(a["od_w_kvb"][0], [np.concatenate([512 * c + r(128), 512 * c + 256 + r(128),
                                                              512 * c + 128 + r(128), 512 * c + 384 + r(128)])
                                              for c in range(3)])
    out["woutM"] = chunks_of(a["od_w_out"][0], even[:4])
    out["winE"] = chunks_of(a["ab_w_in_2"][0], even[:16])
    out["woutE"] = chunks_of(a["ab_w_out_2"][0], even[:4])
    heads = np.concatenate([h * 64 + r(64) for h in BANDED_ORDER])
    w = a["c_w_in_2"][0]
    out["winC"] = chunks_of(w, [heads[256 * c:256 * c + 256] for c in range(4)] + [1024 + r(256), 1280 + r(256)]
                            + [1536 + heads[256 * c:256 * c + 256] for c in range(4)])
    out["woutC"] = chunks_of(a["c_w_out_2"][0][heads], even[:4])
    vecs = dict(c=col(a["c"]), cc=col(a["c_ctx"]), c2=col(a["c_2"]), lb=col(a["ev_lb_logits"]),
                onorm=col(a["ev_onorm_w"]), qa=col(a["od_qa_norm_w"]), kva=col(a["od_kva_norm_w"]),
                subln=col(a["diff_subln_g_2"]), fg=col(a["final_g_2"]))
    for l in range(2):
        vecs[f"ab{l}"], vecs[f"ab{2 + l}"] = col(a["ada_b"][l]), col(a["ada_b_2"][l])
        vecs[f"nm{l}"], vecs[f"nf{l}"] = col(a["norm_mix_w"][l]), col(a["norm_ffn_w"][l])
        vecs[f"ng{l}"] = col(a["norm_g_2"][l])
        vecs[f"cw{l}"], vecs[f"cb{l}"] = col(a["ffn_conv_w"][l]), col(a["ffn_conv_b"][l])
    for x, w in (("q", a["od_q_norm_w"][0]), ("k", a["od_k_norm_w"][0])):
        vecs[x + "n"] = col(w[:P])
        vecs[x + "p"] = col(np.concatenate([w[P:], w[P:]]))
    lam = np.concatenate([a[f"diff_{x}_2"][0] for x in ("lq1", "lk1", "lq2", "lk2")])
    vecs["lam"] = np.broadcast_to(lam[None], (P, 256))
    vecs["sink"] = np.broadcast_to(a["c_sink_2"][0][BANDED_ORDER][None], (P, 16))
    out["vecs"] = np.concatenate([vecs[name] for name in VECS], 1)
    out["xl"] = a["x"][0].T.reshape(KT, P, S).transpose(1, 0, 2)
    out["xc"] = a["ctx"][0].T.reshape(KT, P, CTX).transpose(1, 0, 2)
    out["vnw"] = np.broadcast_to(a["ev_vnorm_w"][0][None], (P, 4, P))
    out["bsb"] = np.broadcast_to(a["ev_bs"][0][None], (P, 4, P))
    out["wst"] = a["ev_ws"][0].transpose(2, 0, 1)
    return {k: np.ascontiguousarray(v) for k, v in out.items()}


def kernel(**inputs):
    import concourse.bacc as bacc
    from concourse.bass_utils import run_bass_kernel_spmd

    arrays = laid_out({k: np.asarray(v) for k, v in inputs.items()})
    nc = bacc.Bacc("TRN2", target_bir_lowering=False, num_devices=1)
    dram = {k: nc.dram_tensor(k + "_dram", v.shape, F32, kind="ExternalInput").ap() for k, v in arrays.items()}
    out = nc.dram_tensor("out_dram", (P, KT, S), F32, kind="ExternalOutput").ap()
    two_blocks(nc, dram, out)
    r = run_bass_kernel_spmd(nc, [{k + "_dram": v for k, v in arrays.items()}], core_ids=[0])
    y = r.results[0]["out_dram"]
    return np.ascontiguousarray(y.transpose(2, 1, 0).reshape(1, S, D))
```

```python
from contextlib import ExitStack

import numpy as np
import concourse.bass as bass
from concourse import mybir

F32 = mybir.dt.float32
F32R = mybir.dt.float32r
U32 = mybir.dt.uint32
ALU = mybir.AluOpType
ACT = mybir.ActivationFunctionType
AX = mybir.AxisListType

P = 128
D = 1024
KT = D // P
S = 512
CTX = 256
T = S + CTX
SEGS = [(0, S), (S, CTX)]
FF = 2816
FT = FF // P
EPS = 1e-6
F_MIN = 1e-6
HEADS_M = 6
NSLOT = 3
SLOT = FF
LEVELS = (64, 32, 16, 8, 4)
LEAF = 4
LAM_INIT = 0.8 - 0.6
WINDOW = 128

CONST = dict(ident=P, ones=P, ones64=P, rot=P, masks=12 * P, scan=T + 1)
VECS = dict(
    c=KT, cc=KT, c2=KT, ab0=48, ab1=48, ab2=24, ab3=24, nm0=KT, nm1=KT, nf0=KT, nf1=KT, ng0=KT, ng1=KT,
    fg=KT, lb=8, onorm=1, cw0=3 * FT, cw1=3 * FT, cb0=FT, cb1=FT, qa=3, kva=2, qn=1, qp=1, kn=1, kp=1,
    subln=1, lam=4 * 64, sink=16,
)


def offsets(table):
    at, out = 0, {}
    for name, n in table.items():
        out[name] = (at, at + n)
        at += n
    return out, at


CONST_AT, CONST_N = offsets(CONST)
VECS_AT, VECS_N = offsets(VECS)

WEIGHTS = dict(
    ada0=(24, 2048, (0, 1, 2)), ada1=(24, 2048, (0, 1, 2)), ada2=(12, 2048, (0, 1, 2)), ada3=(12, 2048, (0, 1, 2)),
    win0=(5, 2048, (0, 1, 2)), win1=(5, 2048, (0, 1, 2)), wmlp=(4, 2048, (0, 1, 2)),
)
ADAS = ("ada0", "ada1", "ada2", "ada3")
SPLIT = dict(
    wout0=(8, D), up0=(2 * FT, D), down0=(2 * FT, D), winM=(8, D), qb=(9, 3 * P), kvb=(6, 4 * P), woutM=(8, D),
    up1=(2 * FT, D), down1=(FT, D), winE=(32, D), woutE=(8, D), winC=(20, D), woutC=(8, D),
)
SPLIT_BEFORE, _n = {}, 0
for _name, (_k, _) in SPLIT.items():
    SPLIT_BEFORE[_name] = _n
    _n += _k
B8 = tuple(range(8))
SUMS = dict(
    ada0=(1, (0,)), ada1=(1, (1,)), ada2=(1, (2,)), ada3=(1, (3,)),
    n0=(2, B8), win0=(22, B8), hgS0=(36, (0, 1, 2)), hgK0=(6, (3,)), hgO0=(12, (4, 5)), hgU0=(10, (6, 7)), ro0=(4, B8),
    win1=(22, B8), hgS1=(36, (0, 1, 2)), hgK1=(6, (3,)), hgO1=(12, (4, 5)), hgU1=(10, (6, 7)), ro1=(4, B8),
    wmlp=(20, B8), sv=(8, B8), wout0=(16, B8),
    n1=(2, B8), up0=(88, B8), down0=(8, B8), down0c=(4, (0, 1, 2, 3)),
    n2=(2, B8), winM=(11, B8), nlat=(5, B8), ropek=(1, B8), qb=(9, B8), kvb=(24, B8), nqk=(21, B8), ropeq=(3, B8),
    fa=(4, B8), fb=(2, B8),
    mS=(24, (0, 2)), mT=(24, (4,)), mV=(6, (6, 7)), woutM=(8, B8),
    n3=(1, B8), up1=(44, (0, 1, 2, 3)), down1=(8, B8),
    n4=(1, B8), winE=(32, B8), aS=(32, (0, 1, 2)), aT=(32, (3, 4, 5)), aV=(4, (6, 7)),
    bS=(32, (0, 1, 2)), bT=(16, (3, 4, 5)), bV=(4, (6, 7)), nB=(4, B8), woutE=(8, B8),
    n5=(1, B8), winC=(20, B8), cS=(64, (0, 1, 2)), cT=(64, (3, 4, 5)), cV=(8, (6, 7)), woutC=(8, B8),
    n6=(1, B8),
)


def uses(table, n_rings, ring):
    total, out = [0] * n_rings, {}
    for name, row in table.items():
        n, places = row[0], row[ring]
        out[name] = {b: total[b] for b in places}
        for k in range(n):
            total[places[k % len(places)]] += 1
    return out


SLOT_USED = uses(WEIGHTS, NSLOT, 2)
BANK_USED = uses(SUMS, 8, 1)


def slot_use(stage, k, loops=0):
    ring = WEIGHTS[stage][2]
    s = ring[k % len(ring)]
    return s, loops + (SLOT_USED[stage][s] + k // len(ring))


def bank_use(stage, k, loops=0):
    ring = SUMS[stage][1]
    b = ring[k % len(ring)]
    return b, loops + (BANK_USED[stage][b] + k // len(ring))


BANKS_BEFORE = {}
_n = [0] * 8
for _name, (_k, _places) in SUMS.items():
    BANKS_BEFORE[_name] = list(_n)
    for _j in range(_k):
        _n[_places[_j % len(_places)]] += 1
NORM_STAGES = [x for x in SUMS if x in ("n0", "ro0", "ro1", "n1", "n2", "nlat", "nqk", "n3", "n4", "nB", "n5", "n6")]
H_ITEMS = dict(n0=0, n1=2, n2=4, n3=6, n4=7, n5=8)
NORMS_UP_TO = {x: sum(SUMS[y][0] for y in NORM_STAGES[:NORM_STAGES.index(x) + 1]) for x in NORM_STAGES}

PASSES = dict(a=(8, 1), b=(4, 2), c=(16, 1))
HEADS_BEFORE = dict(a=0, b=8, c=12)
PROBS_BEFORE = dict(a=0, b=32, c=64)
BANDED_ORDER = [8 * a + r + 4 * x for a in range(2) for r in range(4) for x in range(2)]


class Step:

    def __init__(self, eng, sem):
        self.eng, self.sem, self.n = eng, sem, 0

    def mark(self, ins):
        self.n += 1
        ins.then_inc(self.sem, 1)
        return self.n

    def link(self, ins):
        self.eng.wait_ge(self.sem, self.mark(ins))

    def settle(self):
        if self.n:
            self.eng.wait_ge(self.sem, self.n)


def hgrn_steps():
    out = []
    for i in range(3):
        fwd = (4, 5) if i == 0 else (2 * i - 2, 2 * i - 1)
        bwd = (5, 4) if i == 0 else (5 - 2 * i, 4 - 2 * i)
        out += [(0, fwd, i), (1, bwd, i)]
    return out


def two_blocks(nc, dram, out):
    with ExitStack() as ctx:
        def sb(name, *shape):
            return ctx.enter_context(nc.sbuf_tensor(name, [P, *shape], F32))

        def sem(name):
            return ctx.enter_context(nc.semaphore(name))

        ps = ctx.enter_context(nc.psum_tensor("ps", [P, 8, 512], F32))
        const, vecs = sb("const", CONST_N), sb("vecs", VECS_N)
        XL, XC = sb("XL", KT, S), sb("XC", KT, CTX)
        mod = sb("mod", 2, 48, 2)
        mod2 = sb("mod2", 2, 24)
        gain = sb("gain", 4, KT, 2)
        gain2 = sb("gain2", 2, KT)
        cs = sb("cs", KT, 2)
        cs2 = sb("cs2", KT)
        small = sb("small", 96)
        SQ = sb("SQ", 2, S)
        R = sb("R", 2, S)
        csR = ctx.enter_context(nc.sbuf_tensor("csR", [P, KT, 4], F32R))
        cs2R = ctx.enter_context(nc.sbuf_tensor("cs2R", [P, KT, 2], F32R))
        ARENA = 26130
        RING, HB = NSLOT * SLOT, KT * T

        def parts(name, at, *shape):
            with nc.sbuf_tensor(f"{name}_before", [P, at], F32), nc.sbuf_tensor(name, [P, *shape], F32R) as place:
                assert at + int(np.prod(shape)) <= RING + HB + ARENA
            return place[:]

        H_AT, ARENA_AT = RING, RING + HB
        WHR, WLR = parts("w_high", 2 * D, 2, D), parts("w_low", 4 * D, 2, D)
        HH = (parts("h_high", H_AT, KT, S), parts("h_ctx_high", H_AT + KT * S, KT, CTX))
        LOW_AT = dict(n1=24 * T, n2=15 * T, n3=24 * T, n4=32 * S, n5=32 * S)
        LOW = {at: (parts(f"h_low{at}", ARENA_AT + at, KT, S), parts(f"h_ctx_low{at}", ARENA_AT + at + KT * S, KT, CTX))
               for at in sorted(set(LOW_AT.values()))}
        YH0, YL0 = (parts(f"y{x}_both", ARENA_AT + x * KT * T, KT, T) for x in (1, 2))
        YH, YLo = (parts(f"y{x}", ARENA_AT + x * KT * S, KT, S) for x in (0, 1))
        ADH, ADL = (parts(f"ada{x}", ARENA_AT + x * NSLOT * 2048, NSLOT, 2048) for x in (0, 1))
        GS = parts("hidden", ARENA_AT + 24 * T, 2, 2, S)
        QLH, QLL = (parts(f"q_lat{x}", H_AT + x * 3 * S, 3, S) for x in (0, 1))
        KVH, KVL = (parts(f"kv_lat{x}", H_AT + 6 * S + x * 2 * T, 2, T) for x in (0, 1))
        ring = sb("ring", NSLOT, SLOT)
        Hbuf = sb("Hbuf", HB)
        arena = sb("arena", ARENA)
        HL = Hbuf[:, 0:KT * S].rearrange("p (k n) -> p k n", k=KT)
        HC = Hbuf[:, KT * S:].rearrange("p (k n) -> p k n", k=KT)
        RAW = [ring[:, 0, p * D:(p + 1) * D] for p in range(2)]
        WH = [WHR[:, p, :] for p in range(2)]
        WL = [WLR[:, p, :] for p in range(2)]

        def C(name):
            a, b = CONST_AT[name]
            return const[:, a:b]

        def V(name, k=None):
            a, b = VECS_AT[name]
            return vecs[:, a:b] if k is None else vecs[:, a + k:a + k + 1]

        def carve(*shapes, at=0):
            views = []
            for shape in shapes:
                n = int(np.prod(shape))
                v = arena[:, at:at + n]
                if len(shape) > 1:
                    names = [f"d{i}" for i in range(len(shape))]
                    v = v.rearrange(f"p ({' '.join(names)}) -> p {' '.join(names)}",
                                    **dict(zip(names[1:], shape[1:])))
                views.append(v)
                at += n
            assert at <= ARENA, at
            return views

        X, H = (XL, XC), (HL, HC)

        def tiles(flat, at, k, n):
            return flat[:, at:at + k * n].rearrange("p (k n) -> p k n", k=k)

        def low(at):
            return tiles(arena, at, KT, S), tiles(arena, at + KT * S, KT, CTX)

        ident = C("ident")
        masks = C("masks").rearrange("p (l n) -> p l n", n=P)

        bank_full = [sem(f"bank_full{b}") for b in B8]
        bank_free = [sem(f"bank_free{b}") for b in B8]
        slot_full = [sem(f"slot_full{s}") for s in range(NSLOT)]
        slot_free = [sem(f"slot_free{s}") for s in range(NSLOT)]
        act_step, dve_step, pool_step = sem("act_step"), sem("dve_step"), sem("pool_step")
        const_in = sem("const_in")
        mods_ready = sem("mods_ready")
        cs_ready = sem("cs_ready")
        sq_ready, sq_used = sem("sq_ready"), sem("sq_used")
        norm_done = sem("norm_done")
        h_ready = sem("h_ready")
        lb_step = sem("lb_step")
        out_done = sem("out_done")
        ada_spent = [sem(f"ada_spent{c}") for c in range(NSLOT)]
        ada_hi, cs_hi = sem("ada_hi"), sem("cs_hi")
        raw_full, raw_spent, w_spent = ([sem(f"{x}{p}") for p in range(2)] for x in ("raw_full", "raw_spent", "w_spent"))
        w_hi = sem("w_hi")
        y_hi, y_lo = sem("y_hi"), sem("y_lo")
        lat_hi, lat_lo = sem("lat_hi"), sem("lat_lo")
        g_hi, g_lo = sem("g_hi"), sem("g_lo")

        def bank_ap(stage, k):
            return ps[:, bank_use(stage, k)[0], :]

        def open_bank(eng, stage, k, loops=0):
            b, used = bank_use(stage, k, loops)
            if not (isinstance(used, int) and used == 0):
                eng.wait_ge(bank_free[b], used)
            return ps[:, b, :]

        def sums_done(ins, stage, k):
            ins.then_inc(bank_full[bank_use(stage, k)[0]], 1)

        def await_sums(eng, stage, k, loops=0):
            b, used = bank_use(stage, k, loops)
            eng.wait_ge(bank_full[b], used + 1)
            return ps[:, b, :]

        def taken(ins, stage, k):
            ins.then_inc(bank_free[bank_use(stage, k)[0]], 1)

        def await_taken(eng, stage, k, loops=0):
            b, used = bank_use(stage, k, loops)
            eng.wait_ge(bank_free[b], used + 1)

        def await_all_taken(eng, stage, n=None):
            n = SUMS[stage][0] if n is None else n
            for k in range(max(0, n - len(SUMS[stage][1])), n):
                await_taken(eng, stage, k)

        def await_chunk(eng, stage, k, loops=0):
            s, used = slot_use(stage, k, loops)
            eng.wait_ge(slot_full[s], (used + 1) * 16)
            return ring[:, s, :]

        def chunk_done(ins, stage, k):
            ins.then_inc(slot_free[slot_use(stage, k)[0]], 1)

        def load_chunk(eng, stage, k, row, loops=0):
            s, used = slot_use(stage, k, loops)
            if not (isinstance(used, int) and used == 0):
                eng.wait_ge(slot_free[s], used)
            L = WEIGHTS[stage][1]
            eng.dma_start(ring[:, s, 0:L], dram[stage][row]).then_inc(slot_full[s], 16)

        def split_use(stage, k, pairs=0):
            n = SPLIT_BEFORE[stage] + k
            return n % 2, pairs + n // 2

        def load_split(eng, stage, k, row, pairs=0):
            p, used = split_use(stage, k, pairs)
            if not (isinstance(used, int) and used == 0):
                eng.wait_ge(raw_spent[p], used)
            L = SPLIT[stage][1]
            eng.dma_start(RAW[p][:, 0:L], dram[stage][row]).then_inc(raw_full[p], 16)

        def split_hi(stage, k, pairs=0):
            p, used = split_use(stage, k, pairs)
            nc.scalar.wait_ge(raw_full[p], (used + 1) * 16)
            if not (isinstance(used, int) and used == 0):
                nc.scalar.wait_ge(w_spent[p], used)
            L = SPLIT[stage][1] if k < SPLIT[stage][0] else D
            nc.scalar.activation(WH[p][:, 0:L], RAW[p][:, 0:L], ACT.Copy).then_inc(w_hi, 1)

        def split_lo(stage, k, pairs=0):
            p, _ = split_use(stage, k, pairs)
            L = SPLIT[stage][1]
            nc.gpsimd.wait_ge(w_hi, 2 * pairs + (SPLIT_BEFORE[stage] + k + 1))
            nc.gpsimd.tensor_tensor(WL[p][:, 0:L], RAW[p][:, 0:L], WH[p][:, 0:L].bitcast(F32), ALU.subtract)\
                .then_inc(raw_spent[p], 1)

        def await_parts(eng, stage, k, pairs=0):
            p, used = split_use(stage, k, pairs)
            eng.wait_ge(raw_spent[p], used + 1)
            return WH[p], WL[p]

        def parts_done(pe, stage, k, sums, g, loops=0, pairs=0):
            await_sums(pe, sums, g, loops)
            pe.sem_inc(w_spent[split_use(stage, k, pairs)[0]], 1)

        class Norms:

            def __init__(self, eng, step=None):
                self.eng, self.step, self.sq, self.items = eng, step, 0, 0

            def squares(self, srcs, ready=None):
                for j, src in enumerate(srcs):
                    if ready:
                        ready(j)
                    if self.sq >= 2:
                        self.eng.wait_ge(sq_used, self.sq - 1)
                    n = src.shape[-1]
                    nc.scalar.activation(SQ[:, self.sq % 2, 0:n], src, ACT.Square).then_inc(sq_ready, 1)
                    self.sq += 1

            def mean(self, stage, k, ones, srcs):
                bank = open_bank(self.eng, stage, k)
                n = srcs[0].shape[-1]
                for j, src in enumerate(srcs):
                    self.eng.wait_ge(sq_ready, self.sq + 1)
                    ins = nc.tensor.matmul(bank[:, 0:n], ones, SQ[:, self.sq % 2, 0:n],
                                           start=(j == 0), stop=(j == len(srcs) - 1))
                    ins.then_inc(sq_used, 1)
                    self.sq += 1
                self.eng.wait_ge(sq_used, self.sq)
                self.eng.sem_inc(bank_full[bank_use(stage, k)[0]], 1)

            def root(self, stage, k, n, width):
                if self.items >= 2:
                    self.eng.wait_ge(norm_done, self.items - 1)
                bank = await_sums(self.eng, stage, k)
                taken(nc.scalar.activation(R[:, self.items % 2, 0:n], bank[:, 0:n], ACT.Sqrt,
                                           bias=small[:, 0:1], scale=1.0 / width), stage, k)
                self.items += 1

            def scale(self, stage, k, srcs, gains, dsts, shifts=None, highs=None, lows=None):
                await_taken(self.eng, stage, k)
                n = srcs[0].shape[-1]
                r = R[:, self.items % 2, 0:n]
                self.step.link(nc.vector.reciprocal(r, r))
                for j, (src, g, dst) in enumerate(zip(srcs, gains, dsts)):
                    ins = nc.vector.scalar_tensor_tensor(dst, src, g, r, ALU.mult, ALU.mult)
                    if j == len(srcs) - 1:
                        ins.then_inc(norm_done, 1)
                    elif shifts:
                        self.step.mark(ins)
                self.items += 1
                if shifts:
                    self.step.settle()
                    self.eng.wait_ge(norm_done, self.items)
                    for j, dst in enumerate(dsts):
                        if highs:
                            self.step.mark(nc.vector.tensor_scalar(highs[j], dst, shifts[j], None, ALU.add))
                        else:
                            nc.vector.tensor_scalar(dst, dst, shifts[j], None, ALU.add).then_inc(h_ready, 1)
                    if highs:
                        self.step.settle()
                        for j, dst in enumerate(dsts):
                            nc.vector.scalar_tensor_tensor(lows[j], dst, shifts[j], highs[j].bitcast(F32), ALU.add,
                                                           ALU.subtract).then_inc(h_ready, 1)

        def modulated(l, which, segs, parts_of=None):
            items = []
            for s in segs:
                x, h = X[s], H[s]
                hi = lo = None
                if parts_of:
                    at = LOW_AT[parts_of]
                    h, hi, lo = low(at)[s], HH[s], LOW[at][s]
                items.append(([x[:, k, :] for k in range(KT)], (C("ones"), D),
                              [gain[:, 2 * l + which, k, s:s + 1] for k in range(KT)],
                              [h[:, k, :] for k in range(KT)],
                              [mod[:, l, 24 * which + k, s:s + 1] for k in range(KT)],
                              hi and [hi[:, k, :] for k in range(KT)], lo and [lo[:, k, :] for k in range(KT)]))
            return items

        def modulated2(l, parts_of):
            at = LOW_AT[parts_of]
            h, hi, lo = low(at)[0], HH[0], LOW[at][0]
            return [([XL[:, k, :] for k in range(KT)], (C("ones"), D), [gain2[:, l, k:k + 1] for k in range(KT)],
                     [h[:, k, :] for k in range(KT)], [mod2[:, l, k:k + 1] for k in range(KT)],
                     [hi[:, k, :] for k in range(KT)], [lo[:, k, :] for k in range(KT)])]

        def norm_act(nrm, stage, items, ready=None):
            for k, it in enumerate(items):
                nrm.squares(it[0], ready and (lambda j, k=k: ready(k, j)))
                if k:
                    nrm.root(stage, k - 1, items[k - 1][0][0].shape[-1], items[k - 1][1][1])
            nrm.root(stage, len(items) - 1, items[-1][0][0].shape[-1], items[-1][1][1])

        def norm_pe(nrm, stage, items):
            for k, it in enumerate(items):
                nrm.mean(stage, k, it[1][0], it[0])

        def norm_dve(nrm, stage, items):
            for k, it in enumerate(items):
                nrm.scale(stage, k, it[0], *it[2:])

        def features(pe, stage, sums, g, w, kt, m, width, src, segs, loops=0, last=None, kmaj=None):
            for i, s in enumerate(segs):
                bank = open_bank(pe, sums, g + i, loops)
                n = SEGS[s][1]
                for k in range(kt):
                    ins = nc.tensor.matmul(bank[:, 0:n], w[:, k * width + m:k * width + m + P], src(s, k),
                                           start=(k == 0), stop=(k == kt - 1))
                sums_done(ins, sums, g + i)
            return g + len(segs)

        def tokens(pe, sums, g, w, kt, width, m0, n, src, tiles):
            for t in tiles:
                bank = open_bank(pe, sums, g)
                for k in range(kt):
                    ins = nc.tensor.matmul(bank[:, 0:n], src(t, k), w[:, k * width + m0:k * width + m0 + n],
                                           start=(k == 0), stop=(k == kt - 1))
                sums_done(ins, sums, g)
                g += 1
            return g

        def split_features(pe, stage, c, sums, g, kt, width, src, segs, ready=None, loops=0, pairs=0):
            wh, wl = await_parts(pe, stage, c, pairs)
            for i, s in enumerate(segs):
                bank = open_bank(pe, sums, g + i, loops)
                n = SEGS[s][1]
                for k in range(kt):
                    if ready:
                        ready(s, k)
                    hi, lo = src(s, k)
                    cols = slice(k * width, k * width + P)
                    nc.tensor.matmul(bank[:, 0:n], wh[:, cols], hi, start=(k == 0), stop=False)
                    nc.tensor.matmul(bank[:, 0:n], wh[:, cols], lo, start=False, stop=False)
                    ins = nc.tensor.matmul(bank[:, 0:n], wl[:, cols], hi, start=False, stop=(k == kt - 1))
                sums_done(ins, sums, g + i)
            return g + len(segs)

        def split_tokens(pe, stage, c, sums, g, kt, width, m0, src, groups):
            wh, wl = await_parts(pe, stage, c)
            for group in groups:
                bank = open_bank(pe, sums, g)
                for j, t in enumerate(group):
                    for k in range(kt):
                        hi, lo = src(t, k)
                        cols = slice(k * width + m0, k * width + m0 + P)
                        to = bank[:, j * P:(j + 1) * P]
                        nc.tensor.matmul(to, hi, wh[:, cols], start=(k == 0), stop=False)
                        nc.tensor.matmul(to, lo, wh[:, cols], start=False, stop=False)
                        ins = nc.tensor.matmul(to, hi, wl[:, cols], start=False, stop=(k == kt - 1))
                sums_done(ins, sums, g)
                g += 1
            return g

        def h_parts(norm):
            lo = LOW[LOW_AT[norm]]
            return lambda s, k: (HH[s][:, k, :], lo[s][:, k, :])

        def h_tok_parts(norm):
            lo = LOW[LOW_AT[norm]][0]
            return lambda t, k: (HH[0][:, k, t * P:(t + 1) * P], lo[:, k, t * P:(t + 1) * P])

        def h_there(pe, norm):
            return lambda s, k: pe.wait_ge(h_ready, KT * (H_ITEMS[norm] + s) + k + 1)

        def h_seg(s, k):
            return H[s][:, k, :]

        def h_tok(t, k):
            return HL[:, k, t * P:(t + 1) * P] if t < 4 else HC[:, k, (t - 4) * P:(t - 3) * P]

        def release(pe, stage, k, sums, g, loops=0):
            await_sums(pe, sums, g, loops)
            pe.sem_inc(slot_free[slot_use(stage, k)[0]], 1)

        Y, = carve((8, T))
        (A_q, A_k0, A_b0, A_k1, A_b1, A_v, A_g, WK, ACC, KD, ST, EL) = carve(
            (2, T), (2, T), (2, T), (2, T), (2, T), (6, 256), (2, T), (2, 9, 2, 2, P), (2, 2, 2, P), (2, 2, 2, P),
            (2, 2, 2, P), (2, 2, 2), at=4 * T)
        A_k, A_b = (A_k0, A_k1), (A_b0, A_b1)
        U, VB, VNW, BSB, WST, MT, VSQ = carve((4, T), (24, P), (4, P), (4, P), (4, P), (2, S), (24, P), at=8 * T)
        VB4 = VB.rearrange("p (t q) n -> p t q n", q=4)
        ssq, rsq = small[:, 8:32], small[:, 32:56]
        G, FA = carve((FT, T), (2, T))

        hg_q = sem("hg_q")
        hg_g = sem("hg_g")
        hg_b = sem("hg_b")
        hg_e = sem("hg_e")
        hg_f = sem("hg_f")
        hg_ln = sem("hg_ln")
        hg_diff = sem("hg_diff")
        hg_exp = sem("hg_exp")
        hg_ops = sem("hg_ops")
        hg_acc = sem("hg_acc")
        hg_st = sem("hg_st")
        hg_round = sem("hg_round")
        mlp_v = sem("mlp_v")
        mlp_u = sem("mlp_u")
        mlp_tab = sem("mlp_tab")
        y_ready = sem("y_ready")

        STEPS = hgrn_steps()
        STATE_NO = {}
        for _d, _chunks, _i in STEPS:
            for _j in range(2):
                if 2 * _i + _j < 5:
                    STATE_NO[(_d, 2 * _i + _j)] = len(STATE_NO)

        def half(ap, m, second):
            v = ap.rearrange("p h (g x) -> p h g x", x=2 * m)
            return v[:, :, :, m:2 * m] if second else v[:, :, :, 0:m]

        def wk(w, a):
            return WK[:, w, a, :, :, :].rearrange("p h c n -> p h (c n)")

        def tok(buf, chunks):
            t0 = min(chunks) * P
            return buf[:, :, t0:t0 + 2 * P]

        def readout_items(r):
            return [([Y[:, 2 * r + j, a:a + n]], (C("ones"), P), [V("onorm", 0)], [Y[:, 2 * r + j, a:a + n]], None)
                    for j in range(2) for a, n in SEGS]

        def seg_of(buf, k, s):
            return buf[:, k, SEGS[s][0]:SEGS[s][0] + SEGS[s][1]]

        def lat_items():
            q = [M_QL[:, k, :] for k in range(3)]
            items = [(q, (C("ones"), 3 * P), [V("qa", k) for k in range(3)], q, None)]
            for s in range(2):
                kv = [seg_of(M_KV, k, s) for k in range(2)]
                items.append((kv, (C("ones"), 2 * P), [V("kva", k) for k in range(2)], kv, None))
            for s in range(2):
                pe_ = [seg_of(M_PE, 0, s)]
                items.append((pe_, (C("ones64"), 64), [V("kp", 0)], pe_, None))
            return items

        def qk_items():
            heads = [(M_QN[:, h, :], C("ones"), P, V("qn", 0)) for h in range(6)]
            heads += [(M_QP[:, j, :], C("ones64"), 64, V("qp", 0)) for j in range(3)]
            heads += [(seg_of(M_KN, h, s), C("ones"), P, V("kn", 0)) for h in range(6) for s in range(2)]
            return [([x], (o, w), [g], [x], None) for x, o, w, g in heads]

        def subln_items():
            return [([HL[:, 4 + h, :]], (C("ones"), P), [small[:, 6:7]], [HL[:, 4 + h, :]], None) for h in range(4)]

        def final_items():
            return [([XL[:, k, :] for k in range(KT)], (C("ones"), D), [V("fg", k) for k in range(KT)],
                     [HL[:, k, :] for k in range(KT)], None)]

        G_BEFORE = (0, 2 * FT)
        ffn_tap = [sem("ffn_tap0"), sem("ffn_tap1")]
        ffn_silu = [sem("ffn_silu0"), sem("ffn_silu1")]

        (M_C, M_QL, M_KV, M_PE, M_QN, M_QP, M_KN, M_V, M_P, M_T, M_COS, M_SIN) = carve(
            (2, S), (3, S), (2, T), (1, T), (6, S), (3, S), (6, T), (6, 6, P), (2, T), (6, S), (S,), (S,))
        M_T2, = carve((6, S), at=2 * S)
        M_PT = (M_T, M_T2)
        M_AB, = carve((4, 2, 2 * P), at=2 * S)
        M_DFT, = carve((8, S), at=2 * S + 3 * S + 2 * T + T + 6 * S + 3 * S + 6 * T + 6 * T)
        M_TMP = M_T[:, 5, :]
        M_CC, = carve((2 * P,), at=ARENA - 2 * P)
        M_DG, = carve((2, P), at=ARENA - 4 * P)
        YM = HL
        m_tab = sem("m_tab")
        m_dft = sem("m_dft")
        m_rope = sem("m_rope")
        m_max = sem("m_max")
        m_diag = sem("m_diag")

        (E_QA, E_KA, E_VA, E_QB, E_KB, E_VB, E_G, E_S, E_P, E_T, E_BIAS, E_DG) = carve(
            (4, S), (4, S), (4, 4, P), (4, S), (4, S), (4, 4, P), (8, S), (2, S), (4, S), (2, 4, S), (2, 896), (4, P))
        (C_Q, C_K, C_V, C_G) = carve((8, S), (2, S), (4, 2, P), (8, S))
        C_BIAS = E_BIAS[:, :, 0:384]
        e_bias = [sem("e_bias0"), sem("e_bias1")]
        e_p, e_dg = sem("e_p"), sem("e_dg")
        SINKS = small[:, 24:40]
        e_head = sem("e_head")
        lam_sem = sem("lam_sem")

        def key_tiles(kind, i):
            return range(4) if kind != "c" else range(max(0, i - 1), min(4, i + 2))

        block = ctx.enter_context(nc.Block())

        @block.sync
        def _(sp):
            sp.dma_start(vecs[:, :], dram["vecs"]).then_inc(const_in, 16)
            sp.dma_start(const[:, :], dram["const"]).then_inc(const_in, 16)
            sp.dma_start(XL[:, :, :], dram["xl"]).then_inc(const_in, 16)
            sp.dma_start(XC[:, :, :], dram["xc"]).then_inc(const_in, 16)
            for stage, (n, _, slots) in WEIGHTS.items():
                body = len(slots)
                first = body if SLOT_USED[stage][slots[0]] == 0 else 0
                for k in range(first):
                    load_chunk(sp, stage, k, k)
                rounds = n // body
                if rounds > 1:
                    with sp.Fori(first // body, rounds) as i:
                        for k in range(body):
                            load_chunk(sp, stage, k, i * body + k, i)
                for k in range(rounds * body if rounds > 1 else first, n):
                    load_chunk(sp, stage, k, k)
            for s in range(NSLOT):
                uses_ = sum(1 for st in WEIGHTS for k in range(WEIGHTS[st][0]) if WEIGHTS[st][2][k % NSLOT] == s)
                sp.wait_ge(slot_free[s], uses_)

            def tables(kinds, first_head):
                hh = first_head
                for kind in kinds:
                    for h in range(PASSES[kind][0]):
                        if hh >= 2:
                            pk = "a" if hh - 2 < 8 else "b" if hh - 2 < 12 else "c"
                            u = (4 * (hh - 2 - HEADS_BEFORE[pk]) + 4) * PASSES[pk][1] - 1
                            await_taken(sp, pk + "S", u)
                        to = E_BIAS[:, hh % 2, :] if kind != "c" else C_BIAS[:, hh % 2, :]
                        sp.dma_start(to, dram["bias_" + kind][h]).then_inc(e_bias[hh % 2], 16)
                        hh += 1

            for stage, (n, _) in SPLIT.items():
                first = 2 if SPLIT_BEFORE[stage] == 0 else 0
                for k in range(first):
                    load_split(sp, stage, k, k)
                if stage in ("woutE", "woutC"):
                    first = 2
                with sp.Fori(first // 2, n // 2) as i:
                    for k in range(2):
                        load_split(sp, stage, k, i * 2 + k, i)
                if n % 2:
                    load_split(sp, stage, n - 1, n - 1)
                if stage == "winM":
                    await_all_taken(sp, "down0c")
                    for name, to in (("cos", M_COS), ("sin", M_SIN)):
                        sp.dma_start(to, dram[name]).then_inc(m_tab, 16)
                    for name, to in (("cc", M_CC), ("dft", M_DFT)):
                        sp.dma_start(to, dram[name]).then_inc(m_dft, 16)
                for into, kinds, first_head, after in (("winE", "ab", 0, "woutE"), ("winC", "c", 12, "woutC")):
                    if stage == into:
                        for k in range(2):
                            load_split(sp, after, k, k)
                        await_all_taken(sp, stage)
                        tables(kinds, first_head)
            sp.wait_ge(norm_done, NORMS_UP_TO["n6"])
            sp.dma_start(out, HL[:, :, :]).then_inc(out_done, 16)
            sp.wait_ge(out_done, 16)

        @block.tensor
        def _(pe):
            nrm = Norms(pe)

            def mods(stage, vec):
                b, w_ = SUMS[stage][1][0], vec.shape[-1]
                open_bank(pe, stage, 0)
                with pe.Fori(0, WEIGHTS[stage][0] // NSLOT) as i:
                    for c in range(NSLOT):
                        s, used = slot_use(stage, c, i)
                        pe.wait_ge(slot_free[s], used + 1)
                        for m in range(2):
                            to = ps[:, b, bass.ds((i * NSLOT + c) * 2 * w_ + m * w_, w_)]
                            for k in range(KT):
                                cols = slice(k * 256 + m * P, k * 256 + (m + 1) * P)
                                nc.tensor.matmul(to, ADH[:, c, cols], vec[:, k, :], start=(k == 0), stop=False)
                                ins = nc.tensor.matmul(to, ADL[:, c, cols], vec[:, k, :], start=False,
                                                       stop=(k == KT - 1))
                        ins.then_inc(ada_spent[c], 1)
                pe.wait_ge(ada_spent[NSLOT - 1], 1 + SLOT_USED[stage][NSLOT - 1] + WEIGHTS[stage][0] // NSLOT)
                pe.sem_inc(bank_full[b], 1)

            for c in range(NSLOT):
                pe.sem_inc(ada_spent[c], 1)
            pe.wait_ge(const_in, 64)
            pe.wait_ge(cs_ready, 5)
            mods("ada0", csR)
            mods("ada1", csR)
            mods("ada2", cs2R)
            mods("ada3", cs2R)

            norm_pe(nrm, "n0", modulated(0, 0, (0, 1)))
            pe.wait_ge(h_ready, 2 * KT)

            def hgrn(r):
                win, SS, SK, SO, SU = (f"{x}{r}" for x in ("win", "hgS", "hgK", "hgO", "hgU"))
                g = 0
                for c in range(5):
                    w = await_chunk(pe, win, c)
                    if c == 3:
                        g = tokens(pe, win, g, w, KT, 256, 0, 256, h_tok, range(6))
                    else:
                        for m in range(2):
                            g = features(pe, win, win, g, w, KT, m * P, 256, h_seg, (0, 1))
                    release(pe, win, c, win, g - 1)

                def scores(n):
                    w = n % 2
                    pe.wait_ge(hg_ops, 6 * r + n + 1)
                    for l in range(6):
                        bank = open_bank(pe, SS, 6 * n + l).rearrange("p (h c t) -> p h c t", h=2, c=2)
                        ka, qa = (l, l) if l < 5 else (6, 5)
                        for h in range(2):
                            for c in range(2):
                                ins = nc.tensor.matmul(bank[:, h, c, :], WK[:, w, ka, h, c, :], WK[:, w, qa, h, c, :],
                                                       start=True, stop=True)
                        sums_done(ins, SS, 6 * n + l)
                    bank = open_bank(pe, SK, n).rearrange("p (h c t) -> p h c t", h=2, c=2)
                    for h in range(2):
                        for c in range(2):
                            ins = nc.tensor.transpose(bank[:, h, c, :], WK[:, w, 7, h, c, :], ident)
                    sums_done(ins, SK, n)

                def outputs(n):
                    d, chunks, i = STEPS[n]
                    w, lo = n % 2, min(chunks)
                    pe.wait_ge(hg_acc, 6 * r + n + 1)
                    await_taken(pe, SK, n)
                    for j, ch in enumerate(chunks):
                        c, q = ch - lo, 2 * i + j
                        if q:
                            pe.wait_ge(hg_st, 10 * r + STATE_NO[(d, q - 1)] + 1)
                        bank = open_bank(pe, SO, 2 * n + j)
                        for h in range(2):
                            ins = nc.tensor.matmul(bank[:, h * P:(h + 1) * P], A_v[:, ch, h * P:(h + 1) * P],
                                                   ACC[:, w, h, c, :], start=True, stop=(q == 0))
                            if q:
                                ins = nc.tensor.matmul(bank[:, h * P:(h + 1) * P], ST[:, d, (q - 1) % 2, h, :],
                                                       WK[:, w, 8, h, c, :], start=False, stop=True)
                        sums_done(ins, SO, 2 * n + j)
                        if q < 5:
                            u = STATE_NO[(d, q)]
                            bank = open_bank(pe, SU, u)
                            for h in range(2):
                                ins = nc.tensor.matmul(bank[:, h * P:(h + 1) * P], KD[:, w, h, c, :],
                                                       A_v[:, ch, h * P:(h + 1) * P], start=True, stop=True)
                            sums_done(ins, SU, u)

                for n in range(7):
                    if n < 6:
                        scores(n)
                    if n:
                        outputs(n - 1)
                norm_pe(nrm, f"ro{r}", readout_items(r))

            hgrn(0)
            hgrn(1)

            g = 0
            for c in range(4):
                w = await_chunk(pe, "wmlp", c)
                if c < 2:
                    for m in range(2):
                        g = features(pe, "wmlp", "wmlp", g, w, KT, m * P, 256, h_seg, (0, 1))
                else:
                    g = tokens(pe, "wmlp", g, w, KT, 256, 0, 256, h_tok, range(6))
                release(pe, "wmlp", c, "wmlp", g - 1)
            pe.wait_ge(mlp_v, 1)
            for q in range(4):
                for i, (a, n) in enumerate(SEGS):
                    bank = open_bank(pe, "sv", 2 * q + i)
                    for c in range(n // P):
                        ins = nc.tensor.matmul(bank[:, c * P:(c + 1) * P], VB4[:, a // P + c, q, :], WST[:, q, :],
                                               start=True, stop=True)
                    sums_done(ins, "sv", 2 * q + i)

            def project_out(stage, hi, lo, segs, before):
                g = 0
                for c in range(KT):
                    g = split_features(pe, stage, c, stage, g, KT, P,
                                       lambda s, k: (seg_of(hi, k, s), seg_of(lo, k, s)), segs,
                                       ready=(lambda s, k: pe.wait_ge(y_lo, before + k + 1)) if c == 0 else None)
                    parts_done(pe, stage, c, stage, g - 1)

            def ffn(l, segs, norm):
                up, down = f"up{l}", f"down{l}"
                ns = len(segs)
                for s in segs:
                    h_there(pe, norm)(s, KT - 1)
                with pe.Fori(0, FT // 2) as i:
                    for c in range(4):
                        split_features(pe, up, c, up, ns * c, KT, P, h_parts(norm), segs, loops=i, pairs=2 * i)
                        parts_done(pe, up, c, up, ns * c + ns - 1, loops=i, pairs=2 * i)
                for x, s in enumerate(segs):
                    n = SEGS[s][1]
                    sums = down + "c" if s else down
                    per = S // n

                    def hidden(c, pairs, start, stop):
                        k = FT * x + c
                        wh, wl = await_parts(pe, down, k, pairs)
                        pe.wait_ge(g_lo, 2 * pairs + (G_BEFORE[l] + k + 1))
                        p = split_use(down, k)[0]
                        hi, lo = GS[:, p, 0, 0:n], GS[:, p, 1, 0:n]
                        for m in range(KT):
                            if start and m % per == 0:
                                open_bank(pe, sums, m // per)
                            to = bank_ap(sums, m // per)[:, (m % per) * n:(m % per + 1) * n]
                            cols = slice(m * P, (m + 1) * P)
                            MM = nc.tensor.matmul
                            MM(to, wh[:, cols], hi, start=start and m % per == 0, stop=False, skip_group_check=True)
                            MM(to, wh[:, cols], lo, start=False, stop=False, skip_group_check=True)
                            ins = MM(to, wl[:, cols], hi, start=False, stop=stop, skip_group_check=True)
                            if stop and m % per == per - 1:
                                sums_done(ins, sums, m // per)
                        if not stop:
                            ins.then_inc(w_spent[p], 1)
                        else:
                            await_sums(pe, sums, KT // per - 1)
                            pe.sem_inc(w_spent[p], 1)

                    hidden(0, 0, True, False)
                    hidden(1, 0, False, False)
                    with pe.Fori(1, FT // 2 - 1) as i:
                        for c in range(2):
                            hidden(c, i, False, False)
                    hidden(FT - 2, 0, False, False)
                    hidden(FT - 1, 0, False, True)

            project_out("wout0", YH0, YL0, (0, 1), 0)
            norm_pe(nrm, "n1", modulated(0, 1, (0, 1), "n1"))
            ffn(0, (0, 1), "n1")

            norm_pe(nrm, "n2", modulated(1, 0, (0, 1), "n2"))
            for s in range(2):
                h_there(pe, "n2")(s, KT - 1)
            g = 0
            for c in range(8):
                g = split_features(pe, "winM", c, "winM", g, KT, P, h_parts("n2"), (0,) if c < 5 else (0, 1))
                parts_done(pe, "winM", c, "winM", g - 1)
            norm_pe(nrm, "nlat", lat_items())
            pe.wait_ge(norm_done, NORMS_UP_TO["nlat"])
            bank = open_bank(pe, "ropek", 0)
            pe.wait_ge(m_tab, 32)
            sums_done(nc.tensor.matmul(bank[:, :], C("rot"), M_PE[:, 0, 0:S], start=True, stop=True), "ropek", 0)
            pe.wait_ge(lat_lo, 2)
            for c in range(9):
                split_features(pe, "qb", c, "qb", c, 3, P, lambda s, k: (QLH[:, k, :], QLL[:, k, :]), (0,))
                parts_done(pe, "qb", c, "qb", c)
            for h in range(6):
                g = split_features(pe, "kvb", h, "kvb", 4 * h, 2, 2 * P,
                                   lambda s, k: (seg_of(KVH, k, s), seg_of(KVL, k, s)), (0, 1))
                split_tokens(pe, "kvb", h, "kvb", g, 2, 2 * P, P,
                             lambda t, k: (KVH[:, k, t * P:(t + 1) * P], KVL[:, k, t * P:(t + 1) * P]),
                             (range(4), range(4, 6)))
                parts_done(pe, "kvb", h, "kvb", 4 * h + 3)
            norm_pe(nrm, "nqk", qk_items())
            pe.wait_ge(norm_done, NORMS_UP_TO["nqk"])
            for j in range(3):
                bank = open_bank(pe, "ropeq", j)
                sums_done(nc.tensor.matmul(bank[:, :], C("rot"), M_QP[:, j, :], start=True, stop=True), "ropeq", j)
            pe.wait_ge(m_rope, 4)
            pe.wait_ge(m_dft, 32)
            for t in range(4):
                bank = open_bank(pe, "fa", t).rearrange("p (c n) -> p c n", c=2)
                for c in range(2):
                    ins = nc.tensor.matmul(bank[:, c, :], M_C[:, c, t * P:(t + 1) * P], M_CC, start=True, stop=True)
                sums_done(ins, "fa", t)
            await_all_taken(pe, "fa")
            for c in range(2):
                bank = open_bank(pe, "fb", c)
                for t in range(4):
                    for s in range(2):
                        ins = nc.tensor.matmul(bank[:, :], M_AB[:, t, c, s * P:(s + 1) * P], M_DFT[:, 4 * s + t, :],
                                               start=(t == 0 and s == 0), stop=(t == 3 and s == 1))
                sums_done(ins, "fb", c)
            await_all_taken(pe, "fb")
            for b in range(8):
                pe.wait_ge(bank_free[b], BANKS_BEFORE["mS"][b])
            units = [(h, i) for h in range(HEADS_M) for i in range(4)]

            def m_scores(u):
                h, i = units[u]
                b = bank_use("mS", u)[0]
                open_bank(pe, "mS", u)
                o = 64 * (h % 2)
                for j, (a, n) in enumerate(SEGS):
                    nc.tensor.matmul(ps[:, b + j, 0:n], M_QN[:, h, i * P:(i + 1) * P], M_KN[:, h, a:a + n],
                                     start=True, stop=False)
                    ins = nc.tensor.matmul(ps[:, b + j, 0:n], M_QP[o:o + 64, h // 2, i * P:(i + 1) * P],
                                           M_PE[o:o + 64, 0, a:a + n], start=False, stop=True)
                sums_done(ins, "mS", u)

            def m_turn(u):
                await_taken(pe, "mS", u)
                pe.wait_ge(m_diag, u + 1)
                open_bank(pe, "mT", u)
                for t in range(6):
                    ins = nc.tensor.matmul(ps[:, 4 + t // 4, (t % 4) * P:(t % 4 + 1) * P],
                                           M_P[:, u % 2, t * P:(t + 1) * P], M_DG[:, u % 2, :], start=True, stop=True)
                sums_done(ins, "mT", u)

            def m_values(h):
                await_taken(pe, "mT", 4 * h + 3)
                bank = open_bank(pe, "mV", h)
                for t in range(6):
                    ins = nc.tensor.matmul(bank[:, :], M_V[:, t, h, :], M_PT[h % 2][:, t, :],
                                           start=(t == 0), stop=(t == 5))
                sums_done(ins, "mV", h)

            for u in range(24 + 2):
                if u < 24:
                    m_scores(u)
                if 1 <= u <= 24:
                    m_turn(u - 1)
                if u >= 5 and u % 4 == 1:
                    m_values((u - 5) // 4)
            project_out("woutM", YH, YLo, (0,), 8)
            norm_pe(nrm, "n3", modulated(1, 1, (0,), "n3"))
            ffn(1, (0,), "n3")

            norm_pe(nrm, "n4", modulated2(0, "n4"))
            for c in range(32):
                if c // 4 in (2, 5):
                    split_tokens(pe, "winE", c, "winE", c, KT, P, 0, h_tok_parts("n4"), (range(4),))
                else:
                    split_features(pe, "winE", c, "winE", c, KT, P, h_parts("n4"), (0,),
                                   ready=h_there(pe, "n4") if c == 0 else None)
                parts_done(pe, "winE", c, "winE", c)
            await_all_taken(pe, "winE")

            def attention(kind):
                heads, two = PASSES[kind]
                n = 4 * heads
                probs = PROBS_BEFORE[kind]

                def scores(u):
                    h, i = u // 4, u % 4
                    kts = key_tiles(kind, i)
                    a, b = kts[0] * P, (kts[-1] + 1) * P
                    for x in range(two):
                        bank = open_bank(pe, kind + "S", two * u + x)
                        if kind == "a":
                            o, q, k = 64 * (h % 2), E_QA[:, h // 2, :], E_KA[:, h // 2, :]
                        elif kind == "b":
                            o, q, k = 64 * x, E_QB[:, h, :], E_KB[:, h, :]
                        else:
                            o, q, k = 64 * (h % 2), C_Q[:, h // 2, :], C_K[:, h // 8, :]
                        ins = nc.tensor.matmul(bank[:, 0:b - a], q[o:o + 64, i * P:(i + 1) * P], k[o:o + 64, a:b],
                                               start=True, stop=True)
                        sums_done(ins, kind + "S", two * u + x)

                def turn(u):
                    pe.wait_ge(e_p, probs + two * (u + 1))
                    pe.wait_ge(e_dg, probs + two * (u + 1))
                    bank = open_bank(pe, kind + "T", u)
                    for j in range(len(key_tiles(kind, u % 4))):
                        for x in range(two):
                            v = probs + two * u + x
                            ins = nc.tensor.matmul(bank[:, j * P:(j + 1) * P], E_P[:, v % 4, j * P:(j + 1) * P],
                                                   E_DG[:, v % 4, :], start=(x == 0), stop=(x == two - 1))
                    sums_done(ins, kind + "T", u)

                def values(h):
                    await_taken(pe, kind + "T", 4 * h + 3)
                    if kind == "b":
                        k, first, last = h, True, True
                        out_, v = slice(0, P), E_VB[:, :, h, :]
                    else:
                        k, first, last = h // 2, h % 2 == 0, h % 2 == 1
                        out_ = slice(64 * (h % 2), 64 * (h % 2) + 64)
                        v = E_VA[:, :, h // 2, out_] if kind == "a" else C_V[:, :, h // 8, out_]
                    if kind == "c":
                        jobs = [(i * P, P, list(key_tiles("c", i))) for i in range(4)]
                    else:
                        jobs = [(0, S, list(range(4)))]
                    bank = open_bank(pe, kind + "V", k) if first else bank_ap(kind + "V", k)
                    for a, n_, kts in jobs:
                        for j, t in enumerate(kts):
                            ins = nc.tensor.matmul(bank[out_, a:a + n_], v[:, t, :], E_T[:, h % 2, t, a:a + n_],
                                                   start=(j == 0), stop=(j == len(kts) - 1))
                    ins.then_inc(e_head, 1)
                    if last:
                        pe.wait_ge(e_head, HEADS_BEFORE[kind] + h + 1)
                        pe.sem_inc(bank_full[bank_use(kind + "V", k)[0]], 1)

                for u in range(n + 2):
                    if u < n:
                        scores(u)
                    if 1 <= u <= n:
                        turn(u - 1)
                    if u >= 5 and u % 4 == 1:
                        values((u - 5) // 4)

            attention("a")
            attention("b")
            norm_pe(nrm, "nB", subln_items())
            project_out("woutE", YH, YLo, (0,), 16)
            norm_pe(nrm, "n5", modulated2(1, "n5"))
            for c in range(20):
                if c in (10, 11):
                    split_tokens(pe, "winC", c, "winC", c, KT, P, 0, h_tok_parts("n5"), (range(4),))
                else:
                    split_features(pe, "winC", c, "winC", c, KT, P, h_parts("n5"), (0,),
                                   ready=h_there(pe, "n5") if c == 0 else None)
                parts_done(pe, "winC", c, "winC", c)
            await_all_taken(pe, "winC")
            attention("c")
            project_out("woutC", YH, YLo, (0,), 24)
            norm_pe(nrm, "n6", final_items())

        @block.scalar
        def _(act):
            nrm = Norms(act)
            A = nc.scalar.activation

            act.wait_ge(const_in, 64)
            A(cs[:, :, 0], V("c"), ACT.Silu).then_inc(cs_ready, 1)
            A(cs[:, :, 1], V("cc"), ACT.Silu).then_inc(cs_ready, 1)
            A(cs2[:, :], V("c2"), ACT.Silu).then_inc(cs_ready, 1)
            act.wait_ge(cs_ready, 3)
            A(csR[:, :, 0:2], cs[:, :, :], ACT.Copy).then_inc(cs_hi, 1)
            A(cs2R[:, :, 0], cs2[:, :], ACT.Copy).then_inc(cs_hi, 1)
            act.wait_ge(lb_step, 3)
            A(small[:, 72:80], small[:, 72:80], ACT.Exp)
            A(small[:, 3:5], small[:, 1:3], ACT.Exp).then_inc(lam_sem, 1)

            for stage in ADAS:
                with act.Fori(0, WEIGHTS[stage][0] // NSLOT) as i:
                    for c in range(NSLOT):
                        raw = await_chunk(act, stage, c, i)
                        act.wait_ge(ada_spent[c], i + (SLOT_USED[stage][c] + 1))
                        A(ADH[:, c, :], raw[:, 0:2048], ACT.Copy).then_inc(ada_hi, 1)

            norm_act(nrm, "n0", modulated(0, 0, (0, 1)))

            def y_high(y, to, n):
                for k in range(KT):
                    A(to[:, k, :], y[:, k, 0:n], ACT.Copy).then_inc(y_hi, 1)

            def hgrn(r):
                win, SS, SK, SO, SU = (f"{x}{r}" for x in ("win", "hgS", "hgK", "hgO", "hgU"))
                if r:
                    act.wait_ge(hg_diff, 6)
                for d in range(2):
                    for j in range(2):
                        for i, (a, n) in enumerate(SEGS):
                            g = 4 * d + 2 * j + i
                            bank = await_sums(act, win, g)
                            taken(A(A_b[d][:, j, a:a + n], bank[:, 0:n], ACT.Exp, scale=-1.0), win, g)
                for d in range(2):
                    act.wait_ge(hg_f, 2 * r + d + 1)
                    A(A_b[d][:, :, :], A_b[d][:, :, :], ACT.Ln).then_inc(hg_ln, 1)
                if r:
                    act.wait_ge(hg_ops, 6)
                for j in range(2):
                    for i, (a, n) in enumerate(SEGS):
                        g = 8 + 2 * j + i
                        bank = await_sums(act, win, g)
                        taken(A(A_q[:, j, a:a + n], bank[:, 0:n], ACT.Silu), win, g)

                def turned_keys(n):
                    if n >= 2:
                        await_sums(act, SO, 2 * (n - 2) + 1)
                        d, _, i = STEPS[n - 2]
                        await_sums(act, SU, STATE_NO[(d, min(2 * i + 1, 4))])
                    bank = await_sums(act, SK, n)
                    taken(A(KD[:, n % 2, :, :, :].rearrange("p h c n -> p (h c n)"), bank[:, :], ACT.Copy), SK, n)

                for n, (d, chunks, i) in enumerate(STEPS):
                    w = n % 2
                    act.wait_ge(hg_diff, 6 * r + n + 1)
                    b = tok(A_b[d], chunks)
                    A(WK[:, w, 0:8, :, :, :].rearrange("p a h c n -> p (a h c n)"),
                      WK[:, w, 0:8, :, :, :].rearrange("p a h c n -> p (a h c n)"), ACT.Exp)
                    e = b.rearrange("p h (c n) -> p h c n", c=2)[:, :, :, P - 1 if d == 0 else 0]
                    if n >= 2:
                        d2, _, i2 = STEPS[n - 2]
                        act.wait_ge(hg_st, 10 * r + STATE_NO[(d2, min(2 * i2 + 1, 4))] + 1)
                    elif r:
                        act.wait_ge(hg_st, 10)
                    A(EL[:, w, :, :], e, ACT.Exp)
                    A(wk(w, 8), b, ACT.Exp).then_inc(hg_exp, 1)
                    if n:
                        turned_keys(n - 1)
                turned_keys(5)
                A(A_g[:, :, :], A_g[:, :, :], ACT.Silu).then_inc(hg_g, 1)
                await_taken(act, SO, 10)
                await_taken(act, SO, 11)
                norm_act(nrm, f"ro{r}", readout_items(r))

            hgrn(0)
            hgrn(1)

            act.wait_ge(hg_round, 2)
            g = 0
            for q in range(4):
                for a, n in SEGS:
                    bank = await_sums(act, "wmlp", g)
                    taken(A(U[:, q, a:a + n], bank[:, 0:n], ACT.Gelu_apprx_tanh), "wmlp", g)
                    g += 1
            for c in range(2):
                for t in range(6):
                    bank = await_sums(act, "wmlp", g)
                    taken(A(VB4[:, t, 2 * c:2 * c + 2, :], bank[:, 0:256].rearrange("p (q n) -> p q n", q=2),
                            ACT.Gelu_apprx_tanh), "wmlp", g)
                    g += 1
            act.wait_ge(mlp_u, 1)
            A(rsq, ssq, ACT.Sqrt, bias=small[:, 0:1], scale=1.0 / P).then_inc(mlp_u, 1)

            def ahead(stage, k):
                if k + 2 < SPLIT[stage][0]:
                    split_hi(stage, k + 2)

            def ffn(l, segs):
                up, down = f"up{l}", f"down{l}"
                ns = len(segs)
                width = sum(SEGS[s][1] for s in segs)
                with act.Fori(0, FT // 2) as i:
                    for c in range(2):
                        split_hi(up, 2 * c + 2, 2 * i)
                        for x in range(ns):
                            await_taken(act, up, 2 * ns * c + x, i)
                        A(FA[:, c, 0:width], FA[:, c, 0:width], ACT.Silu).then_inc(ffn_silu[c], 1)
                        split_hi(up, 2 * c + 3, 2 * i)
                await_all_taken(act, up)
                for x, s in enumerate(segs):
                    a, n = SEGS[s]
                    flat = G.rearrange("p k n -> p (k n)")

                    def g_high(k, c, i=0):
                        p = split_use(down, FT * x + c)[0]
                        A(GS[:, p, 0, 0:n], flat[:, bass.ds(i * (2 * T) + (k * T + a), n)] if not isinstance(i, int)
                          else flat[:, k * T + a:k * T + a + n], ACT.Copy).then_inc(g_hi, 1)
                    for k in range(2):
                        if x:
                            split_hi(down, FT * x + k)
                        g_high(k, k)
                    with act.Fori(1, FT // 2) as i:
                        for k in range(2):
                            split_hi(down, FT * x + k, i)
                            g_high(k, k, i)

            act.wait_ge(y_ready, 1)
            y_high(Y, YH0, T)
            for k in range(8):
                split_hi("wout0", k)
            split_hi("up0", 0)
            split_hi("up0", 1)
            norm_act(nrm, "n1", modulated(0, 1, (0, 1), "n1"), lambda it, j: await_taken(act, "wout0", 2 * j + it))
            ffn(0, (0, 1))
            split_hi("winM", 0)
            split_hi("winM", 1)
            norm_act(nrm, "n2", modulated(1, 0, (0, 1), "n2"),
                     lambda it, j: await_taken(act, "down0c", j // 2) if it else await_taken(act, "down0", j))

            dst = [M_C[:, 0, :], M_C[:, 1, :]] + [M_QL[:, k, :] for k in range(3)]
            dst += [seg_of(M_KV, k, s) for k in range(2) for s in range(2)] + [seg_of(M_PE, 0, s) for s in range(2)]
            first_sum = {0: 0, 1: 1, 2: 2, 3: 3, 4: 4, 5: 5, 7: 6, 9: 7}
            for g, to in enumerate(dst):
                if g in first_sum:
                    ahead("winM", first_sum[g])
                bank = await_sums(act, "winM", g)
                taken(A(to, bank[:, 0:to.shape[-1]], ACT.Copy), "winM", g)
            await_all_taken(act, "winM")
            split_hi("qb", 0)
            split_hi("qb", 1)
            norm_act(nrm, "nlat", lat_items())
            act.wait_ge(norm_done, NORMS_UP_TO["nlat"])
            A(QLH, M_QL, ACT.Copy).then_inc(lat_hi, 1)
            A(KVH, M_KV, ACT.Copy).then_inc(lat_hi, 1)
            for g in range(9):
                c, m = g // 3, g % 3
                ahead("qb", g)
                bank = await_sums(act, "qb", g)
                taken(A(M_QN[:, 2 * c + m, :] if m < 2 else M_QP[:, c, :], bank[:, :], ACT.Copy), "qb", g)
            split_hi("kvb", 0)
            split_hi("kvb", 1)
            for h in range(6):
                ahead("kvb", h)
                for s in range(2):
                    bank = await_sums(act, "kvb", 4 * h + s)
                    taken(A(seg_of(M_KN, h, s), bank[:, 0:SEGS[s][1]], ACT.Copy), "kvb", 4 * h + s)
            await_all_taken(act, "qb")
            await_all_taken(act, "kvb")
            norm_act(nrm, "nqk", qk_items())
            for t in range(4):
                bank = await_sums(act, "fa", t)
                taken(A(M_AB[:, t, :, :].rearrange("p c n -> p (c n)"), bank[:, :], ACT.Copy), "fa", t)
            split_hi("woutM", 0)
            split_hi("woutM", 1)
            for u in range(25):
                if u < 24:
                    act.wait_ge(m_max, u + 1)
                    b = bank_use("mS", u)[0]
                    taken(A(M_P[:, u % 2, :], ps[:, b:b + 2, :].rearrange("p b n -> p (b n)")[:, 0:T], ACT.Exp,
                            bias=small[:, 8 + u % 2:9 + u % 2], scale=float(192 ** -0.5),
                            accum_out=small[:, 12 + u % 2:13 + u % 2]), "mS", u)
                if u:
                    h, i = (u - 1) // 4, (u - 1) % 4
                    if h >= 2 and i == 0:
                        await_sums(act, "mV", h - 2)
                    await_sums(act, "mT", u - 1)
                    taken(A(M_PT[h % 2][:, :, i * P:(i + 1) * P],
                            ps[:, 4:6, :].rearrange("p b n -> p (b n)")[:, 0:T].rearrange("p (t n) -> p t n", t=6),
                            ACT.Copy), "mT", u - 1)
            await_all_taken(act, "mV")
            await_all_taken(act, "fb")
            y_high(YM, YH, S)
            for k in range(2, 8):
                split_hi("woutM", k)
            split_hi("up1", 0)
            split_hi("up1", 1)
            norm_act(nrm, "n3", modulated(1, 1, (0,), "n3"), lambda it, j: await_taken(act, "woutM", j))
            ffn(1, (0,))

            split_hi("winE", 0)
            split_hi("winE", 1)
            norm_act(nrm, "n4", modulated2(0, "n4"), lambda it, j: await_taken(act, "down1", j))
            dst = [(E_QA[:, k, :], 0.125) for k in range(4)] + [(E_KA[:, k, :], 1.0) for k in range(4)] + [None] * 4
            dst += [(E_QB[:, k, :], 0.125) for k in range(4)] + [(E_KB[:, k, :], 1.0) for k in range(4)] + [None] * 4
            for g in range(32):
                ahead("winE", g)
                if g >= 24:
                    bank = await_sums(act, "winE", g)
                    taken(A(E_G[:, g - 24, :], bank[:, :], ACT.Silu), "winE", g)
                elif dst[g]:
                    bank = await_sums(act, "winE", g)
                    taken(A(dst[g][0], bank[:, :], ACT.Copy, scale=dst[g][1]), "winE", g)
            split_hi("woutE", 0)
            split_hi("woutE", 1)

            def attention(kind):
                heads, two = PASSES[kind]
                probs = PROBS_BEFORE[kind]
                for u in range(4 * heads + 1):
                    if u < 4 * heads:
                        n = P * len(key_tiles(kind, u % 4))
                        for x in range(two):
                            v = probs + two * u + x
                            await_taken(act, kind + "S", two * u + x)
                            if kind == "c":
                                A(small[:, 20 + v % 4:21 + v % 4], V("sink", u // 4), ACT.Exp,
                                  bias=small[:, 8 + v % 4:9 + v % 4])
                            A(E_P[:, v % 4, 0:n], E_S[:, v % 2, 0:n], ACT.Exp, scale=-1.0,
                              bias=small[:, 8 + v % 4:9 + v % 4],
                              accum_out=small[:, 12 + v % 4:13 + v % 4]).then_inc(e_p, 1)
                    if u:
                        h, i = (u - 1) // 4, (u - 1) % 4
                        n = HEADS_BEFORE[kind] + h
                        if n >= 2 and i == 0:
                            act.wait_ge(e_head, n - 1)
                        kts = key_tiles(kind, i)
                        bank = await_sums(act, kind + "T", u - 1)
                        taken(A(E_T[:, h % 2, kts[0]:kts[-1] + 1, i * P:(i + 1) * P],
                                bank[:, 0:P * len(kts)].rearrange("p (t n) -> p t n", n=P), ACT.Copy),
                              kind + "T", u - 1)

            attention("a")
            attention("b")
            await_all_taken(act, "bV")
            norm_act(nrm, "nB", subln_items())
            act.wait_ge(y_ready, 2)
            y_high(HL, YH, S)
            for k in range(2, 8):
                split_hi("woutE", k)
            split_hi("winC", 0)
            split_hi("winC", 1)
            norm_act(nrm, "n5", modulated2(1, "n5"), lambda it, j: await_taken(act, "woutE", j))
            for g in range(20):
                ahead("winC", g)
                if g in (10, 11):
                    continue
                bank = await_sums(act, "winC", g)
                if g < 10:
                    to, scale = (C_Q[:, g, :], 0.125) if g < 8 else (C_K[:, g - 8, :], 1.0)
                    taken(A(to, bank[:, :], ACT.Copy, scale=scale), "winC", g)
                else:
                    taken(A(C_G[:, g - 12, :], bank[:, :], ACT.Silu), "winC", g)
            split_hi("woutC", 0)
            split_hi("woutC", 1)
            attention("c")
            await_all_taken(act, "cV")
            y_high(HL, YH, S)
            for k in range(2, 8):
                split_hi("woutC", k)
            norm_act(nrm, "n6", final_items(), lambda it, j: await_taken(act, "woutC", j))

        @block.gpsimd
        def _(pool):
            TT = nc.gpsimd.tensor_tensor

            def differences(r, n):
                d, chunks, _ = STEPS[n]
                w, SO = n % 2, f"hgO{r}"
                if n >= 2:
                    await_sums(pool, SO, 2 * (n - 2) + 1)
                elif r:
                    await_sums(pool, "hgO0", 2 * (n + 4) + 1)
                pool.wait_ge(hg_b, 2 * r + d + 1)
                b = tok(A_b[d], chunks)
                for l, m in enumerate(LEVELS):
                    x = wk(w, l)
                    g = CTX // (2 * m)
                    at = b.rearrange("p h (g x) -> p h g x", x=2 * m)[:, :, :, m - 1 + d:m + d]
                    at = at.to_broadcast([P, 2, g, m])
                    early, late = half(b, m, False), half(b, m, True)
                    if d == 0:
                        TT(half(x, m, False), at, early, ALU.subtract)
                        TT(half(x, m, True), late, at, ALU.subtract)
                    else:
                        TT(half(x, m, False), early, at, ALU.subtract)
                        TT(half(x, m, True), at, late, ALU.subtract)
                def blocks(y, m):
                    return y.rearrange("p h (g x) -> p h g x", x=m)
                lb_ = blocks(b, LEAF)
                at = lb_[:, :, :, 1 + d:2 + d].to_broadcast([P, 2, CTX // LEAF, LEAF])
                TT(blocks(wk(w, 5), LEAF), lb_, at, ALU.subtract)
                TT(blocks(wk(w, 6), LEAF), at, lb_, ALU.subtract)
                cb = blocks(b, P)
                e = P - 1 if d == 0 else 0
                TT(blocks(wk(w, 7), P), cb[:, :, :, e:e + 1].to_broadcast([P, 2, 2, P]), cb,
                   ALU.subtract).then_inc(hg_diff, 1)

            for r in range(2):
                for n in range(6):
                    differences(r, n)
            pool.wait_ge(hg_round, 2)
            for name, to in (("vnw", VNW), ("bsb", BSB), ("wst", WST)):
                pool.dma_start(to, dram[name]).then_inc(mlp_tab, 16)
            for stage, (n, _) in SPLIT.items():
                with pool.Fori(0, n // 2) as i:
                    for k in range(2):
                        split_lo(stage, k, i)
                if n % 2:
                    split_lo(stage, n - 1)

        @block.vector
        def _(dve):
            step = Step(dve, dve_step)
            nrm = Norms(dve, step)
            TT, TS, STT = nc.vector.tensor_tensor, nc.vector.tensor_scalar, nc.vector.scalar_tensor_tensor

            dve.wait_ge(const_in, 64)
            step.mark(nc.vector.memset(small[:, 0:1], EPS))
            TT(small[:, 72:80], V("lb"), V("lb"), ALU.subtract).then_inc(lb_step, 1)
            lam = V("lam").rearrange("p (a n) -> p a n", a=4)
            for x in range(2):
                nc.vector.tensor_tensor_reduce(SQ[:, x, 0:64], lam[:, 2 * x, :], lam[:, 2 * x + 1, :], 1.0, 0.0,
                                               ALU.mult, ALU.add, small[:, 1 + x:2 + x]).then_inc(lb_step, 1)
            step.mark(TS(small[:, 6:7], V("subln", 0), 1.0 - LAM_INIT, None, ALU.mult))
            dve.wait_ge(lam_sem, 1)
            step.link(nc.vector.reciprocal(small[:, 80:88], small[:, 72:80]))
            step.link(TT(small[:, 72:80], small[:, 72:80], small[:, 80:88], ALU.mult))
            step.link(TT(small[:, 56:64], small[:, 72:80], small[:, 72:80], ALU.subtract))
            step.mark(TS(small[:, 64:72], small[:, 56:64], -1.0, 1.0, ALU.mult, ALU.add))
            step.link(TT(small[:, 5:6], small[:, 4:5], small[:, 3:4], ALU.subtract))
            step.link(TS(small[:, 5:6], small[:, 5:6], -LAM_INIT, None, ALU.add))

            dve.wait_ge(cs_hi, 2)
            TT(csR[:, :, 2:4], cs[:, :, :], csR[:, :, 0:2].bitcast(F32), ALU.subtract).then_inc(cs_ready, 1)
            TT(cs2R[:, :, 1], cs2[:, :], cs2R[:, :, 0].bitcast(F32), ALU.subtract).then_inc(cs_ready, 1)
            before = 0
            for stage in ADAS:
                with dve.Fori(0, WEIGHTS[stage][0] // NSLOT) as i:
                    for c in range(NSLOT):
                        dve.wait_ge(ada_hi, i * NSLOT + (before + c + 1))
                        TT(ADL[:, c, :], ring[:, c, 0:2048], ADH[:, c, :].bitcast(F32), ALU.subtract)\
                            .then_inc(slot_free[c], 1)
                before += WEIGHTS[stage][0]

            for l in range(2):
                bank = await_sums(dve, f"ada{l}", 0)[:, 0:192].rearrange("p (k s) -> p k s", s=4)
                step.link(TT(mod[:, l, :, :], bank[:, :, 0:2], V(f"ab{l}").unsqueeze(2).to_broadcast([P, 48, 2]),
                             ALU.add))
                taken(TT(mod[:, l, :, :], bank[:, :, 2:4], mod[:, l, :, :], ALU.add), f"ada{l}", 0)
                await_taken(dve, f"ada{l}", 0)
                for which, name in enumerate((f"nm{l}", f"nf{l}")):
                    o = 24 * which + 8
                    step.mark(STT(gain[:, 2 * l + which, :, :], mod[:, l, o:o + 8, :], 1.0,
                                  V(name).unsqueeze(2).to_broadcast([P, KT, 2]), ALU.add, ALU.mult))
            for l in range(2):
                bank = await_sums(dve, f"ada{2 + l}", 0)[:, 0:48].rearrange("p (k s) -> p k s", s=2)
                step.link(TT(mod2[:, l, :], bank[:, :, 0], V(f"ab{2 + l}"), ALU.add))
                taken(TT(mod2[:, l, :], bank[:, :, 1], mod2[:, l, :], ALU.add), f"ada{2 + l}", 0)
                await_taken(dve, f"ada{2 + l}", 0)
                step.mark(STT(gain2[:, l, :], mod2[:, l, 8:16], 1.0, V(f"ng{l}"), ALU.add, ALU.mult))
            step.settle()

            norm_dve(nrm, "n0", modulated(0, 0, (0, 1)))

            touched = set()

            def hgrn(r):
                win, SS, SK, SO, SU = (f"{x}{r}" for x in ("win", "hgS", "hgK", "hgO", "hgU"))
                for d in range(2):
                    for g in range(4 * d, 4 * d + 4):
                        await_taken(dve, win, g)
                    b, k = A_b[d], A_k[d]
                    step.link(TS(b[:, :, :], b[:, :, :], 1.0, None, ALU.add))
                    step.link(nc.vector.reciprocal(b[:, :, :], b[:, :, :]))
                    for j in range(2):
                        o = 4 * d + 2 * r + j
                        step.mark(TS(b[:, j, :], b[:, j, :], small[:, 64 + o:65 + o], small[:, 56 + o:57 + o],
                                     ALU.mult, ALU.add))
                    step.settle()
                    step.link(TS(b[:, :, :], b[:, :, :], F_MIN, None, ALU.max))
                    TS(k[:, :, :], b[:, :, :], -1.0, 1.0, ALU.mult, ALU.add).then_inc(hg_f, 1)
                for d in range(2):
                    dve.wait_ge(hg_ln, 2 * r + d + 1)
                    for j in range(2):
                        x = A_b[d][:, j, :]
                        keep = C("scan")[:, 0:T] if d == 0 else C("scan")[:, 1:T + 1]
                        if d:
                            x, keep = x[:, ::-1], keep[:, ::-1]
                        ins = nc.vector.tensor_tensor_scan(x, keep, x, 0.0, ALU.mult, ALU.add)
                    ins.then_inc(hg_b, 1)
                for t in range(6):
                    bank = await_sums(dve, win, 12 + t)
                    taken(nc.vector.tensor_copy(A_v[:, t, :], bank[:, 0:256]), win, 12 + t)
                for g in range(8, 12):
                    await_taken(dve, win, g)

                def operands(n):
                    d, chunks, _ = STEPS[n]
                    w = n % 2
                    dve.wait_ge(hg_exp, 6 * r + n + 1)
                    q, k = tok(A_q, chunks), tok(A_k[d], chunks)
                    for l, m in enumerate(LEVELS):
                        x = wk(w, l)
                        for second in (False, True):
                            f = q if second == (d == 0) else k
                            TT(half(x, m, second), half(x, m, second), half(f, m, second), ALU.mult)
                    for a, f in ((5, q), (6, k), (7, k), (8, q)):
                        ins = TT(wk(w, a), wk(w, a), f, ALU.mult)
                    ins.then_inc(hg_ops, 1)

                def mask_scores(n):
                    d, w = STEPS[n][0], n % 2
                    acc = ACC[:, w, :, :, :].rearrange("p h c n -> p (h c) n")
                    for l in range(6):
                        bank = await_sums(dve, SS, 6 * n + l).rearrange("p (g n) -> p g n", n=P)
                        m = masks[:, 6 * d + l:6 * d + l + 1, :].to_broadcast([P, 4, P])
                        if l == 0:
                            ins = TT(acc, bank, m, ALU.mult)
                        else:
                            ins = nc.vector.copy_predicated(acc, m.bitcast(U32), bank)
                        taken(ins, SS, 6 * n + l)
                        await_taken(dve, SS, 6 * n + l)
                    dve.sem_inc(hg_acc, 1)

                def results(n):
                    d, chunks, i = STEPS[n]
                    w, lo = n % 2, min(chunks)
                    for j, ch in enumerate(chunks):
                        q = 2 * i + j
                        bank = await_sums(dve, SO, 2 * n + j)[:, 0:2 * P].rearrange("p (h n) -> p h n", h=2)
                        y = Y[:, 2 * r:2 * r + 2, ch * P:(ch + 1) * P]
                        if (r, ch) in touched:
                            ins = TT(y, bank, y, ALU.add)
                        else:
                            ins = nc.vector.tensor_copy(y, bank)
                            touched.add((r, ch))
                        taken(ins, SO, 2 * n + j)
                        if q < 5:
                            u = STATE_NO[(d, q)]
                            bank = await_sums(dve, SU, u)
                            c = ch - lo
                            for h in range(2):
                                new = ST[:, d, q % 2, h, :]
                                if q == 0:
                                    step.mark(nc.vector.tensor_copy(new, bank[:, h * P:(h + 1) * P]))
                                else:
                                    step.mark(STT(new, ST[:, d, (q - 1) % 2, h, :], EL[:, w, h, c:c + 1],
                                                  bank[:, h * P:(h + 1) * P], ALU.mult, ALU.add))
                            step.settle()
                            dve.sem_inc(bank_free[bank_use(SU, u)[0]], 1)
                            dve.sem_inc(hg_st, 1)

                for n in range(7):
                    if n < 6:
                        operands(n)
                    if n == 0:
                        for j in range(2):
                            for i, (a, m) in enumerate(SEGS):
                                g = 18 + 2 * j + i
                                bank = await_sums(dve, win, g)
                                taken(nc.vector.tensor_copy(A_g[:, j, a:a + m], bank[:, 0:m]), win, g)
                    if n < 6:
                        mask_scores(n)
                    if n:
                        results(n - 1)
                norm_dve(nrm, f"ro{r}", readout_items(r))
                dve.wait_ge(norm_done, NORMS_UP_TO[f"ro{r}"])
                dve.wait_ge(hg_g, r + 1)
                TT(Y[:, 2 * r:2 * r + 2, :], Y[:, 2 * r:2 * r + 2, :], A_g[:, :, :], ALU.mult).then_inc(hg_round, 1)

            hgrn(0)
            hgrn(1)

            await_all_taken(dve, "wmlp")
            step.link(TT(VSQ, VB, VB, ALU.mult))
            nc.vector.tensor_reduce(ssq, VSQ, AX.X, ALU.add).then_inc(mlp_u, 1)
            dve.wait_ge(mlp_u, 2)
            step.link(nc.vector.reciprocal(rsq, rsq))
            dve.wait_ge(mlp_tab, 48)
            for t in range(6):
                for q in range(4):
                    o = 4 * t + q
                    ins = STT(VB4[:, t, q, :], VB4[:, t, q, :], rsq[:, o:o + 1], VNW[:, q, :], ALU.mult, ALU.mult)
            ins.then_inc(mlp_v, 1)
            for q in range(4):
                for i, (a, n) in enumerate(SEGS):
                    g = 2 * q + i
                    bank = await_sums(dve, "sv", g)
                    b = BSB[:, q:q + 1, :].to_broadcast([P, n // P, P])
                    taken(TT(MT[:, i, 0:n].rearrange("p (c n) -> p c n", n=P),
                             bank[:, 0:n].rearrange("p (c n) -> p c n", n=P), b, ALU.add), "sv", g)
                    await_taken(dve, "sv", g)
                    ins = TT(Y[:, 4 + q, a:a + n], MT[:, i, 0:n], U[:, q, a:a + n], ALU.mult)
            ins.then_inc(y_ready, 1)

            def add_out(stage, segs, scalar):
                g = 0
                for k in range(KT):
                    for s in segs:
                        bank = await_sums(dve, stage, g)
                        n = SEGS[s][1]
                        taken(STT(X[s][:, k, :], bank[:, 0:n], scalar(k, s), X[s][:, k, :], ALU.mult, ALU.add),
                              stage, g)
                        g += 1

            def ffn(l, segs):
                up, down = f"up{l}", f"down{l}"
                ns = len(segs)
                cw = V(f"cw{l}")
                taps = l * (FT // 2) * 4
                rounds = l * (FT // 2)
                gate2 = lambda k, s: mod[:, l, 40 + k, s:s + 1]
                with dve.Fori(0, FT // 2) as i:
                    for c in range(2):
                        g = 2 * ns * c
                        for x, s in enumerate(segs):
                            a, n = SEGS[s]
                            bank = await_sums(dve, up, g + x, i)
                            TS(FA[:, c, a:a + n], bank[:, 0:n], cw[:, bass.ds(i * 2 + (FT + c), 1)],
                               V(f"cb{l}")[:, bass.ds(i * 2 + c, 1)], ALU.mult, ALU.add).then_inc(ffn_tap[c], 1)
                            dve.wait_ge(ffn_tap[c], i * (2 * ns) + (taps + 2 * x + 1))
                            STT(FA[:, c, a + 1:a + n], bank[:, 0:n - 1], cw[:, bass.ds(i * 2 + c, 1)],
                                FA[:, c, a + 1:a + n], ALU.mult, ALU.add).then_inc(ffn_tap[c], 1)
                            dve.wait_ge(ffn_tap[c], i * (2 * ns) + (taps + 2 * x + 2))
                            taken(STT(FA[:, c, a:a + n - 1], bank[:, 1:n], cw[:, bass.ds(i * 2 + (2 * FT + c), 1)],
                                      FA[:, c, a:a + n - 1], ALU.mult, ALU.add), up, g + x)
                        dve.wait_ge(ffn_silu[c], i + (rounds + 1))
                        for x, s in enumerate(segs):
                            a, n = SEGS[s]
                            bank = await_sums(dve, up, g + ns + x, i)
                            taken(TT(G.rearrange("p k n -> p (k n)")[:, bass.ds(i * (2 * T) + (c * T + a), n)],
                                     bank[:, 0:n], FA[:, c, a:a + n], ALU.mult), up, g + ns + x)
                flat = G.rearrange("p k n -> p (k n)")
                for x, s in enumerate(segs):
                    a, n = SEGS[s]
                    with dve.Fori(0, FT // 2) as i:
                        for c in range(2):
                            p = split_use(down, FT * x + c)[0]
                            dve.wait_ge(g_hi, i * 2 + (G_BEFORE[l] + FT * x + c + 1))
                            TT(GS[:, p, 1, 0:n], flat[:, bass.ds(i * (2 * T) + (c * T + a), n)],
                               GS[:, p, 0, 0:n].bitcast(F32), ALU.subtract).then_inc(g_lo, 1)
                    sums = down + "c" if s else down
                    per = S // n
                    for m in range(KT):
                        bank = await_sums(dve, sums, m // per)[:, (m % per) * n:(m % per + 1) * n]
                        ins = STT(X[s][:, m, :], bank, gate2(m, s), X[s][:, m, :], ALU.mult, ALU.add)
                        if m % per == per - 1:
                            taken(ins, sums, m // per)

            def y_low(y, hi, lo, n, before):
                for k in range(KT):
                    dve.wait_ge(y_hi, before + k + 1)
                    TT(lo[:, k, :], y[:, k, 0:n], hi[:, k, :].bitcast(F32), ALU.subtract).then_inc(y_lo, 1)

            y_low(Y, YH0, YL0, T, 0)
            add_out("wout0", (0, 1), lambda k, s: mod[:, 0, 16 + k, s:s + 1])
            norm_dve(nrm, "n1", modulated(0, 1, (0, 1), "n1"))
            ffn(0, (0, 1))
            norm_dve(nrm, "n2", modulated(1, 0, (0, 1), "n2"))

            norm_dve(nrm, "nlat", lat_items())

            def rotate(stage, g, x, before):
                bank = await_sums(dve, stage, g)
                dve.wait_ge(m_tab, 32)
                if before:
                    dve.wait_ge(m_rope, before)
                taken(TT(M_TMP, bank[:, :], M_SIN, ALU.mult), stage, g)
                step.link(TT(x, x, M_COS, ALU.mult))
                await_taken(dve, stage, g)
                TT(x, x, M_TMP, ALU.add).then_inc(m_rope, 1)

            dve.wait_ge(norm_done, NORMS_UP_TO["nlat"])
            rotate("ropek", 0, M_PE[:, 0, 0:S], 0)
            dve.wait_ge(lat_hi, 2)
            TT(QLL, M_QL, QLH.bitcast(F32), ALU.subtract).then_inc(lat_lo, 1)
            TT(KVL, M_KV, KVH.bitcast(F32), ALU.subtract).then_inc(lat_lo, 1)
            for h in range(6):
                for x, (a, b) in enumerate(((0, 4), (4, 6))):
                    g = 4 * h + 2 + x
                    bank = await_sums(dve, "kvb", g)
                    taken(nc.vector.tensor_copy(M_V[:, a:b, h, :],
                                                bank[:, 0:(b - a) * P].rearrange("p (t n) -> p t n", n=P)), "kvb", g)
            norm_dve(nrm, "nqk", qk_items())
            dve.wait_ge(norm_done, NORMS_UP_TO["nqk"])
            for j in range(3):
                rotate("ropeq", j, M_QP[:, j, :], j + 1)
            for c in range(2):
                bank = await_sums(dve, "fb", c)
                taken(nc.vector.tensor_copy(YM[:, c, :], bank[:, :]), "fb", c)

            def m_out(h):
                bank = await_sums(dve, "mV", h)
                taken(nc.vector.tensor_copy(YM[:, 2 + h, :], bank[:, :]), "mV", h)

            for u in range(25):
                if u < 24:
                    await_sums(dve, "mS", u)
                    b = bank_use("mS", u)[0]
                    step.link(nc.vector.tensor_reduce(small[:, 10 + u % 2:11 + u % 2],
                                                      ps[:, b:b + 2, :].rearrange("p b n -> p (b n)")[:, 0:T],
                                                      AX.X, ALU.max))
                    TS(small[:, 8 + u % 2:9 + u % 2], small[:, 10 + u % 2:11 + u % 2], -float(192 ** -0.5), None,
                       ALU.mult).then_inc(m_max, 1)
                if u:
                    v = (u - 1) % 2
                    await_taken(dve, "mS", u - 1)
                    step.link(nc.vector.reciprocal(small[:, 14 + v:15 + v], small[:, 12 + v:13 + v]))
                    TS(M_DG[:, v, :], ident, small[:, 14 + v:15 + v], None, ALU.mult).then_inc(m_diag, 1)
                if u >= 6 and u % 4 == 2:
                    m_out((u - 6) // 4)
            m_out(5)
            y_low(YM, YH, YLo, S, 8)
            add_out("woutM", (0,), lambda k, s: mod[:, 1, 16 + k, s:s + 1])
            norm_dve(nrm, "n3", modulated(1, 1, (0,), "n3"))
            ffn(1, (0,))

            norm_dve(nrm, "n4", modulated2(0, "n4"))
            for v, g0 in ((E_VA, 8), (E_VB, 20)):
                for j in range(4):
                    bank = await_sums(dve, "winE", g0 + j)
                    taken(nc.vector.tensor_copy(v[:, :, j, :], bank[:, :].rearrange("p (t n) -> p t n", n=P)),
                          "winE", g0 + j)

            def attention(kind, gates):
                heads, two = PASSES[kind]
                probs, hb = PROBS_BEFORE[kind], HEADS_BEFORE[kind]

                def negate_and_bound(u, x):
                    v, h, i = probs + two * u + x, u // 4, u % 4
                    kts = key_tiles(kind, i)
                    n = P * len(kts)
                    at = 384 - P * i if kind != "c" else P * (kts[0] - i + 1)
                    hh = hb + h
                    dve.wait_ge(e_bias[hh % 2], 16 * (hh // 2 + 1))
                    if v >= 2:
                        dve.wait_ge(e_p, v - 1)
                    bank = await_sums(dve, kind + "S", two * u + x)
                    init = 3.0e38 if kind != "c" else SINKS[:, h:h + 1]
                    taken(nc.vector.tensor_tensor_reduce(
                        E_S[:, v % 2, 0:n], bank[:, 0:n], E_BIAS[:, hh % 2, at:at + n], -1.0, init,
                        ALU.add, ALU.min, small[:, 8 + v % 4:9 + v % 4]), kind + "S", two * u + x)

                def inverse(u, x):
                    v = probs + two * u + x
                    dve.wait_ge(e_p, v + 1)
                    s, r = small[:, 12 + v % 4:13 + v % 4], small[:, 16 + v % 4:17 + v % 4]
                    if kind == "c":
                        step.link(TT(s, s, small[:, 20 + v % 4:21 + v % 4], ALU.add))
                    step.link(nc.vector.reciprocal(r, s))
                    if x == 0:
                        ins = TS(E_DG[:, v % 4, :], ident, r, None, ALU.mult)
                    else:
                        ins = TS(E_DG[:, v % 4, :], ident, r, small[:, 5:6], ALU.mult, ALU.mult)
                    ins.then_inc(e_dg, 1)

                def gated(k):
                    bank = await_sums(dve, kind + "V", k)
                    y = HL[:, (4 if kind == "b" else 0) + k, :]
                    if kind == "b":
                        ins = nc.vector.tensor_copy(y, bank[:, :])
                    else:
                        ins = TT(y, bank[:, :], gates[:, k, :], ALU.mult)
                    taken(ins, kind + "V", k)

                pairs = heads // (1 if kind == "b" else 2)
                wait = 4 if kind == "b" else 8
                for u in range(4 * heads + 1):
                    for x in range(two):
                        if u < 4 * heads:
                            negate_and_bound(u, x)
                    for x in range(two):
                        if u:
                            inverse(u - 1, x)
                    if u >= wait + 2 and (u - 2) % wait == 0:
                        gated((u - 2) // wait - 1)
                gated(pairs - 1)

            await_all_taken(dve, "winE")
            attention("a", E_G)
            attention("b", E_G)
            norm_dve(nrm, "nB", subln_items())
            dve.wait_ge(norm_done, NORMS_UP_TO["nB"])
            TT(HL[:, 4:8, :], HL[:, 4:8, :], E_G[:, 4:8, :], ALU.mult).then_inc(y_ready, 1)
            y_low(HL, YH, YLo, S, 16)
            add_out("woutE", (0,), lambda k, s: mod2[:, 0, 16 + k:17 + k])
            norm_dve(nrm, "n5", modulated2(1, "n5"))
            for j in range(2):
                bank = await_sums(dve, "winC", 10 + j)
                taken(nc.vector.tensor_copy(C_V[:, :, j, :], bank[:, :].rearrange("p (t n) -> p t n", n=P)),
                      "winC", 10 + j)
            step.link(TS(SINKS, V("sink"), -1.0, None, ALU.mult))
            await_all_taken(dve, "winC")
            attention("c", C_G)
            y_low(HL, YH, YLo, S, 24)
            add_out("woutC", (0,), lambda k, s: mod2[:, 1, 16 + k:17 + k])
            norm_dve(nrm, "n6", final_items())


def shape_tables():
    f = np.float32
    i = np.arange(P)
    const = np.zeros((P, CONST_N), f)

    def put(name, x):
        a, b = CONST_AT[name]
        const[:, a:b] = x
    put("ident", np.eye(P, dtype=f))
    put("ones", 1.0)
    put("ones64", (i[:, None] // 64 == i[None, :] // 64).astype(f))
    rot = np.zeros((P, P), f)
    for j in range(P):
        if j % 32 < 16:
            rot[j + 16, j] = -1.0
        else:
            rot[j - 16, j] = 1.0
    put("rot", rot)
    m = np.zeros((2, 6, P, P), f)
    s, t = i[:, None], i[None, :]
    for l, h in enumerate(LEVELS):
        m[0, l] = (s // (2 * h) == t // (2 * h)) & (s % (2 * h) < h) & (t % (2 * h) >= h)
    m[0, 5] = (s // LEAF == t // LEAF) & (s <= t)
    m[1] = m[0].transpose(0, 2, 1)
    put("masks", m.reshape(12, P, P).transpose(1, 0, 2).reshape(P, -1))
    put("scan", (np.arange(T + 1) % P != 0).astype(f)[None, :])

    row, col = np.arange(S) // 64, np.arange(S) % 64
    inv = (f(10000.0) ** (-np.arange(0, 32, 2, dtype=f) / f(32))).astype(f)
    ang = np.stack([row, col], 0).astype(f)[:, :, None] * inv
    ang = ang.transpose(0, 2, 1)
    ang = np.tile(np.repeat(ang[:, None], 2, 1).reshape(64, S), (2, 1))
    n = np.arange(64)
    a64 = 2 * np.pi * ((n[:, None] * n[None, :]) % 64) / 64
    n = np.arange(S)
    a512 = 2 * np.pi * ((n[:, None] * n[None, :]) % S) / S
    eye2 = np.eye(2)
    cc = np.concatenate([np.kron(eye2, np.cos(a64)), -np.kron(eye2, np.sin(a64))], 1) / np.sqrt(S * 64.0)
    dft = np.concatenate([np.cos(a512).reshape(4, P, S), np.sin(a512).reshape(4, P, S)], 0).transpose(1, 0, 2)

    def slopes(n):
        return (f(2.0) ** (f(-8.0) * np.arange(1, n + 1, dtype=f) / f(n))).astype(f)
    delta = np.abs(np.arange(896)[None, :] - 384 - i[:, None])
    times = (delta <= 64).astype(int) + ((delta % 4 == 0) & (delta <= 256)) + (delta % 16 == 0)
    log_times = np.where(times > 0, np.log(np.maximum(times, 1)), -1e30)
    bias_a = np.stack([-sl * delta.astype(f) + log_times for sl in slopes(8)])
    bias_b = np.stack([-sl * delta.astype(f) for sl in slopes(4)])
    delta = np.abs(np.arange(384)[None, :] - P - i[:, None])
    sl = slopes(16)
    bias_c = np.stack([np.where(delta <= WINDOW, -sl[h] * delta.astype(f), -1e30) for h in BANDED_ORDER])
    return {k: np.ascontiguousarray(v, dtype=f) for k, v in dict(
        const=const, cos=np.cos(ang), sin=np.sin(ang), cc=cc, dft=dft, bias_a=bias_a, bias_b=bias_b,
        bias_c=bias_c).items()}


def chunks_of(w, columns):
    k = w.shape[0] // P
    w = w.reshape(k, P, w.shape[1])
    return np.stack([np.ascontiguousarray(w[:, :, c].transpose(1, 0, 2)).reshape(P, -1) for c in columns])


def laid_out(a):
    r = np.arange
    narrow = [r(c * P, (c + 1) * P) for c in range(64)]
    even = [r(c * 256, (c + 1) * 256) for c in range(64)]

    def col(v):
        v = np.asarray(v)
        return v.reshape(-1, P).T

    out = dict(shape_tables())
    for l in range(2):
        out[f"ada{l}"] = chunks_of(a["ada_w"][l], even[:24])
        out[f"ada{2 + l}"] = chunks_of(a["ada_w_2"][l], even[:12])
        w = a["ffn_w_up"][l]
        out[f"up{l}"] = chunks_of(w, [x + r(j * P, (j + 1) * P) for j in range(FT) for x in (0, FF)])
        down = a["ffn_w_down"][l].reshape(FT, P, D)
        out[f"down{l}"] = np.concatenate([down, down]) if l == 0 else down
    w = a["ev_w_in"][0]
    for h in range(2):
        out[f"win{h}"] = chunks_of(w, [x + 256 * h + r(256) for x in (1024, 1536, 0, 512, 2048)])
    out["wmlp"] = chunks_of(w, [2560 + r(256), 2816 + r(256), 3072 + r(256), 3328 + r(256)])
    out["wout0"] = chunks_of(a["ev_w_out"][0], narrow[:8])
    out["winM"] = chunks_of(a["od_w_in"][0], narrow[:7] + [np.concatenate([896 + r(64), 896 + r(64)])])
    out["qb"] = chunks_of(a["od_w_qb"][0], [x for c in range(3) for x in (
        384 * c + r(128), 384 * c + 192 + r(128), np.concatenate([384 * c + 128 + r(64), 384 * c + 320 + r(64)]))])
    out["kvb"] = chunks_of(a["od_w_kvb"][0], [256 * h + r(256) for h in range(HEADS_M)])
    out["woutM"] = chunks_of(a["od_w_out"][0], narrow[:8])
    out["winE"] = chunks_of(a["ab_w_in_2"][0], narrow[:32])
    out["woutE"] = chunks_of(a["ab_w_out_2"][0], narrow[:8])
    heads = np.concatenate([h * 64 + r(64) for h in BANDED_ORDER])
    out["winC"] = chunks_of(a["c_w_in_2"][0], [heads[P * c:P * c + P] for c in range(8)]
                            + [1024 + P * c + r(P) for c in range(4)] + [1536 + heads[P * c:P * c + P] for c in range(8)])
    out["woutC"] = chunks_of(a["c_w_out_2"][0][heads], narrow[:8])
    vecs = dict(c=col(a["c"]), cc=col(a["c_ctx"]), c2=col(a["c_2"]), lb=col(a["ev_lb_logits"]),
                onorm=col(a["ev_onorm_w"]), qa=col(a["od_qa_norm_w"]), kva=col(a["od_kva_norm_w"]),
                subln=col(a["diff_subln_g_2"]), fg=col(a["final_g_2"]))
    for l in range(2):
        vecs[f"ab{l}"], vecs[f"ab{2 + l}"] = col(a["ada_b"][l]), col(a["ada_b_2"][l])
        vecs[f"nm{l}"], vecs[f"nf{l}"] = col(a["norm_mix_w"][l]), col(a["norm_ffn_w"][l])
        vecs[f"ng{l}"] = col(a["norm_g_2"][l])
        vecs[f"cw{l}"], vecs[f"cb{l}"] = col(a["ffn_conv_w"][l]), col(a["ffn_conv_b"][l])
    for x, w in (("q", a["od_q_norm_w"][0]), ("k", a["od_k_norm_w"][0])):
        vecs[x + "n"] = col(w[:P])
        vecs[x + "p"] = col(np.concatenate([w[P:], w[P:]]))
    lam = np.concatenate([a[f"diff_{x}_2"][0] for x in ("lq1", "lk1", "lq2", "lk2")])
    vecs["lam"] = np.broadcast_to(lam[None], (P, 256))
    vecs["sink"] = np.broadcast_to(a["c_sink_2"][0][BANDED_ORDER][None], (P, 16))
    out["vecs"] = np.concatenate([vecs[name] for name in VECS], 1)
    out["xl"] = a["x"][0].T.reshape(KT, P, S).transpose(1, 0, 2)
    out["xc"] = a["ctx"][0].T.reshape(KT, P, CTX).transpose(1, 0, 2)
    out["vnw"] = np.broadcast_to(a["ev_vnorm_w"][0][None], (P, 4, P))
    out["bsb"] = np.broadcast_to(a["ev_bs"][0][None], (P, 4, P))
    out["wst"] = a["ev_ws"][0].transpose(2, 0, 1)
    return {k: np.ascontiguousarray(v) for k, v in out.items()}


def kernel(**inputs):
    import concourse.bacc as bacc
    from concourse.bass_utils import run_bass_kernel_spmd

    arrays = laid_out({k: np.asarray(v) for k, v in inputs.items()})
    nc = bacc.Bacc("TRN2", target_bir_lowering=False, num_devices=1)
    dram = {k: nc.dram_tensor(k + "_dram", v.shape, F32, kind="ExternalInput").ap() for k, v in arrays.items()}
    out = nc.dram_tensor("out_dram", (P, KT, S), F32, kind="ExternalOutput").ap()
    two_blocks(nc, dram, out)
    r = run_bass_kernel_spmd(nc, [{k + "_dram": v for k, v in arrays.items()}], core_ids=[0])
    y = r.results[0]["out_dram"]
    return np.ascontiguousarray(y.transpose(2, 1, 0).reshape(1, S, D))
```
